# Optimizing a Trainium2 kernel written in Bass

```python
import jax, jax.numpy as jnp
from jax import lax
import numpy as np

D_MODEL = 1024
BATCH = 1
SEQ = 128
DEPTH = 1
DEC_BATCH = 1
DEC_SEQ = 512
PAST_LEN = 128

GRID_W = 64
D_MIX = D_MODEL
HEAD_DIM = 64
D_A = D_MIX // 2
N_HEADS_A = D_A // HEAD_DIM
R_DECAY = 64
R_ICLR = 64
R_GATE = 128
D_B = D_MIX // 4
N_GROUPS_B = D_B // HEAD_DIM
CHUNK = 128
D_C = D_MIX - D_A - D_B
CONV_K = 31
N_EXPERTS = 16
N_EXPERT_GROUPS = 4
EXPERTS_PER_GROUP = N_EXPERTS // N_EXPERT_GROUPS
TOP_K = 2
D_EXPERT = D_MODEL // 4
MOE_BLOCK = 128
NORM_EPS = 1e-6
LN_EPS = 1e-5
LN_X_EPS = 64e-5
COLS_A = 3 * D_A + 2 * R_DECAY + 2 * R_ICLR + R_GATE
COLS_B = 2 * D_B
COLS_C = 2 * D_C
D_PROJ = COLS_A + COLS_B + COLS_C
SPLIT_A = [D_A, 2 * D_A, 3 * D_A, 3 * D_A + R_DECAY, 3 * D_A + 2 * R_DECAY,
           3 * D_A + 2 * R_DECAY + R_ICLR, 3 * D_A + 2 * R_DECAY + 2 * R_ICLR]

kernel_name = 'hybrid_rwkv7_gmlp_conformer_moe_dit_step'

def _rmsnorm(x, g):
    xf = x.astype(jnp.float32)
    y = xf * lax.rsqrt(jnp.mean(xf * xf, axis=-1, keepdims=True) + NORM_EPS)
    return (y * g.astype(jnp.float32)).astype(x.dtype)

def _layernorm(x, g, b):
    xf = x.astype(jnp.float32)
    mu = jnp.mean(xf, axis=-1, keepdims=True)
    var = jnp.mean(jnp.square(xf - mu), axis=-1, keepdims=True)
    y = (xf - mu) * lax.rsqrt(var + LN_EPS)
    return (y * g.astype(jnp.float32) + b.astype(jnp.float32)).astype(x.dtype)

def _head_norm(y, g, b):
    mu = jnp.mean(y, axis=-1, keepdims=True)
    var = jnp.mean(jnp.square(y - mu), axis=-1, keepdims=True)
    yn = (y - mu) * lax.rsqrt(var + LN_X_EPS)
    return yn.reshape(y.shape[0], y.shape[1], -1) * g.astype(jnp.float32) + b.astype(jnp.float32)

def _l2norm(t):
    tf = t.astype(jnp.float32)
    return tf / jnp.maximum(jnp.sqrt(jnp.sum(tf * tf, axis=-1, keepdims=True)), 1e-12)

def _centred_shift(p):
    prev = jnp.pad(p[:, :-1], ((0, 0), (1, 0), (0, 0)))
    nxt = jnp.pad(p[:, 1:], ((0, 0), (0, 1), (0, 0)))
    return 0.5 * (prev + nxt)

def _rwkv7_scan(s0, r, decay, kt, v, kk, a, reverse):
    xs = tuple(jnp.moveaxis(t.astype(jnp.float32), 1, 0) for t in (r, decay, kt, v, kk, a))

    def step(s, inp):
        r_t, w_t, k_t, v_t, kk_t, a_t = inp
        s_kk = jnp.einsum('bhvk,bhk->bhv', s, kk_t)
        s = (s * w_t[:, :, None, :]
             - s_kk[..., None] * (kk_t * a_t)[:, :, None, :]
             + v_t[..., None] * k_t[:, :, None, :])
        return s, jnp.einsum('bhvk,bhk->bhv', s, r_t)

    s, ys = lax.scan(step, s0.astype(jnp.float32), xs, reverse=reverse)
    return s, jnp.moveaxis(ys, 0, 1)

def _depthwise_conv(x, w, b):
    y = lax.conv_general_dilated(x, w[:, None, :].astype(x.dtype), (1,),
                                 [(CONV_K // 2, CONV_K // 2)],
                                 dimension_numbers=('NWC', 'WIO', 'NWC'),
                                 feature_group_count=x.shape[-1])
    return y + b

def _token_mixers(h, s0, grid_w, lp):
    B, T, _ = h.shape
    p = h @ lp['w_in']
    pa, pb, pc = jnp.split(p, [COLS_A, COLS_A + COLS_B], axis=-1)

    pa = pa + lp['mu_shift'] * (_centred_shift(pa) - pa)
    r, k, v, wd_f, wd_b, ad_f, ad_b, gd = jnp.split(pa, SPLIT_A, axis=-1)

    def heads(t):
        return t.reshape(B, T, N_HEADS_A, HEAD_DIM)

    g = jax.nn.sigmoid(gd) @ lp['g2']
    ys, kts, states = [], [], []
    for d, (wd, ad) in enumerate(((wd_f, ad_f), (wd_b, ad_b))):
        wlog = -jax.nn.softplus(-(lp['w0'][d] + jnp.tanh(wd) @ lp['w2'][d])) - 0.5
        decay = jnp.exp(-jnp.exp(wlog.astype(jnp.float32)))
        a = jax.nn.sigmoid(lp['a0'][d] + ad @ lp['a2'][d])
        kk = _l2norm(heads(k * lp['k_k'][d]))
        kt = k * (1 + (a - 1) * lp['k_a'][d])
        s_d, y_d = _rwkv7_scan(s0[:, d], heads(r), heads(decay), heads(kt), heads(v), kk,
                               heads(a), reverse=(d == 1))
        ys.append(y_d)
        kts.append(kt)
        states.append(s_d)
    y = _head_norm(ys[0] + ys[1], lp['lnx_g'], lp['lnx_b'])
    bonus = jnp.sum(heads(r) * heads(kts[0] + kts[1]) * lp['r_k'], axis=-1, keepdims=True) * heads(v)
    ya = ((y + bonus.reshape(B, T, D_A)) * g).astype(h.dtype)

    u, vg = jnp.split(jax.nn.gelu(pb), 2, axis=-1)
    vg = _layernorm(vg, lp['gmlp_norm_g'], lp['gmlp_norm_b'])
    vg = vg.reshape(B, T // CHUNK, CHUNK, N_GROUPS_B, HEAD_DIM)
    sv = jnp.einsum('gpq,bnqgc->bnpgc', lp['gmlp_ws'], vg) + lp['gmlp_bs'].T[:, :, None]
    yb = _rmsnorm(u * sv.reshape(B, T, D_B), lp['beta_b'])

    a_c, b_c = jnp.split(pc, 2, axis=-1)
    gl = a_c * jax.nn.sigmoid(b_c)
    if grid_w is not None:
        rows = T // grid_w
        gl = gl.reshape(B * rows, grid_w, D_C)
    yc = _depthwise_conv(gl, lp['conv_w'], lp['conv_b']).reshape(B, T, D_C)
    yc = _rmsnorm(jax.nn.silu(_layernorm(yc, lp['conv_norm_g'], lp['conv_norm_b'])), lp['beta_c'])

    out = jnp.concatenate([ya, yb, yc], axis=-1) @ lp['w_out']
    return out, jnp.stack(states, axis=1).astype(h.dtype)

def _moe(h, lp):
    B, T, D = h.shape
    ht = h.reshape(B * T, D)
    probs = jax.nn.softmax((ht @ lp['w_router']).astype(jnp.float32), axis=-1)
    sel = probs + lp['b_router'].astype(jnp.float32)
    grp_score = lax.top_k(sel.reshape(-1, N_EXPERT_GROUPS, EXPERTS_PER_GROUP), TOP_K)[0].sum(-1)
    best = jnp.argmax(grp_score, axis=-1)
    in_grp = (jnp.arange(N_EXPERTS) // EXPERTS_PER_GROUP)[None, :] == best[:, None]
    _, idx = lax.top_k(jnp.where(in_grp, sel, -jnp.inf), TOP_K)
    w = jnp.take_along_axis(probs, idx, axis=-1)
    w = w / jnp.sum(w, axis=-1, keepdims=True)
    gates = jnp.sum(jax.nn.one_hot(idx, N_EXPERTS, dtype=jnp.float32) * w[..., None], axis=1).astype(h.dtype)

    def block(args):
        hb, gb = args
        gu = jnp.einsum('td,edf->tef', hb, lp['moe_w_gu'])
        g_, u_ = jnp.split(gu, 2, axis=-1)
        act = jax.nn.silu(g_) * u_ * gb[..., None]
        return jnp.einsum('tef,efd->td', act, lp['moe_w_down'])

    out = lax.map(block, (ht.reshape(-1, MOE_BLOCK, D), gates.reshape(-1, MOE_BLOCK, N_EXPERTS)))
    return out.reshape(B, T, D)

def _layer(x, mod, s0, grid_w, lp):
    sh1, sc1, gt1, sh2, sc2, gt2 = jnp.split(mod, 6, axis=-1)
    h = _rmsnorm(x, lp['norm1_g']) * (1 + sc1) + sh1
    mix, s_new = _token_mixers(h, s0, grid_w, lp)
    x = x + gt1 * mix
    h = _rmsnorm(x, lp['norm2_g']) * (1 + sc2) + sh2
    x = x + gt2 * _moe(h, lp)
    return x, s_new

def setup_inputs(seed: int = 0) -> dict:
    key = jax.random.key(seed)
    ks = iter(jax.random.split(key, 64))

    def nrm(shape, scale=1.0):
        return scale * jax.random.normal(next(ks), shape, jnp.float32)

    def gain(shape):
        return 1.0 + nrm(shape, 0.02)

    L = DEPTH
    return {
        'x_prompt': nrm((BATCH, SEQ, D_MODEL)),
        'x_sample': nrm((DEC_BATCH, DEC_SEQ, D_MODEL)),
        'state_rwkv': nrm((DEC_BATCH, DEPTH, 2, N_HEADS_A, HEAD_DIM, HEAD_DIM), 0.5),
        'c': nrm((DEC_BATCH, D_MODEL)),
        'c_ctx': nrm((D_MODEL,)),
        'norm1_g': gain((L, D_MODEL)),
        'norm2_g': gain((L, D_MODEL)),
        'ada_w': nrm((L, D_MODEL, 6 * D_MODEL), 0.5 * D_MODEL ** -0.5),
        'ada_b': nrm((L, 6 * D_MODEL), 0.02),
        'w_in': nrm((L, D_MODEL, D_PROJ), D_MODEL ** -0.5),
        'mu_shift': jax.random.uniform(next(ks), (L, COLS_A), jnp.float32),
        'w0': nrm((L, 2, D_A), 1.5) - 2.0,
        'w2': nrm((L, 2, R_DECAY, D_A), R_DECAY ** -0.5),
        'a0': nrm((L, 2, D_A), 0.1),
        'a2': nrm((L, 2, R_ICLR, D_A), R_ICLR ** -0.5),
        'k_k': 0.85 + nrm((L, 2, D_A), 0.02),
        'k_a': gain((L, 2, D_A)),
        'g2': nrm((L, R_GATE, D_A), R_GATE ** -0.5),
        'r_k': nrm((L, N_HEADS_A, HEAD_DIM), 0.1),
        'lnx_g': gain((L, D_A)),
        'lnx_b': nrm((L, D_A), 0.02),
        'gmlp_norm_g': gain((L, D_B)),
        'gmlp_norm_b': nrm((L, D_B), 0.02),
        'gmlp_ws': nrm((L, N_GROUPS_B, CHUNK, CHUNK), CHUNK ** -0.5),
        'gmlp_bs': gain((L, N_GROUPS_B, CHUNK)),
        'beta_b': gain((L, D_B)),
        'conv_w': nrm((L, CONV_K, D_C), CONV_K ** -0.5),
        'conv_b': nrm((L, D_C), 0.02),
        'conv_norm_g': gain((L, D_C)),
        'conv_norm_b': nrm((L, D_C), 0.02),
        'beta_c': gain((L, D_C)),
        'w_out': nrm((L, D_MIX, D_MODEL), D_MIX ** -0.5),
        'w_router': nrm((D_MODEL, N_EXPERTS), D_MODEL ** -0.5),
        'b_router': nrm((N_EXPERTS,), 0.01),
        'moe_w_gu': nrm((L, N_EXPERTS, D_MODEL, 2 * D_EXPERT), D_MODEL ** -0.5),
        'moe_w_down': nrm((L, N_EXPERTS, D_EXPERT, D_MODEL), D_EXPERT ** -0.5),
        'final_g': gain((D_MODEL,)),
    }

def reference(x_prompt, x_sample, state_rwkv, c, c_ctx, norm1_g, norm2_g, ada_w, ada_b, w_in,
              mu_shift, w0, w2, a0, a2, k_k, k_a, g2, r_k, lnx_g, lnx_b, gmlp_norm_g, gmlp_norm_b,
              gmlp_ws, gmlp_bs, beta_b, conv_w, conv_b, conv_norm_g, conv_norm_b, beta_c, w_out,
              w_router, b_router, moe_w_gu, moe_w_down, final_g):
    def layer_params(l):
        return dict(norm1_g=norm1_g[l], norm2_g=norm2_g[l], w_in=w_in[l], mu_shift=mu_shift[l],
                    w0=w0[l], w2=w2[l], a0=a0[l], a2=a2[l], k_k=k_k[l], k_a=k_a[l], g2=g2[l],
                    r_k=r_k[l], lnx_g=lnx_g[l], lnx_b=lnx_b[l], gmlp_norm_g=gmlp_norm_g[l],
                    gmlp_norm_b=gmlp_norm_b[l], gmlp_ws=gmlp_ws[l], gmlp_bs=gmlp_bs[l],
                    beta_b=beta_b[l], conv_w=conv_w[l], conv_b=conv_b[l],
                    conv_norm_g=conv_norm_g[l], conv_norm_b=conv_norm_b[l], beta_c=beta_c[l],
                    w_out=w_out[l], w_router=w_router, b_router=b_router,
                    moe_w_gu=moe_w_gu[l], moe_w_down=moe_w_down[l])

    xp = x_prompt
    s_zero = jnp.zeros((x_prompt.shape[0], 2, N_HEADS_A, HEAD_DIM, HEAD_DIM), x_prompt.dtype)
    ctx_states = []
    for l in range(DEPTH):
        mod = (jax.nn.silu(c_ctx) @ ada_w[l] + ada_b[l])[None, None, :]
        xp, s_l = _layer(xp, mod, s_zero, None, layer_params(l))
        ctx_states.append(s_l)
    new_state_rwkv = jnp.stack(ctx_states, axis=1)

    xs = x_sample
    for l in range(DEPTH):
        mod = (jax.nn.silu(c) @ ada_w[l] + ada_b[l])[:, None, :]
        xs, _ = _layer(xs, mod, state_rwkv[:, l], GRID_W, layer_params(l))

    y_prompt = _rmsnorm(xp, final_g)
    y_sample = _rmsnorm(xs, final_g)
    return (y_prompt, y_sample, new_state_rwkv)


_drawn_inputs = setup_inputs


def setup_inputs(seed=0):
    import zlib

    import numpy as np

    out = dict(_drawn_inputs(seed))
    spreads = {}
    factors = {'state_rwkv': 4.557,
     'lnx_g': 37.12,
     'lnx_b': 46.722,
     'gmlp_norm_g': 43.717,
     'gmlp_norm_b': 30.103,
     'gmlp_bs': 31.366,
     'beta_b': 26.965,
     'conv_b': 3.428,
     'conv_norm_g': 23.321,
     'conv_norm_b': 30.766,
     'beta_c': 25.563,
     'final_g': 2.679,
     'norm2_g': 4.446}
    for name, (base, spread) in spreads.items():
        noise = np.random.default_rng([zlib.crc32(name.encode()), seed]).standard_normal(out[name].shape)
        drawn = base * np.exp(spread * noise) if base else spread * noise
        out[name] = __import__('jax').numpy.asarray(drawn.astype(out[name].dtype))
    for name, factor in factors.items():
        out[name] = (out[name] * factor).astype(out[name].dtype)
    return out
```

```python
from contextlib import ExitStack

import concourse.bass as bass
from concourse import mybir

ALU = mybir.AluOpType
ACT = mybir.ActivationFunctionType
AX = mybir.AxisListType
F32 = mybir.dt.float32
I32 = mybir.dt.int32
U32 = mybir.dt.uint32

P = 128


class Counts:

    def __init__(self, known):
        self.known, self.seen, self.total, self.sems = known, {}, {}, {}

    def open(self, nc, ctx):
        self.nc, self.ctx = nc, ctx

    def sem(self, name):
        if name not in self.sems:
            self.sems[name] = self.ctx.enter_context(self.nc.semaphore(name))
        return self.sems[name]

    def up(self, name, key=None, by=1):
        self.total[name] = self.total.get(name, 0) + by
        self.seen[(name, key)] = self.seen[(name, None)] = self.total[name]
        return self.sem(name), by

    def at(self, name, key=None):
        return self.sem(name), self.known[(name, key)] if self.known is not None else 1


def build(nc, A, outs, counts):
    D = 1024
    KD = D // P
    NT = 5
    SEQ, LAT = 128, 512
    T = SEQ + LAT
    TW = T + 1
    DA, DB, DC = 512, 256, 256
    HD = 64
    NH = DA // HD
    CONV_K = 31
    HALF = CONV_K // 2
    GRID = 64
    COLS_A = 1920
    NEXP = 16
    EPS_RMS, EPS_LN, EPS_LNX = 1e-6, 1e-5, 64e-5
    up, at = counts.up, counts.at

    def up16(name, key=None):
        return up(name, key, 16)

    def col(t):
        return 0 if t == 0 else 1 + t * P

    ctx = ExitStack()
    with ctx:
        counts.open(nc, ctx)

        def sb(name, shape, dt=F32):
            return ctx.enter_context(nc.sbuf_tensor(name, shape, dt))

        ps = [ctx.enter_context(nc.psum_tensor(f"bank{i}", [P, 512], F32)) for i in range(8)]

        ident = sb("ident", [P, P])
        halfones = sb("half_ones", [P, P])
        level = sb("level_mask", [P, 7, P])
        gmask = sb("causal_mask", [P, 2, 2, P])
        keep = sb("scan_keep", [P, TW])
        headsel = sb("head_select", [P, 2])

        PR = dict(norm1=(0, 8), norm2=(8, 8), mu=(16, 15), w0=(31, 8), a0=(39, 8), k_k=(47, 8), k_a=(55, 8),
                  r_k=(63, 4), conv_b=(67, 2), c_ctx=(69, 8), c=(77, 8), gmlp_bs=(85, 4))
        NPR = 89
        pcol = sb("param_cols", [P, NPR])
        ka_keep = sb("ka_keep", [P, 8])
        eps = sb("eps", [P, 4])
        GN_G, GN_B, BETA_B, CN_G, CN_B, BETA_C = range(6)
        silu_c = sb("silu_c", [P, KD, 2])
        modT = sb("mod_cols", [P, 2, KD, 2])
        SH1, SC1 = range(2)
        gain = sb("gain_cols", [P, 1, KD, 2])
        rkvT = sb("rkvT", [P, 3, 4, TW])
        loraT = sb("loraT", [P, 3, TW])
        lora_w = sb("lora_w", [P, 2, DA])
        g2_sb = sb("g2", [P, DA])
        sumsq = sb("sum_squares", [P, 3, NT])
        rstd = sb("rstd", [P, 5, NT])
        mv = sb("mean_var", [P, 2, NT, 2])
        bst = sb("bn_stats", [P, 2, NT, 6])
        catBC = sb("catBC", [P, 4, T])

        AR = 36752
        arena = sb("arena", [P, AR])
        pos = [0]

        def carve(n, at_=None):
            if at_ is not None:
                pos[0] = at_
            v = arena[:, pos[0]:pos[0] + n]
            pos[0] += n
            assert pos[0] <= AR, pos[0]
            return v

        wring = carve(2 * KD * 512).rearrange("p (s k n) -> p s k n", s=2, k=KD)
        h1T = carve(KD * T).rearrange("p (k t) -> p k t", k=KD)
        CONVW = GRID + 2 * HALF
        NROW = T // GRID
        NORM = pos[0]
        xin = carve(2 * D).rearrange("p (s d) -> p s d", s=2)
        xn = carve(2 * D).rearrange("p (s d) -> p s d", s=2)
        nend = pos[0]
        praw = carve(2 * 643, at_=NORM).rearrange("p (s t) -> p s t", s=2)
        psc = carve(2 * TW).rearrange("p (s t) -> p s t", s=2)
        nbsum = carve(TW)
        gl = carve(NT * 512, at_=nend).rearrange("p (t n) -> p t n", t=NT)
        glu = carve(2 * NROW * CONVW).rearrange("p (c r w) -> p c r w", c=2, r=NROW)
        acc = carve(2 * T).rearrange("p (c t) -> p c t", c=2)
        same = carve(8 * P).rearrange("p (l q) -> p l q", l=8)
        bc_b = carve(6 * 256).rearrange("p (i n) -> p i n", i=6)
        wsT = carve(4 * P).rearrange("p (g q) -> p g q", g=4)
        modrow = carve(512)[0:2, :]
        adab = carve(512)[0:2, :]
        prow = carve(P)[0:NPR, :]
        crow = carve(P)[0:2 * CONV_K, :]
        ccol, mu_keep, mu_half = carve(2 * CONV_K), carve(15), carve(15)
        wsrow = gl[:, 4, :].rearrange("p (g q) -> p g q", g=4)


        CHUNKS = [5, 4, 3, 1, 0, 2]
        CW = {c: COLS_A - 3 * 512 if c == 3 else 512 for c in range(6)}
        C0 = {c: c * 512 if c < 4 else COLS_A + (c - 4) * 512 for c in range(6)}
        RING = [("ada", j) for j in range(4)] + [("proj", c) for c in CHUNKS]
        TILES = [(c, m) for c in CHUNKS if c != 4 for m in range(CW[c] // P)]
        ATILES = [x for x in TILES if x[0] != 5]

        def last_use(n):
            kind, j = RING[n]
            if kind == "ada":
                return at("ada_mm", j)
            return at("proj_B", NT - 1) if j == 4 else at("proj", (j, CW[j] // P - 1))

        TURN = [(1, 0, 2), (3, 2, 2), (2, 4, 1)]

        def turned(t):
            return ((1, 0), (1, 256), (3, 0), (3, 256), (2, 0))[t]

        def bank_done(t):
            return (1, 1, 3, 3, 4)[t]

        def h1_act(act, t):
            gi = min(t, 1)
            act.wait_ge(*at("gain1"))
            act.wait_ge(*at("mod1"))
            for hf in range(1):
                act.wait_ge(*at("xn_T", (t, hf)))
                for k in range(4):
                    nc.scalar.activation(h1T[:, k, t * P:(t + 1) * P], ps[4 + (2 * t + hf) % 4][:, (k % 4) * P:(k % 4 + 1) * P],
                                         ACT.Identity, bias=modT[:, SH1, k, gi:gi + 1], scale=gain[:, 0, k, gi:gi + 1]) \
                        .then_inc(*up("h1T_act", (t, hf)))

        def cat_copy(act, c0, name):
            for b, t0, n in TURN:
                act.wait_ge(*at(name, t0 + n - 1))
                for c in range(2):
                    src = ps[b][:, 0:n * 256].rearrange("p (t c q) -> p c t q", t=n, c=2)[:, c]
                    dst = catBC[:, c0 + c, t0 * P:(t0 + n) * P].rearrange("p (t q) -> p t q", q=P)
                    nc.scalar.copy(dst, src).then_inc(*up("catBC", (c0, b)))

        def ada_row(dve, j):
            dve.wait_ge(*at("ada_mm", j))
            dve.wait_ge(*at("ada_b_landed", j))
            if j >= 1:
                dve.wait_ge(*at("mod_row_used", j - 1))
            nc.vector.tensor_tensor(modrow, ps[2][0:2, :], adab, ALU.add).then_inc(*up("mod_row", j))

        def norm_rows(dve, name, i, r, src, dst, g, b):
            v = nc.vector
            for t in range(NT):
                v.tensor_scalar(dst(t), src(t), mv[:, i, t, 0:1], rstd[:, r, t:t + 1], ALU.subtract, ALU.mult) \
                    .then_inc(*up(name + "_centred", t))
            for t in range(NT):
                dve.wait_ge(*at(name + "_centred", t))
                v.tensor_tensor(dst(t), dst(t), bc_b[:, g, :], ALU.mult).then_inc(*up(name + "_scaled", t))
            for t in range(NT):
                dve.wait_ge(*at(name + "_scaled", t))
                v.tensor_tensor(dst(t), dst(t), bc_b[:, b, :], ALU.add).then_inc(*up(name + "_norm", t))

        def ada_mm(pe, n):
            kind, j = RING[n]
            pe.wait_ge(*at(f"ring_landed{n % 2}", n))
            if j >= 1:
                pe.wait_ge(*at("mod_row", j - 1))
            for k in range(KD):
                x = nc.tensor.matmul(ps[2][0:2, :], silu_c[:, k, :], wring[:, n % 2, k, :], start=(k == 0), stop=(k == KD - 1))
            x.then_inc(*up("ada_mm", j))

        def ada_cols(pe, j):
            pe.wait_ge(*at("mod_row", j))
            which = (SH1, SC1)[j // 2]
            for i in range(4):
                o = 256 + (which * KD + (j % 2) * 4 + i) * 2
                x = nc.tensor.transpose(ps[0][:, o:o + 2], modrow[:, i * P:(i + 1) * P], ident[0:2, 0:2])
            x.then_inc(*up("mod_row_used", j))

        def turn(pe, name, src_name, src):
            for t in range(NT):
                b, o = turned(t)
                pe.wait_ge(*at(src_name, t))
                for c in range(2):
                    x = nc.tensor.transpose(ps[b][:, o + c * P:o + (c + 1) * P], src(t)[c], ident[:, :])
                x.then_inc(*up(name, t))

        QT, RT, BT, KT = range(4)
        qrkb = carve(2 * 2 * 4 * TW, at_=0).rearrange("p (r d i t) -> p r d i t", r=2, d=2, i=4)
        lw, iclr, cum, excl, rn, kk, kt, ktsum = [carve(TW) for _ in range(8)]
        mats = carve(4 * 4 * 512).rearrange("p (s u i q) -> p s u i q", s=4, u=4, i=4)
        MAT_N, MAT_NR, MAT_L, MAT_LR = range(4)
        invT = carve(4 * 512).rearrange("p (s u q) -> p s u q", s=4, u=4)
        inv = carve(2 * 512).rearrange("p (s u q) -> p s u q", s=2, u=4)
        wmat = carve(2 * 512).rearrange("p (s u q) -> p s u q", s=2, u=4)
        nlev = carve(2 * 512).rearrange("p (s u q) -> p s u q", s=2, u=4)
        kbtm = carve(4 * 512).rearrange("p (s d i c) -> p s d i c", s=4, d=2, i=2)
        vtm = carve(2 * NT * P).rearrange("p (r t c) -> p r t c", r=2, t=NT)
        xsb = carve(2 * 256).rearrange("p (s c) -> p s c", s=2)
        usb = carve(2 * 256).rearrange("p (s c) -> p s c", s=2)
        YTM0 = pos[0]
        ytm = carve(NT * DA).rearrange("p (t c) -> p t c", t=NT)
        state = carve(2 * 256).rearrange("p (r d c) -> p r d c", r=2, d=2)
        stin = carve(256).rearrange("p (d c) -> p d c", d=2)
        stout = carve(256).rearrange("p (d c) -> p d c", d=2)
        edge = carve(2 * 20).rearrange("p (r d i t) -> p r d i t", r=2, d=2, i=2)
        eedge = carve(2 * 20).rearrange("p (r d i t) -> p r d i t", r=2, d=2, i=2)
        comb = carve(2 * 6).rearrange("p (r d j) -> p r d j", r=2, d=2)
        bonus = sb("bonus", [P, NT, NH])
        DECAY = float(2.718281828459045 ** -0.5)

        BATCH = [(m, s) for m in range(4) for s in range(NT)]
        PAIRS = [(2 * q, 2 * q + 1) for q in range(len(BATCH) // 2)]

        def tile_of(d, s):
            return s if (s == 0 or d == 0) else NT - s

        def merge(main, extra):
            out, k = [], 0
            for i, x in enumerate(main):
                out.append(x)
                while k < len(extra) and (k + 1) * len(main) <= (i + 1) * len(extra):
                    out.append(extra[k])
                    k += 1
            return out + extra[k:]

        def prep_steps(m):
            out = []
            for d in range(2):
                out += [("low_rank", m, d), ("decay", m, d), ("key_norm", m, d), ("centre", m, d), ("operands", m, d),
                        ("scaled", m, d)]
            return [("values", m)] + out + [("bonus", m)]

        SCHEDULE = list(prep_steps(0))
        for b in PAIRS[0]:
            SCHEDULE += [("gram", b), ("turn_keys", b)]
        for q, (b0, b1) in enumerate(PAIRS):
            rec = []
            if q:
                for b in PAIRS[q - 1]:
                    rec += [("solve_x", b), ("solve_u", b), ("update", b)]
            nxt = []
            if q + 1 < len(PAIRS):
                for b in PAIRS[q + 1]:
                    nxt += [("gram", b), ("turn_keys", b)]
            main = [("level0", b0), ("level0", b1)]
            for l in range(1, 7):
                main += [("w", l, b0), ("w", l, b1), ("ma", l, b0), ("ma", l, b1)]
            early, late = main[:14], main[14:]
            a, z = merge(early, rec), merge(late, nxt)
            for m in range(1, 4):
                first, todo = (5 * m) // 2, prep_steps(m)
                if q == first - 2:
                    if q:
                        z = merge(z, todo[:len(todo) // 2])
                    else:
                        a, z = merge(a, todo[:len(todo) // 4]), merge(z, todo[len(todo) // 4:len(todo) // 2])
                if q == first - 1:
                    a = merge(a, todo[len(todo) // 2:])
            steps = a + z
            SCHEDULE += steps
        for b in PAIRS[-1]:
            SCHEDULE += [("solve_x", b), ("solve_u", b), ("update", b)]

        TEMPS = []
        for st in SCHEDULE:
            k = st[0]
            if k == "low_rank":
                TEMPS += [("low_rank", st[1], st[2], w, part) for w in range(2) for part in range(2)]
            elif k == "key_norm":
                TEMPS += [("key_norm", st[1], st[2], part) for part in range(2)]
            elif k == "values":
                TEMPS += [("values", st[1], part) for part in range(2)]
            elif k == "bonus":
                TEMPS += [("state_in", st[1]), ("bonus", st[1])]
            elif k == "gram":
                TEMPS += [("gram", st[1], u) for u in range(4)]
            elif k == "turn_keys":
                TEMPS += [("turn_keys", st[1])]
            elif k == "update" and BATCH[st[1]][1] == 0:
                TEMPS += [("state_out", st[1])]
        TEMP_AT = {k: i for i, k in enumerate(TEMPS)}

        def temp(key):
            return ps[TEMP_AT[key] % 2]

        def temp_free(pe, key):
            i = TEMP_AT[key]
            if i >= 2:
                pe.wait_ge(*at("read_" + TEMPS[i - 2][0], TEMPS[i - 2]))

        PARTS = [(0, P + 1), (P + 1, LAT)]

        def cols_of(part):
            c0, n = PARTS[part]
            return slice(c0, c0 + n)

        def tcols(t):
            return slice(col(t), col(t) + P)

        def lora_ap(w, d, m):
            return lora_w[d * HD:(d + 1) * HD, w, m * P:(m + 1) * P]

        def scan_loads(sp):
            for st in SCHEDULE:
                if st[0] == "values":
                    m = st[1]
                    if m:
                        sp.wait_ge(*at("state_in_T", m - 1))
                    else:
                        sp.wait_ge(*at("state_in_zero"))
                    for d in range(2):
                        for h in range(2):
                            sp.dma_start(stin[h * HD:(h + 1) * HD, d, h * HD:(h + 1) * HD],
                                         A["state_rwkv"][0, 0, d, 2 * m + h]).then_inc(*up16("state_in_landed", m))
                if st[0] == "update" and BATCH[st[1]][1] == 0:
                    m = BATCH[st[1]][0]
                    sp.wait_ge(*at("read_state_out", ("state_out", st[1])))
                    for d in range(2):
                        for h in range(2):
                            sp.dma_start(outs[2][0, 0, d, 2 * m + h], stout[h * HD:(h + 1) * HD, d, h * HD:(h + 1) * HD]) \
                                .then_inc(*up16("state_stored", m))
            post_loads(sp)

        def scan_pool(pool):
            g = nc.gpsimd
            pool.wait_ge(*at("yc_T", NT - 1))
            pool.wait_ge(*at("catBC"))
            g.memset(stin[:, :, :], 0.0).then_inc(*up("state_in_zero"))
            g.memset(state[:, :, :, :], 0.0).then_inc(*up("state_zero"))
            for st in SCHEDULE:
                if st[0] in ("level0", "w"):
                    b = st[-1]
                    l = 0 if st[0] == "level0" else st[1] + 1
                    if l > 6:
                        continue
                    s = b % 2
                    if l == 0:
                        pool.wait_ge(*at("read_gram", ("gram", b, 3)))
                        if b >= 2:
                            pool.wait_ge(*at("w_mm", (6, b - 2)))
                    elif l == 1:
                        pass
                    else:
                        pool.wait_ge(*at("w_mm", (l - 1, b)))
                    g.tensor_tensor(nlev[:, s, :, :], mats[:, b % 4, :, MAT_N, :],
                                    level[:, l:l + 1, :].to_broadcast([P, 4, P]), ALU.mult).then_inc(*up("n_level", (l, b)))
                    if st[0] == "level0":
                        pool.wait_ge(*at("level0_sum", b))
                        g.tensor_tensor(nlev[:, s, :, :], mats[:, b % 4, :, MAT_N, :],
                                        level[:, 1:2, :].to_broadcast([P, 4, P]), ALU.mult).then_inc(*up("n_level", (1, b)))
            post_pool(pool)

        def scan_act(act):
            a = nc.scalar
            for st in SCHEDULE:
                k = st[0]
                if k == "values":
                    m = st[1]
                    r = m % 2
                    act.wait_ge(*at("values_T", (m, 0)))
                    if m >= 2:
                        act.wait_ge(*at("y_mm", 5 * (m - 2) + 4))
                    a.copy(vtm[:, r, 0:4, :].rearrange("p t c -> p (t c)"), temp(("values", m, 0))[:, :]) \
                        .then_inc(*up("read_values", ("values", m, 0)))
                    act.wait_ge(*at("values_T", (m, 1)))
                    a.copy(vtm[:, r, 4, :], temp(("values", m, 1))[:, 0:P]).then_inc(*up("read_values", ("values", m, 1)))
                elif k == "low_rank":
                    _, m, d = st
                    if (m, d) == (0, 0):
                        act.wait_ge(*at("lora"))
                    else:
                        act.wait_ge(*at("operands_done", (m, d - 1) if d else (m - 1, 1)))
                    for w in range(2):
                        bias = PR["w0" if w == 0 else "a0"][0] + 4 * d + m
                        dst = (lw, iclr)[w]
                        for part in range(2):
                            act.wait_ge(*at("low_rank_mm", (m, d, w, part)))
                            a.activation(dst[:, cols_of(part)], temp(("low_rank", m, d, w, part))[:, 0:PARTS[part][1]],
                                         ACT.Sigmoid, bias=pcol[:, bias:bias + 1]) \
                                .then_inc(*up("read_low_rank", ("low_rank", m, d, w, part)))
                elif k == "decay":
                    _, m, d = st
                    kc = PR["k_k"][0] + 4 * d + m
                    a.activation(rn, rkvT[:, 1, m, :], ACT.Square, scale=pcol[:, kc:kc + 1]).then_inc(*up("key_square", (m, d)))
                elif k == "centre":
                    _, m, d = st
                    r = m % 2
                    act.wait_ge(*at("read_key_norm", ("key_norm", m, d, 1)))
                    a.activation(rn, rn, ACT.Abs_reciprocal_sqrt).then_inc(*up("key_rnorm", (m, d)))
                    act.wait_ge(*at("centred", (m, d)))
                    if m >= 2:
                        act.wait_ge(*at("y_mm", 5 * (m - 2) + 4))
                    a.activation(eedge[:, r, d, :, :], edge[:, r, d, :, :], ACT.Exp).then_inc(*up("edge_exp", (m, d)))
                    qe, re, ke = ((excl, 1.0), (cum, 1.0), (cum, -1.0)) if d == 0 else ((cum, -1.0), (excl, -1.0), (excl, 1.0))
                    for i, (src, sc) in ((QT, qe), (KT, ke), (RT, re)):
                        a.activation(qrkb[:, r, d, i, :], src, ACT.Exp, scale=sc).then_inc(*up("factor", (m, d, i)))
                elif k == "bonus":
                    m = st[1]
                    act.wait_ge(*at("bonus_mm", m))
                    a.copy(bonus[:, :, 2 * m:2 * m + 2], temp(("bonus", m))[:, 0:2 * NT].rearrange("p (t h) -> p t h", t=NT)) \
                        .then_inc(*up("read_bonus", ("bonus", m)))
                elif k == "turn_keys":
                    b = st[1]
                    act.wait_ge(*at("keys_T", b))
                    if b >= 4:
                        act.wait_ge(*at("s_mm", b - 4))
                    a.copy(kbtm[:, b % 4, :, :, :].rearrange("p d i c -> p (d i c)"), temp(("turn_keys", b))[:, :]) \
                        .then_inc(*up("read_turn_keys", ("turn_keys", b)))
                elif k == "level0":
                    b = st[1]
                    act.wait_ge(*at("inv_T", b))
                    a.copy(inv[:, b % 2, :, :].rearrange("p u q -> p (u q)"), ps[2 + 2 * (b % 2)][:, :]).then_inc(*up("inv", (0, b)))
                elif k == "ma":
                    _, l, b = st
                    if l < 6:
                        act.wait_ge(*at("m_mm", (l, b)))
                        act.wait_ge(*at("a_mm", (l, b)))
                        a.copy(inv[:, b % 2, :, :].rearrange("p u q -> p (u q)"), ps[2 + 2 * (b % 2)][:, :]) \
                            .then_inc(*up("inv", (l, b)))
                    act.wait_ge(*at("a_mm", (l, b)))
                    a.copy(invT[:, b % 4, :, :].rearrange("p u q -> p (u q)"), ps[3 + 2 * (b % 2)][:, :]) \
                        .then_inc(*up("inv_t", (l, b)))
                elif k == "solve_x":
                    b = st[1]
                    act.wait_ge(*at("x_mm", b))
                    a.copy(xsb[:, b % 2, :], ps[6][:, 0:256]).then_inc(*up("x_copy", b))
                elif k == "solve_u":
                    b = st[1]
                    act.wait_ge(*at("u_mm", b))
                    a.copy(usb[:, b % 2, :], ps[7][:, 0:256]).then_inc(*up("u_copy", b))
            post_act(act)

        def scan_dve(dve):
            v = nc.vector
            dve.wait_ge(*at("yc_T", NT - 1))
            dve.wait_ge(*at("catBC"))
            for st in SCHEDULE:
                k = st[0]
                if k == "decay":
                    _, m, d = st
                    r = m % 2
                    dve.wait_ge(*at("read_low_rank", ("low_rank", m, d, 0, 1)))
                    if m or d:
                        dve.wait_ge(*at("factor", (m, d - 1, RT) if d else (m - 1, 1, RT)))
                    v.tensor_scalar(lw, lw, -DECAY, None, ALU.mult).then_inc(*up("log_decay", (m, d)))
                    dve.wait_ge(*at("log_decay", (m, d)))
                    dve.wait_ge(*at("const", "all"))
                    v.tensor_tensor_scan(cum, keep[:, :], lw, 0.0, ALU.mult, ALU.add).then_inc(*up("decay_sum", (m, d)))
                    dve.wait_ge(*at("decay_sum", (m, d)))
                    v.tensor_copy(edge[:, r, d, 0, 0:1], cum[:, 63:64]).then_inc(*up("edge", (m, d)))
                    v.tensor_copy(edge[:, r, d, 0, 1:NT], cum[:, P + 1:TW].rearrange("p (t q) -> p t q", q=P)[:, :, 63]) \
                        .then_inc(*up("edge", (m, d)))
                elif k == "key_norm":
                    _, m, d = st
                    for part in range(2):
                        dve.wait_ge(*at("key_norm_mm", (m, d, part)))
                        v.tensor_scalar(rn[:, cols_of(part)], temp(("key_norm", m, d, part))[:, 0:PARTS[part][1]], 1e-24, None,
                                        ALU.max).then_inc(*up("read_key_norm", ("key_norm", m, d, part)))
                elif k == "centre":
                    _, m, d = st
                    r = m % 2
                    dve.wait_ge(*at("edge", (m, d)))
                    v.tensor_scalar(cum[:, 0:P + 1], cum[:, 0:P + 1], edge[:, r, d, 0, 0:1], None, ALU.subtract) \
                        .then_inc(*up("centre", (m, d)))
                    lat = cum[:, P + 1:TW].rearrange("p (t q) -> p t q", q=P)
                    v.tensor_tensor(lat, lat, edge[:, r, d, 0, 1:NT].unsqueeze(2).to_broadcast([P, NT - 1, P]), ALU.subtract) \
                        .then_inc(*up("centre", (m, d)))
                    dve.wait_ge(*at("centre", (m, d)))
                    v.tensor_copy(edge[:, r, d, 1, 0:1], cum[:, P - 1:P]).then_inc(*up("centred"))
                    v.tensor_copy(edge[:, r, d, 1, 1:NT], lat[:, :, P - 1]).then_inc(*up("centred"))
                    v.tensor_tensor(excl, cum, lw, ALU.subtract).then_inc(*up("centred", (m, d)))
                elif k == "operands":
                    _, m, d = st
                    kc, ka = PR["k_k"][0] + 4 * d + m, PR["k_a"][0] + 4 * d + m
                    K = rkvT[:, 1, m, :]
                    dst = ktsum if d == 0 else kt
                    dve.wait_ge(*at("key_rnorm", (m, d)))
                    if m or d:
                        dve.wait_ge(*at("operands_done", (m, d - 1) if d else (m - 1, 1)))
                    if m and d == 0:
                        dve.wait_ge(*at("bonus_terms", m - 1))
                    v.scalar_tensor_tensor(kk, K, pcol[:, kc:kc + 1], rn, ALU.mult, ALU.mult).then_inc(*up("kk", (m, d)))
                    dve.wait_ge(*at("read_low_rank", ("low_rank", m, d, 1, 1)))
                    v.tensor_scalar(dst, iclr, pcol[:, ka:ka + 1], ka_keep[:, 4 * d + m:4 * d + m + 1], ALU.mult, ALU.add) \
                        .then_inc(*up("key_mix", (m, d)))
                    dve.wait_ge(*at("kk", (m, d)))
                    dve.wait_ge(*at("key_mix", (m, d)))
                    v.tensor_tensor(dst, dst, K, ALU.mult).then_inc(*up("kt", (m, d)))
                    v.tensor_tensor(iclr, iclr, kk, ALU.mult).then_inc(*up("kk_iclr", (m, d)))
                elif k == "scaled":
                    _, m, d = st
                    r = m % 2
                    src = ktsum if d == 0 else kt
                    q = qrkb[:, r, d]
                    dve.wait_ge(*at("factor", (m, d, RT)))
                    v.scalar_tensor_tensor(q[:, QT, :], kk, -1.0, q[:, QT, :], ALU.mult, ALU.mult).then_inc(*up("scaled", (m, d)))
                    v.tensor_tensor(q[:, RT, :], rkvT[:, 0, m, :], q[:, RT, :], ALU.mult).then_inc(*up("scaled", (m, d)))
                    dve.wait_ge(*at("kk_iclr", (m, d)))
                    v.tensor_tensor(q[:, BT, :], iclr, q[:, KT, :], ALU.mult).then_inc(*up("scaled_b", (m, d)))
                    dve.wait_ge(*at("scaled_b", (m, d)))
                    v.tensor_tensor(q[:, KT, :], src, q[:, KT, :], ALU.mult).then_inc(*up("operands_done", (m, d)))
                elif k == "bonus":
                    m = st[1]
                    r = m % 2
                    rk = PR["r_k"][0] + m
                    dve.wait_ge(*at("operands_done", (m, 1)))
                    v.tensor_tensor(ktsum, ktsum, kt, ALU.add).then_inc(*up("kt_sum", m))
                    dve.wait_ge(*at("kt_sum", m))
                    v.scalar_tensor_tensor(ktsum, ktsum, pcol[:, rk:rk + 1], rkvT[:, 0, m, :], ALU.mult, ALU.mult) \
                        .then_inc(*up("bonus_terms", m))
                    dve.wait_ge(*at("edge_exp", (m, 1)))
                    for d in range(2):
                        v.tensor_tensor(comb[:, r, d, :], eedge[:, r, d, 1, 1:4], eedge[:, r, d, 0, 2:5], ALU.mult) \
                            .then_inc(*up("comb", m))
                    dve.wait_ge(*at("state_in_T", m))
                    if m >= 2:
                        dve.wait_ge(*at("y_mm", 5 * (m - 2) + 4))
                    dve.wait_ge(*at("state_zero"))
                    for d in range(2):
                        pre = eedge[:, r, 0, 0, 1:2] if d == 0 else eedge[:, r, 1, 1, 4:5]
                        v.tensor_scalar(state[:, r, d, :], temp(("state_in", m))[:, d * P:(d + 1) * P], pre, None, ALU.mult) \
                            .then_inc(*up("read_state_in", ("state_in", m)))
                elif k == "gram":
                    b = st[1]
                    for u in range(4):
                        dve.wait_ge(*at("gram_mm", (b, u)))
                        if b >= 4:
                            dve.wait_ge(*at("y_mm", b - 4))
                        if b == 0 and u == 0:
                            dve.wait_ge(*at("const", "all"))
                        v.tensor_tensor(mats[:, b % 4, u, :, :].rearrange("p (k q) t -> p k q t", k=2),
                                        temp(("gram", b, u))[:, :].rearrange("p (k q t) -> p k q t", k=2, q=2),
                                        gmask[:, u // 2, :, :].unsqueeze(1).to_broadcast([P, 2, 2, P]), ALU.mult) \
                            .then_inc(*up("read_gram", ("gram", b, u)))
                elif k == "level0":
                    b = st[1]
                    dve.wait_ge(*at("n_level", (0, b)))
                    if b >= 4:
                        dve.wait_ge(*at("u_mm", b - 4))
                    v.tensor_tensor(invT[:, b % 4, :, :], nlev[:, b % 2, :, :], ident[:, :].unsqueeze(1).to_broadcast([P, 4, P]),
                                    ALU.add).then_inc(*up("level0_sum", b))
                elif k == "w":
                    _, l, b = st
                    dve.wait_ge(*at("w_mm", (l, b)))
                    v.tensor_tensor(wmat[:, b % 2, :, :], ps[2 + 2 * (b % 2)][:, :].rearrange("p (u q) -> p u q", u=4),
                                    ident[:, :].unsqueeze(1).to_broadcast([P, 4, P]), ALU.add).then_inc(*up("w_sum", (l, b)))
                elif k == "update":
                    b = st[1]
                    m, s = BATCH[b]
                    r = m % 2
                    dve.wait_ge(*at("s_mm", b))
                    if s == 0:
                        if m:
                            dve.wait_ge(*at("state_stored", m - 1))
                        for d in range(2):
                            post = eedge[:, r, 0, 1, 0:1] if d == 0 else eedge[:, r, 1, 0, 0:1]
                            v.tensor_scalar(stout[:, d, :], ps[6][:, d * P:(d + 1) * P], post, None, ALU.mult) \
                                .then_inc(*up("state_scaled", b))
                        dve.wait_ge(*at("state_out_T", b))
                        v.tensor_copy(stout[:, :, :].rearrange("p d c -> p (d c)"), temp(("state_out", b))[:, 0:256]) \
                            .then_inc(*up("read_state_out", ("state_out", b)))
                    elif s < NT - 1:
                        dve.wait_ge(*at("y_mm", b))
                        for d in range(2):
                            j = s - 1 if d == 0 else NT - 2 - s
                            for h in range(2):
                                hs = slice(h * HD, (h + 1) * HD)
                                v.tensor_scalar(state[hs, r, d, hs], ps[6][hs, d * P + h * HD:d * P + (h + 1) * HD],
                                                comb[hs, r, d, j:j + 1], None, ALU.mult).then_inc(*up("state_next", b))
                    dve.wait_ge(*at("y_mm", b))
                    for d in range(2):
                        dst = ytm[:, tile_of(d, s), m * P:(m + 1) * P]
                        src = ps[7][:, 256 + d * P:256 + (d + 1) * P]
                        if s in (1, 2) or (s == 0 and d == 0):
                            v.tensor_copy(dst, src).then_inc(*up("y_part", b))
                        else:
                            if s:
                                dve.wait_ge(*at("y_part", b - 1 if s == 3 else 5 * m + 1))
                            else:
                                dve.wait_ge(counts.sem("y_part"), counts.total["y_part"])
                            v.tensor_tensor(dst, dst, src, ALU.add).then_inc(*up("y_part", b))
            post_dve(dve)

        def scan_pe(pe):
            T_ = nc.tensor
            for st in SCHEDULE:
                k = st[0]
                if k == "values":
                    m = st[1]
                    if m == 0:
                        pe.wait_ge(*at("mixed"))
                        pe.wait_ge(*at("catBC"))
                    for part in range(2):
                        temp_free(pe, ("values", m, part))
                        for t in (range(4) if part == 0 else [4]):
                            x = T_.transpose(temp(("values", m, part))[:, (t % 4) * P:(t % 4 + 1) * P], rkvT[:, 2, m, tcols(t)],
                                             ident[:, :])
                        x.then_inc(*up("values_T", (m, part)))
                elif k == "low_rank":
                    _, m, d = st
                    if (m, d) == (0, 0):
                        pe.wait_ge(*at("lora"))
                        pe.wait_ge(*at("lora_w_landed"))
                    for w in range(2):
                        for part in range(2):
                            temp_free(pe, ("low_rank", m, d, w, part))
                            T_.matmul(temp(("low_rank", m, d, w, part))[:, 0:PARTS[part][1]], lora_ap(w, d, m),
                                      loraT[d * HD:(d + 1) * HD, w, cols_of(part)], start=True, stop=True) \
                                .then_inc(*up("low_rank_mm", (m, d, w, part)))
                elif k == "key_norm":
                    _, m, d = st
                    pe.wait_ge(*at("key_square", (m, d)))
                    for part in range(2):
                        temp_free(pe, ("key_norm", m, d, part))
                        T_.matmul(temp(("key_norm", m, d, part))[:, 0:PARTS[part][1]], halfones[:, :], rn[:, cols_of(part)],
                                  start=True, stop=True).then_inc(*up("key_norm_mm", (m, d, part)))
                elif k == "bonus":
                    m = st[1]
                    temp_free(pe, ("state_in", m))
                    pe.wait_ge(*at("state_in_landed", m))
                    for d in range(2):
                        x = T_.transpose(temp(("state_in", m))[:, d * P:(d + 1) * P], stin[:, d, :], ident[:, :])
                    x.then_inc(*up("state_in_T", m))
                    temp_free(pe, ("bonus", m))
                    pe.wait_ge(*at("bonus_terms", m))
                    for t in range(NT):
                        x = T_.matmul(temp(("bonus", m))[:, 2 * t:2 * t + 2], ktsum[:, tcols(t)], headsel[:, :], start=True, stop=True)
                    x.then_inc(*up("bonus_mm", m))
                elif k == "gram":
                    b = st[1]
                    m, s = BATCH[b]
                    pe.wait_ge(*at("operands_done", (m, 1)))
                    for u in range(4):
                        d, h = u // 2, u % 2
                        hs = slice(h * HD, (h + 1) * HD)
                        tc = tcols(tile_of(d, s))
                        out = temp(("gram", b, u))
                        temp_free(pe, ("gram", b, u))
                        for i, key in enumerate((BT, KT)):
                            x = T_.matmul(out[:, i * 256:(i + 1) * 256], qrkb[hs, m % 2, d, key, tc],
                                          qrkb[hs, m % 2, d, QT:RT + 1, tc], start=True, stop=True)
                        x.then_inc(*up("gram_mm", (b, u)))
                elif k == "turn_keys":
                    b = st[1]
                    m, s = BATCH[b]
                    temp_free(pe, ("turn_keys", b))
                    for d in range(2):
                        for i, key in enumerate((BT, KT)):
                            x = T_.transpose(temp(("turn_keys", b))[:, (2 * d + i) * P:(2 * d + i + 1) * P],
                                             qrkb[:, m % 2, d, key, tcols(tile_of(d, s))], ident[:, :])
                    x.then_inc(*up("keys_T", b))
                elif k == "level0":
                    b = st[1]
                    pe.wait_ge(*at("level0_sum", b))
                    if b >= 2:
                        pe.wait_ge(*at("w_sum", (6, b - 2)))
                    for u in range(4):
                        x = T_.transpose(ps[2 + 2 * (b % 2)][:, u * P:(u + 1) * P], invT[:, b % 4, u, :], ident[:, :])
                    x.then_inc(*up("inv_T", b))
                elif k == "w":
                    _, l, b = st
                    pe.wait_ge(*at("inv", (l - 1, b)))
                    pe.wait_ge(*at("n_level", (l, b)))
                    for u in range(4):
                        x = T_.matmul(ps[2 + 2 * (b % 2)][:, u * P:(u + 1) * P], nlev[:, b % 2, u, :], inv[:, b % 2, u, :],
                                      start=True, stop=True)
                    x.then_inc(*up("w_mm", (l, b)))
                elif k == "ma":
                    _, l, b = st
                    pe.wait_ge(*at("w_sum", (l, b)))
                    if l > 1:
                        pe.wait_ge(*at("inv_t", (l - 1, b)))
                    elif b >= 2:
                        pe.wait_ge(*at("inv_t", (6, b - 2)))
                    if l < 6:
                        for u in range(4):
                            x = T_.matmul(ps[2 + 2 * (b % 2)][:, u * P:(u + 1) * P], invT[:, b % 4, u, :], wmat[:, b % 2, u, :],
                                          start=True, stop=True)
                        x.then_inc(*up("m_mm", (l, b)))
                    for u in range(4):
                        x = T_.matmul(ps[3 + 2 * (b % 2)][:, u * P:(u + 1) * P], wmat[:, b % 2, u, :], invT[:, b % 4, u, :],
                                      start=True, stop=True)
                    x.then_inc(*up("a_mm", (l, b)))
                elif k == "solve_x":
                    b = st[1]
                    m, s = BATCH[b]
                    r = m % 2
                    if b:
                        pe.wait_ge(*(at("state_scaled", b - 1) if BATCH[b - 1][1] == 0 else
                                     at("state_next", b - 1) if BATCH[b - 1][1] < NT - 1 else at("y_part", b - 1)))
                    if s == 1:
                        pe.wait_ge(*at("read_state_in", ("state_in", m)))
                    for d in range(2):
                        if s:
                            T_.matmul(ps[6][:, d * P:(d + 1) * P], qrkb[:, r, d, QT, tcols(tile_of(d, s))], state[:, r, d, :],
                                      start=(d == 0), stop=False, skip_group_check=True)
                        for h in range(2):
                            o = d * P + h * HD
                            x = T_.matmul(ps[6][:, o:o + HD], mats[:, b % 4, 2 * d + h, MAT_L, :],
                                          vtm[:, r, tile_of(d, s), h * HD:(h + 1) * HD], start=(s == 0 and o == 0),
                                          stop=(o == 192),
                                          skip_group_check=True)
                    x.then_inc(*up("x_mm", b))
                elif k == "solve_u":
                    b = st[1]
                    pe.wait_ge(*at("x_copy", b))
                    pe.wait_ge(*at("inv_t", (6, b)))
                    if b:
                        pe.wait_ge(*at("y_part", b - 1))
                    for u in range(4):
                        o = u * HD
                        x = T_.matmul(ps[7][:, o:o + HD], invT[:, b % 4, u, :], xsb[:, b % 2, o:o + HD], start=True, stop=True)
                    x.then_inc(*up("u_mm", b))
                elif k == "update":
                    b = st[1]
                    m, s = BATCH[b]
                    r = m % 2
                    pe.wait_ge(*at("u_copy", b))
                    pe.wait_ge(*at("read_turn_keys", ("turn_keys", b)))
                    for d in range(2):
                        out = ps[6][:, d * P:(d + 1) * P]
                        t = tile_of(d, s)
                        if s:
                            T_.matmul(out, ident[:, :], state[:, r, d, :], start=True, stop=False)
                        T_.matmul(out, kbtm[:, b % 4, d, 1, :], vtm[:, r, t, :], start=(s == 0), stop=False)
                        x = T_.matmul(out, kbtm[:, b % 4, d, 0, :], usb[:, b % 2, d * P:(d + 1) * P], start=False, stop=True)
                    x.then_inc(*up("s_mm", b))
                    for d in range(2):
                        t = tile_of(d, s)
                        if s:
                            T_.matmul(ps[7][:, 256 + d * P:256 + (d + 1) * P], qrkb[:, r, d, RT, tcols(t)], state[:, r, d, :],
                                      start=(d == 0), stop=False, skip_group_check=True)
                        for h in range(2):
                            o = d * P + h * HD
                            T_.matmul(ps[7][:, 256 + o:256 + o + HD], mats[:, b % 4, 2 * d + h, MAT_LR, :],
                                      vtm[:, r, t, h * HD:(h + 1) * HD], start=(s == 0 and o == 0), stop=False,
                                      skip_group_check=True)
                            x = T_.matmul(ps[7][:, 256 + o:256 + o + HD], mats[:, b % 4, 2 * d + h, MAT_NR, :],
                                          usb[:, b % 2, o:o + HD], start=False, stop=(o == 192), skip_group_check=True)
                    x.then_inc(*up("y_mm", b))
                    if s == 0:
                        temp_free(pe, ("state_out", b))
                        pe.wait_ge(*at("state_scaled", b))
                        for d in range(2):
                            x = T_.transpose(temp(("state_out", b))[:, d * P:(d + 1) * P], stout[:, d, :], ident[:, :])
                        x.then_inc(*up("state_out_T", b))
            post_pe(pe)

        FE = 2 * 256
        DE = FE // 2
        ENDLESS = 1e30
        CAP = (2 * T - NEXP) // P + NEXP
        GATE1, SHIFT2, SCALE2, GATE2 = range(4)
        mods = carve(4 * 2 * D, at_=0).rearrange("p (i g n) -> p i g n", i=4, g=2)
        x1 = carve(NT * D).rearrange("p (t n) -> p t n", t=NT)
        bc_row = carve(D)
        MOE0 = pos[0]
        wout = carve(KD * D).rearrange("p (k n) -> p k n", k=KD)
        aring = carve(2 * KD * 512).rearrange("p (s k n) -> p s k n", s=2, k=KD)
        h2 = carve(2 * D).rearrange("p (s n) -> p s n", s=2)
        assert pos[0] <= YTM0
        wgu = carve(2 * KD * FE, at_=MOE0).rearrange("p (s k n) -> p s k n", s=2, k=KD)
        wdn = carve(2 * 2 * D).rearrange("p (s k n) -> p s k n", s=2, k=2)
        hrow = carve(2 * D).rearrange("p (s n) -> p s n", s=2)
        hT = carve(2 * D).rearrange("p (s k q) -> p s k q", s=2, k=KD)
        act_in = carve(DE)
        actg = carve(2 * DE).rearrange("p (s n) -> p s n", s=2)
        actT = carve(2 * DE).rearrange("p (s n) -> p s n", s=2)
        assert pos[0] <= YTM0
        yrow = carve(2 * D, at_=YTM0).rearrange("p (s n) -> p s n", s=2)
        modrow2 = carve(512, at_=YTM0 + NT * DA)[0:2, :]
        adab2 = carve(512)[0:2, :]
        hmv = carve(NT * NH * 2).rearrange("p (t h i) -> p t h i", t=NT, h=NH)
        hrstd = carve(NT * NH).rearrange("p (t h) -> p t h", t=NT)

        def region(ap):
            at_ = [0]

            def take(n):
                v = ap[:, at_[0]:at_[0] + n]
                at_[0] += n
                assert at_[0] <= ap.shape[1], at_[0]
                return v
            return take

        take = region(rkvT[:, 0:2, :, :].rearrange("p a m t -> p (a m t)"))
        catA = take(2 * 4 * P).rearrange("p (s k q) -> p s k q", s=2, k=4)
        vbonus = take(DA)
        h2T = take(D).rearrange("p (k q) -> p k q", k=KD)
        bc_lnx = take(2 * DA).rearrange("p (i n) -> p i n", i=2)
        mixed = take(D)
        take = region(loraT[:, 0:2, :].rearrange("p a t -> p (a t)"))
        group_row = take(2 * P).rearrange("p (g q) -> p g q", g=2)[0:2]
        ones = take(P)
        w1, w2_, slot1, slot2 = [take(NT) for _ in range(4)]
        pick_gate = [w1, w2_]
        tokid = take(NT)
        prio16, prio4, step128, tile_no, part_no = take(NEXP), take(4), take(NT), take(CAP), take(1)
        b_router_bc = take(NEXP)
        wr_sb = take(KD * NEXP).rearrange("p (k e) -> p k e", k=KD)
        bst2 = take(NH * 6).rearrange("p (h i) -> p h i", h=NH)
        stok = take(P)
        slot_u = take(2 * NT).bitcast(U32).rearrange("p (k t) -> p k t", k=2)
        weight_u, token_u = [take(CAP).bitcast(U32) for _ in range(2)]
        take = region(arena[:, YTM0:YTM0 + NT * DA])
        logit, sel, masked, pick1, pick2, prod, prefix, tot = [take(NT * NEXP) for _ in range(8)]
        pairs = take(NT * 4 * 6).rearrange("p (t g i) -> p t g i", t=NT, g=4)
        gsc, gpr = take(NT * 4), take(NT * 4)
        rmax, rsum, p1, p2 = [take(NT) for _ in range(4)]
        nexp, ctile, cend, base = [take(NEXP) for _ in range(4)]
        steps5 = take(NEXP * NT)
        tcmp = take(CAP * NEXP)
        texp = take(CAP)

        h_dram = nc.dram_tensor("h2_rows", (T, D), F32).ap()
        y_dram = nc.dram_tensor("slot_rows", (CAP * P, D), F32).ap()
        tok_dram = nc.dram_tensor("slot_tokens", (CAP * P, 1), F32).ap()
        wgu_rows = A["moe_w_gu"].rearrange("l e (p k) n -> (l e p) (k n)", k=KD)
        wdn_rows = A["moe_w_down"].rearrange("l e (p k) n -> (l e p) (k n)", k=2)

        ORDER = [("head", 0), ("ada", 4), ("ada", 5), ("spread", 4), ("turn_a", 0), ("head", 1), ("ada", 6), ("spread", 5),
                 ("ada", 7), ("spread", 6), ("mix", 0), ("turn_a", 1), ("head", 2), ("ada", 8), ("spread", 7), ("ada", 9),
                 ("spread", 8), ("mix", 1), ("turn_a", 2), ("head", 3), ("ada", 10), ("spread", 9), ("ada", 11),
                 ("spread", 10), ("spread", 11), ("h2", 0), ("mix", 2), ("turn_a", 3), ("head", 4), ("h2", 1), ("mix", 3),
                 ("turn_a", 4), ("h2", 2), ("mix", 4), ("h2", 3), ("h2", 4)]

        def scan_done(eng):
            for n in ("y_part", "u_copy", "y_mm", "n_level", "read_turn_keys", "read_gram", "state_stored", "read_bonus",
                      "bonus_terms", "factor", "read_values", "inv_t", "comb", "read_state_in", "read_state_out",
                      "state_next", "key_mix", "read_low_rank"):
                eng.wait_ge(*at(n))

        def post_loads(sp):
            scan_done(sp)

            def ada_load(j):
                if j >= 6:
                    sp.wait_ge(*at("pe_did", ("ada", j - 2)))
                src = A["ada_w"][0].rearrange("(k p) n -> p k n", p=P)[:, :, j * 512:(j + 1) * 512]
                sp.dma_start(aring[:, j % 2, :, :], src).then_inc(*up16(f"ring_landed{j % 2}", ("ada", j)))
                if j > 4:
                    sp.wait_ge(*at("dve_did", ("ada", j - 1)))
                sp.dma_start(adab2, A["ada_b"][:, j * 512:(j + 1) * 512].to_broadcast([2, 512])) \
                    .then_inc(*up16("ada_b_landed", ("ada", j)))
            for i, n in enumerate(("lnx_g", "lnx_b")):
                sp.dma_start(bc_lnx[:, i, :], A[n].to_broadcast([P, DA])).then_inc(*up16("lnx_landed"))
            ada_load(4)
            for hf in range(2):
                sp.dma_start(wout[:, 4 * hf:4 * hf + 4, :],
                             A["w_out"][0].rearrange("(k p) n -> p k n", p=P)[:, 4 * hf:4 * hf + 4, :]) \
                    .then_inc(*up16("w_out_landed"))
            for t in range(NT):
                src = A["x_prompt"][0] if t == 0 else A["x_sample"][0, (t - 1) * P:t * P, :]
                sp.dma_start(x1[:, t, :], src).then_inc(*up16("w_out_landed"))
            sp.dma_start(bc_row, A["norm2_g"].to_broadcast([P, D])).then_inc(*up16("norm2_landed"))
            sp.dma_start(wr_sb, A["w_router"].rearrange("(k p) e -> p k e", p=P)).then_inc(*up16("norm2_landed"))
            sp.dma_start(b_router_bc, A["b_router"].rearrange("(o e) -> o e", o=1).to_broadcast([P, NEXP])) \
                .then_inc(*up16("norm2_landed"))
            for j in range(5, 12):
                ada_load(j)
            sp.wait_ge(*at("pool_did", "zero"))
            sp.dma_start(tok_dram.rearrange("(i p) o -> i (p o)", p=P), stok[0:CAP, :]).then_inc(*up16("slots_cleared"))
            for t in range(NT):
                sp.wait_ge(*at("dve_did", ("h2", t)))
                if t:
                    sp.wait_ge(*at("h2_stored", t - 1))
                sp.dma_start(h_dram[t * P:(t + 1) * P, :], h2[:, t % 2, :]).then_inc(*up16("h2_stored", t))
            sp.wait_ge(*at("dve_did", ("spread", 9)))
            sp.dma_start(bc_row, A["final_g"].rearrange("(o e) -> o e", o=1).to_broadcast([P, D])).then_inc(*up16("final_g_landed"))
            sp.wait_ge(*at("slots_scattered"))
            sp.dma_start(stok[0:CAP, :], tok_dram.rearrange("(i p) o -> i (p o)", p=P)).then_inc(*up16("slots_read"))
            for i in range(CAP):
                sp.wait_ge(*at("act_did", ("down", i)))
                sp.wait_ge(*at("dve_did", ("down", i)))
                sp.dma_start(y_dram[i * P:(i + 1) * P, :], yrow[:, i % 2, :]).then_inc(*up16(f"y_stored{i % 2}", i))
            for t in range(NT):
                sp.wait_ge(*at("dve_did", ("out", t)))
                dst = outs[0][0] if t == 0 else outs[1][0, (t - 1) * P:t * P, :]
                sp.dma_start(dst, comb_rows[t % 2][0]).then_inc(*up16(f"stored{t % 2}", t))

        comb_rows = [[wgu[:, s, 2 * i:2 * i + 2, :].rearrange("p k n -> p (k n)") for i in range(2)] for s in range(2)]

        def post_pool(pool):
            g = nc.gpsimd
            scan_done(pool)
            g.memset(ones, 1.0).then_inc(*up("pool_did", "ones"))
            g.memset(group_row, 0.0).then_inc(*up("pool_did", "rows_zero"))
            g.memset(stok, 0.0).then_inc(*up("pool_did", "zero"))
            g.iota(tokid, pattern=[[P, NT]], base=0, channel_multiplier=1, allow_small_or_imprecise_dtypes=True) \
                .then_inc(*up("pool_did"))
            g.iota(prio16, pattern=[[-1, NEXP]], base=NEXP, channel_multiplier=0, allow_small_or_imprecise_dtypes=True) \
                .then_inc(*up("pool_did"))
            g.iota(prio4, pattern=[[-1, 4]], base=4, channel_multiplier=0, allow_small_or_imprecise_dtypes=True) \
                .then_inc(*up("pool_did"))
            g.iota(step128, pattern=[[P, NT]], base=0, channel_multiplier=0, allow_small_or_imprecise_dtypes=True) \
                .then_inc(*up("pool_did"))
            g.iota(tile_no, pattern=[[1, CAP]], base=0, channel_multiplier=0, allow_small_or_imprecise_dtypes=True) \
                .then_inc(*up("pool_did"))
            g.iota(part_no, pattern=[[0, 1]], base=0, channel_multiplier=1, allow_small_or_imprecise_dtypes=True) \
                .then_inc(*up("pool_did"))
            pool.wait_ge(*at("pool_did", "rows_zero"))
            g.affine_select(out=group_row, in_=group_row, pattern=[[-1, 2], [0, P]], compare_op=ALU.not_equal,
                            fill=1.0, base=0, channel_multiplier=1).then_inc(*up("pool_did", "consts"))
            pool.wait_ge(*at("dve_did", "slots"))
            pool.wait_ge(*at("slots_cleared"))
            for k in range(2):
                for t in range(NT):
                    g.indirect_dma_start(tok_dram, bass.IndirectOffsetOnAxis(ap=slot_u[:, k, t:t + 1], axis=0),
                                         tokid[:, t:t + 1], None).then_inc(*up16("slots_scattered"))

            def fetch_weights(i):
                s = i % 2
                if i >= 2:
                    pool.wait_ge(*at("pe_did", ("gu", i - 2)))
                g.indirect_dma_start(wgu[:, s, :, :].rearrange("p k n -> p (k n)"), None, wgu_rows,
                                     bass.IndirectOffsetOnAxis(ap=weight_u[:, i:i + 1], axis=0)).then_inc(*up16(f"gu_landed{s}", i))
                if i >= 2:
                    pool.wait_ge(*at("pe_did", ("down", i - 2)))
                g.indirect_dma_start(wdn[:, s, :, :].rearrange("p k n -> p (k n)"), None, wdn_rows,
                                     bass.IndirectOffsetOnAxis(ap=weight_u[:, i:i + 1], axis=0)).then_inc(*up16(f"down_landed{s}", i))

            def fetch_rows(i):
                s = i % 2
                if i >= 2:
                    pool.wait_ge(*at("pe_did", ("turn_h", i - 2)))
                g.indirect_dma_start(hrow[:, s, :], None, h_dram,
                                     bass.IndirectOffsetOnAxis(ap=token_u[:, i:i + 1], axis=0)).then_inc(*up16(f"rows_landed{s}", i))
            pool.wait_ge(*at("dve_did", "experts"))
            for n in (("pe_did", ("mix", NT - 1)), ("pe_did", ("ada", 11)), ("h2_stored", NT - 1)):
                pool.wait_ge(*at(*n))
            fetch_weights(0)
            pool.wait_ge(*at("dve_did", "tokens"))
            fetch_rows(0)
            for i in range(1, CAP):
                fetch_rows(i)
                fetch_weights(i)
            for s in range(2):
                pool.wait_ge(*at(f"y_stored{s}"))
            pool.wait_ge(*at("pe_did", ("gu", CAP - 1)))
            for t in range(NT):
                if t >= 2:
                    pool.wait_ge(*at(f"stored{t % 2}", t - 2))
                for k in range(2):
                    g.indirect_dma_start(comb_rows[t % 2][k], None, y_dram,
                                         bass.IndirectOffsetOnAxis(ap=slot_u[:, k, t:t + 1], axis=0)) \
                        .then_inc(*up16(f"picks_landed{t % 2}", t))
            pool.wait_ge(*at("stored0"))
            pool.wait_ge(*at("stored1"))

        def post_act(act):
            a = nc.scalar
            scan_done(act)
            for k, t in ORDER:
                if k == "head":
                    act.wait_ge(*at("dve_did", ("head_var", t)))
                    a.activation(hrstd[:, t, :], hmv[:, t, :, 1], ACT.Abs_reciprocal_sqrt, bias=eps[:, 2:3]) \
                        .then_inc(*up("act_did", ("head", t)))
                elif k == "spread":
                    if t // 2 - 2 == SCALE2:
                        continue
                    act.wait_ge(*at("pe_did", ("spread", t)))
                    for gi in range(2):
                        a.copy(mods[:, t // 2 - 2, gi, (t % 2) * 512:(t % 2 + 1) * 512], ps[1 + gi][:, :]) \
                            .then_inc(*up("act_did", ("spread", t)))
                elif k == "turn_a":
                    act.wait_ge(*at("pe_did", ("turn_a", t)))
                    if t >= 2:
                        act.wait_ge(*at("pe_did", ("mix", t - 2)))
                    a.copy(catA[:, t % 2, :, :].rearrange("p k q -> p (k q)"), ps[5][:, :]).then_inc(*up("act_did", ("turn_a", t)))
                elif k == "mix":
                    act.wait_ge(*at("dve_did", ("mix", t)))
                    if t >= 2:
                        act.wait_ge(*at("pe_did", ("turn_h2", t - 2)))
                        act.wait_ge(*at("h2_stored", t - 2))
                    a.activation(h2[:, t % 2, :], x1[:, t, :], ACT.Square, accum_out=sumsq[:, 0, t:t + 1]).then_inc(*up("act_did", ("square", t)))
                    act.wait_ge(*at("act_did", ("square", t)))
                    a.activation(rstd[:, 0, t:t + 1], sumsq[:, 0, t:t + 1], ACT.Abs_reciprocal_sqrt, bias=eps[:, 0:1],
                                 scale=1.0 / D).then_inc(*up("act_did", ("mix", t)))
                elif k == "h2":
                    act.wait_ge(*at("pe_did", ("turn_h2", t)))
                    if t:
                        act.wait_ge(*at("pe_did", ("router", t - 1)))
                    a.copy(h2T[:, 0:4, :].rearrange("p k q -> p (k q)"), ps[1][:, :]).then_inc(*up("act_did", ("h2", t)))
            act.wait_ge(*at("dve_did", "shifted"))
            a.activation(logit, logit, ACT.Exp).then_inc(*up("act_did", "exp"))
            for i in range(CAP + 1):
                if i < CAP:
                    s = i % 2
                    act.wait_ge(*at("pe_did", ("turn_h", i)))
                    if i >= 2:
                        act.wait_ge(*at("pe_did", ("gu", i - 2)))
                    a.copy(hT[:, s, 0:4, :].rearrange("p k q -> p (k q)"), ps[0][:, :]).then_inc(*up("act_did", ("turn_h", i)))
                    act.wait_ge(*at("pe_did", ("gu", i)))
                    if i:
                        act.wait_ge(*at("dve_did", ("gu", i - 1)))
                    a.activation(act_in, ps[2 + s][:, 0:DE], ACT.Silu).then_inc(*up("act_did", ("gu", i)))
                if i:
                    i -= 1
                    act.wait_ge(*at("pe_did", ("down", i)))
                    if i >= 2:
                        act.wait_ge(*at(f"y_stored{i % 2}", i - 2))
                    a.copy(yrow[:, i % 2, 0:512], ps[5][:, :]).then_inc(*up("act_did", ("down", i)))
            for t in range(NT):
                act.wait_ge(*at("dve_did", ("x2", t)))
                if t:
                    act.wait_ge(*at("act_did", ("out_square", t - 1)))
                a.activation(mixed, x1[:, t, :], ACT.Square, accum_out=sumsq[:, 1, t:t + 1]) \
                    .then_inc(*up("act_did", ("out_square", t)))
                act.wait_ge(*at("act_did", ("out_square", t)))
                a.activation(rstd[:, 1, t:t + 1], sumsq[:, 1, t:t + 1], ACT.Abs_reciprocal_sqrt, bias=eps[:, 0:1],
                             scale=1.0 / D).then_inc(*up("act_did", ("out", t)))

        def post_dve(dve):
            v = nc.vector
            scan_done(dve)

            def did(key):
                return up("dve_did", key)

            def after(key):
                dve.wait_ge(*at("dve_did", key))

            def bc(ap, n):
                return ap.unsqueeze(2).to_broadcast(list(ap.shape) + [n])

            for k, t in ORDER:
                if k == "head":
                    y = ytm[:, t, :]
                    yh = y.rearrange("p (h c) -> p h c", h=NH)
                    if t:
                        after(("head_var", t - 1))
                    for h in range(NH):
                        v.bn_stats(bst2[:, h, :], y[:, h * HD:(h + 1) * HD]).then_inc(*did(("head_stats", t)))
                    after(("head_stats", t))
                    for h in range(NH):
                        v.bn_aggr(hmv[:, t, h, :], bst2[:, h, :]).then_inc(*did(("head_var", t)))
                    after(("head_var", t))
                    v.tensor_tensor(yh, yh, bc(hmv[:, t, :, 0], HD), ALU.subtract).then_inc(*did(("head_centred", t)))
                    dve.wait_ge(*at("pe_did", ("head", t)))
                    v.tensor_tensor(vbonus.rearrange("p (h c) -> p h c", h=NH), ps[4][:, :].rearrange("p (h c) -> p h c", h=NH),
                                    bc(bonus[:, t, :], HD), ALU.mult).then_inc(*did(("v_bonus", t)))
                    after(("head_centred", t))
                    dve.wait_ge(*at("act_did", ("head", t)))
                    v.tensor_tensor(yh, yh, bc(hrstd[:, t, :], HD), ALU.mult).then_inc(*did(("head_scaled", t)))
                    dve.wait_ge(*at("lnx_landed"))
                    after(("head_scaled", t))
                    v.tensor_tensor(y, y, bc_lnx[:, 0, :], ALU.mult).then_inc(*did(("lnx_g", t)))
                    after(("lnx_g", t))
                    v.tensor_tensor(y, y, bc_lnx[:, 1, :], ALU.add).then_inc(*did(("lnx_b", t)))
                    after(("lnx_b", t))
                    v.tensor_tensor(y, y, vbonus, ALU.add).then_inc(*did(("with_bonus", t)))
                    after(("with_bonus", t))
                    v.tensor_tensor(y, y, ps[3][:, :], ALU.mult).then_inc(*did(("head", t)))
                elif k == "ada":
                    dve.wait_ge(*at("pe_did", ("ada", t)))
                    dve.wait_ge(*at("ada_b_landed", ("ada", t)))
                    if t > 4:
                        dve.wait_ge(*at("pe_did", ("spread", t - 1)))
                    v.tensor_tensor(modrow2, ps[0][0:2, :], adab2, ALU.add).then_inc(*did(("ada", t)))
                elif k == "spread":
                    if t // 2 - 2 != SCALE2:
                        continue
                    dve.wait_ge(*at("pe_did", ("spread", t)))
                    dve.wait_ge(*at("norm2_landed"))
                    cs = slice((t % 2) * 512, (t % 2 + 1) * 512)
                    for gi in range(2):
                        v.scalar_tensor_tensor(mods[:, SCALE2, gi, cs], ps[1 + gi][:, :], 1.0, bc_row[:, cs], ALU.add, ALU.mult) \
                            .then_inc(*did(("spread", t)))
                elif k == "mix":
                    gi = min(t, 1)
                    dve.wait_ge(*at("w_out_landed"))
                    dve.wait_ge(*at("act_did", ("spread", 5)))
                    for hf in range(2):
                        dve.wait_ge(*at("pe_did", ("mix", t)))
                        cs = slice(hf * 512, hf * 512 + 512)
                        if t:
                            after(("mix", t - 1))
                        v.tensor_tensor(mixed[:, cs], ps[6 + hf][:, :], mods[:, GATE1, gi, cs], ALU.mult).then_inc(*did(("mixed", t)))
                    after(("mixed", t))
                    v.tensor_tensor(x1[:, t, :], x1[:, t, :], mixed, ALU.add).then_inc(*did(("mix", t)))
                elif k == "h2":
                    gi = min(t, 1)
                    dve.wait_ge(*at("act_did", ("mix", t)))
                    if t >= 2:
                        dve.wait_ge(*at("h2_stored", t - 2))
                        dve.wait_ge(*at("pe_did", ("turn_h2", t - 2)))
                    after(("spread", 9))
                    v.scalar_tensor_tensor(h2[:, t % 2, :], x1[:, t, :], rstd[:, 0, t:t + 1], mods[:, SCALE2, gi, :],
                                           ALU.mult, ALU.mult).then_inc(*did(("h2_scaled", t)))
                    after(("h2_scaled", t))
                    dve.wait_ge(*at("act_did", ("spread", 7)))
                    v.tensor_tensor(h2[:, t % 2, :], h2[:, t % 2, :], mods[:, SHIFT2, gi, :], ALU.add).then_inc(*did(("h2", t)))
                    dve.wait_ge(*at("pe_did", ("turn_h2", t)))
                    if t:
                        dve.wait_ge(*at("pe_did", ("router", t - 1)))
                    v.tensor_copy(h2T[:, 4:8, :].rearrange("p k q -> p (k q)"), ps[2][:, :]).then_inc(*did(("h2_T", t)))
            dve.wait_ge(*at("pool_did", "consts"))
            dve.wait_ge(*at("pe_did", ("router", NT - 1)))
            after(("h2_T", NT - 1))

            def by(ap, n=NEXP):
                return ap.rearrange("p (t e) -> p t e", t=NT)

            lg = ps[0][:, 0:NT * NEXP]
            v.tensor_reduce(rmax, by(lg), AX.X, ALU.max).then_inc(*did("row_max"))
            after("row_max")
            v.tensor_tensor(by(logit), by(lg), bc(rmax, NEXP), ALU.subtract).then_inc(*did("shifted"))
            dve.wait_ge(*at("act_did", "exp"))
            v.tensor_reduce(rsum, by(logit), AX.X, ALU.add).then_inc(*did("exp_sum"))
            after("exp_sum")
            v.reciprocal(rsum, rsum).then_inc(*did("exp_rsum"))
            after("exp_rsum")
            v.tensor_tensor(by(logit), by(logit), bc(rsum, NEXP), ALU.mult).then_inc(*did("probs"))
            after("probs")
            v.tensor_tensor(by(sel), by(logit), b_router_bc.unsqueeze(1).to_broadcast([P, NT, NEXP]), ALU.add).then_inc(*did("sel"))
            after("sel")
            sg = sel.rearrange("p (t g i) -> p t g i", t=NT, g=4)
            for o, n, lag in ((0, 3, 1), (3, 2, 2), (5, 1, 3)):
                v.tensor_tensor(pairs[:, :, :, o:o + n], sg[:, :, :, 0:n], sg[:, :, :, lag:lag + n], ALU.add).then_inc(*did("pairs"))
            after("pairs")
            gs = gsc.rearrange("p (t g) -> p t g", t=NT)
            gp = gpr.rearrange("p (t g) -> p t g", t=NT)
            v.tensor_reduce(gs, pairs, AX.X, ALU.max).then_inc(*did("group_score"))
            after("group_score")

            def first_max(x, w, prio, pick, key):
                v.tensor_reduce(rmax, x, AX.X, ALU.max).then_inc(*did(key + "_max"))
                after(key + "_max")
                v.tensor_tensor(pick, x, bc(rmax, w), ALU.is_equal).then_inc(*did(key + "_ties"))
                after(key + "_ties")
                v.tensor_tensor(pick, pick, prio.unsqueeze(1).to_broadcast([P, NT, w]), ALU.mult).then_inc(*did(key + "_prio"))
                after(key + "_prio")
                v.tensor_reduce(rmax, pick, AX.X, ALU.max).then_inc(*did(key + "_best"))
                after(key + "_best")
                v.tensor_tensor(pick, pick, bc(rmax, w), ALU.is_equal).then_inc(*did(key))
                after(key)

            first_max(gs, 4, prio4, gp, "group")
            v.tensor_scalar(gpr, gpr, 1.0, ENDLESS, ALU.subtract, ALU.mult).then_inc(*did("outside"))
            after("outside")
            v.tensor_tensor(masked.rearrange("p (t g i) -> p t g i", t=NT, g=4), sg, gp.unsqueeze(3).to_broadcast([P, NT, 4, 4]),
                            ALU.add).then_inc(*did("masked"))
            after("masked")
            first_max(by(masked), NEXP, prio16, by(pick1), "pick1")
            v.scalar_tensor_tensor(masked, pick1, -3 * ENDLESS, masked, ALU.mult, ALU.add).then_inc(*did("masked2"))
            after("masked2")
            first_max(by(masked), NEXP, prio16, by(pick2), "pick2")
            for k, (pk, p) in enumerate(((pick1, p1), (pick2, p2))):
                v.tensor_tensor(prod, pk, logit, ALU.mult).then_inc(*did(("prod", k)))
                after(("prod", k))
                v.tensor_reduce(p, by(prod), AX.X, ALU.add).then_inc(*did(("pick_prob", k)))
                after(("pick_prob", k))
            v.tensor_tensor(rsum, p1, p2, ALU.add).then_inc(*did("pick_sum"))
            v.tensor_tensor(prod, pick1, pick2, ALU.add).then_inc(*did("picks"))
            after("pick_sum")
            v.reciprocal(rsum, rsum).then_inc(*did("pick_rsum"))
            after("pick_rsum")
            for w, p in ((w1, p1), (w2_, p2)):
                v.tensor_tensor(w, p, rsum, ALU.mult).then_inc(*did("gates"))
            dve.wait_ge(*at("pe_did", "counts"))
            cn = ps[3][:, 0:NT * NEXP]
            v.tensor_copy(tot, ps[3][:, NT * NEXP:2 * NT * NEXP]).then_inc(*did("tile_counts"))
            v.tensor_copy(prefix[:, 0:NEXP], cn[:, 0:NEXP]).then_inc(*did("prefix0"))
            after("tile_counts")
            v.tensor_copy(nexp, tot[:, 0:NEXP]).then_inc(*did(("prefix", 0)))
            for t in range(1, NT):
                after(("prefix", t - 1))
                es = slice(t * NEXP, (t + 1) * NEXP)
                v.tensor_tensor(prefix[:, es], cn[:, es], nexp, ALU.add).then_inc(*did(("before", t)))
                after(("before", t))
                v.tensor_tensor(nexp, nexp, tot[:, es], ALU.add).then_inc(*did(("prefix", t)))
            after(("prefix", NT - 1))
            s5 = steps5.rearrange("p (e j) -> p e j", e=NEXP)
            v.tensor_tensor(s5, bc(nexp, NT), step128.unsqueeze(1).to_broadcast([P, NEXP, NT]), ALU.is_gt).then_inc(*did("steps"))
            after("steps")
            v.tensor_reduce(ctile, s5, AX.X, ALU.add).then_inc(*did("expert_tiles"))
            after("expert_tiles")
            v.tensor_tensor_scan(cend, ones[:, 0:NEXP], ctile, 0.0, ALU.mult, ALU.add).then_inc(*did("expert_end"))
            after("expert_end")
            v.tensor_tensor(base, cend, ctile, ALU.subtract).then_inc(*did("expert_start"))
            after("expert_start")
            v.tensor_scalar(base, base, float(P), None, ALU.mult).then_inc(*did("expert_base"))
            after("expert_base")
            v.tensor_tensor(by(prefix), by(prefix), base.unsqueeze(1).to_broadcast([P, NT, NEXP]), ALU.add).then_inc(*did("slot_all"))
            after("slot_all")
            for k, (pk, sl) in enumerate(((pick1, slot1), (pick2, slot2))):
                after("picks")
                if k:
                    after(("slot", 0))
                else:
                    dve.wait_ge(*at("pe_did", "counts"))
                v.tensor_tensor(prod, pk, prefix, ALU.mult).then_inc(*did(("slot_prod", k)))
                after(("slot_prod", k))
                v.tensor_reduce(sl, by(prod), AX.X, ALU.add).then_inc(*did(("slot", k)))
                after(("slot", k))
                v.tensor_copy(slot_u[:, k, :], sl).then_inc(*did("slots"))
            tc = tcmp.rearrange("p (i e) -> p i e", i=CAP)
            v.tensor_tensor(tc, bc(tile_no, NEXP), cend.unsqueeze(1).to_broadcast([P, CAP, NEXP]), ALU.is_ge).then_inc(*did("ended"))
            after("ended")
            v.tensor_reduce(texp, tc, AX.X, ALU.add).then_inc(*did("tile_expert"))
            after("tile_expert")
            v.tensor_scalar(texp, texp, float(NEXP - 1), float(P), ALU.min, ALU.mult).then_inc(*did("expert_row"))
            after("expert_row")
            v.tensor_scalar(texp, texp, part_no, None, ALU.add).then_inc(*did("expert_rows"))
            after("expert_rows")
            v.tensor_copy(weight_u, texp).then_inc(*did("experts"))
            dve.wait_ge(*at("pe_did", "slot_tokens"))
            v.tensor_copy(token_u, ps[4][:, 0:CAP]).then_inc(*did("tokens"))
            for i in range(CAP + 1):
                if i < CAP:
                    s = i % 2
                    dve.wait_ge(*at("pe_did", ("turn_h", i)))
                    if i >= 2:
                        dve.wait_ge(*at("pe_did", ("gu", i - 2)))
                    v.tensor_copy(hT[:, s, 4:8, :].rearrange("p k q -> p (k q)"), ps[1][:, :]).then_inc(*did(("turn_h", i)))
                    dve.wait_ge(*at("act_did", ("gu", i)))
                    if i >= 2:
                        dve.wait_ge(*at("pe_did", ("turn_act", i - 2)))
                    v.tensor_tensor(actg[:, s, :], act_in, ps[2 + s][:, DE:FE], ALU.mult).then_inc(*did(("gu", i)))
                    dve.wait_ge(*at("pe_did", ("turn_act", i)))
                    if i >= 2:
                        dve.wait_ge(*at("pe_did", ("down", i - 2)))
                    v.tensor_copy(actT[:, s, :], ps[4][:, 0:DE]).then_inc(*did(("turn_act", i)))
                if i:
                    i -= 1
                    dve.wait_ge(*at("pe_did", ("down", i)))
                    if i >= 2:
                        dve.wait_ge(*at(f"y_stored{i % 2}", i - 2))
                    v.tensor_copy(yrow[:, i % 2, 512:1024], ps[6][:, :]).then_inc(*did(("down", i)))
            for t in range(NT + 1):
                if t < NT:
                    ra, rb = comb_rows[t % 2]
                    gi = min(t, 1)
                    dve.wait_ge(*at(f"picks_landed{t % 2}", t))
                    v.tensor_scalar(ra, ra, w1[:, t:t + 1], None, ALU.mult).then_inc(*did(("gate_a", t)))
                    after(("gate_a", t))
                    v.scalar_tensor_tensor(ra, rb, w2_[:, t:t + 1], ra, ALU.mult, ALU.add).then_inc(*did(("gate_b", t)))
                    after(("gate_b", t))
                    dve.wait_ge(*at("act_did", ("spread", 11)))
                    v.tensor_tensor(ra, ra, mods[:, GATE2, gi, :], ALU.mult).then_inc(*did(("moe", t)))
                    after(("moe", t))
                    v.tensor_tensor(x1[:, t, :], x1[:, t, :], ra, ALU.add).then_inc(*did(("x2", t)))
                if t:
                    t -= 1
                    dve.wait_ge(*at("act_did", ("out", t)))
                    dve.wait_ge(*at("final_g_landed"))
                    after(("x2", t))
                    v.scalar_tensor_tensor(comb_rows[t % 2][0], x1[:, t, :], rstd[:, 1, t:t + 1], bc_row, ALU.mult, ALU.mult) \
                        .then_inc(*did(("out", t)))

        def post_pe(pe):
            T_ = nc.tensor
            scan_done(pe)

            def did(key):
                return up("pe_did", key)

            for k, t in ORDER:
                if k == "head":
                    if t:
                        pe.wait_ge(*at("dve_did", ("head", t - 1)))
                    T_.matmul(ps[3][:, :], loraT[:, 2, tcols(t)], g2_sb[:, :], start=True, stop=True)
                    for m in range(4):
                        x = T_.transpose(ps[4][:, m * P:(m + 1) * P], rkvT[:, 2, m, tcols(t)], ident[:, :])
                    x.then_inc(*did(("head", t)))
                elif k == "turn_a":
                    pe.wait_ge(*at("dve_did", ("head", t)))
                    if t:
                        pe.wait_ge(*at("act_did", ("turn_a", t - 1)))
                    for m in range(4):
                        x = T_.transpose(ps[5][:, m * P:(m + 1) * P], ytm[:, t, m * P:(m + 1) * P], ident[:, :])
                    x.then_inc(*did(("turn_a", t)))
                elif k == "ada":
                    pe.wait_ge(*at(f"ring_landed{t % 2}", ("ada", t)))
                    if t > 4:
                        pe.wait_ge(*at("dve_did", ("ada", t - 1)))
                    for c in range(KD):
                        x = T_.matmul(ps[0][0:2, :], silu_c[:, c, :], aring[:, t % 2, c, :], start=(c == 0), stop=(c == KD - 1))
                    x.then_inc(*did(("ada", t)))
                elif k == "spread":
                    pe.wait_ge(*at("dve_did", ("ada", t)))
                    pe.wait_ge(*at("pool_did", "consts"))
                    if t > 4:
                        pe.wait_ge(*at("dve_did" if (t - 1) // 2 - 2 == SCALE2 else "act_did", ("spread", t - 1)))
                    for gi in range(2):
                        x = T_.matmul(ps[1 + gi][:, :], group_row[:, gi, :], modrow2, start=True, stop=True)
                    x.then_inc(*did(("spread", t)))
                elif k == "mix":
                    pe.wait_ge(*at("act_did", ("turn_a", t)))
                    pe.wait_ge(*at("w_out_landed"))
                    if t:
                        pe.wait_ge(*at("dve_did", ("mixed", t - 1)))
                    for hf in range(2):
                        for c in [4, 5, 6, 7, 0, 1, 2, 3]:
                            lhs = catA[:, t % 2, c, :] if c < 4 else catBC[:, c - 4, t * P:(t + 1) * P]
                            x = T_.matmul(ps[6 + hf][:, :], lhs, wout[:, c, hf * 512:(hf + 1) * 512], start=(c == 4), stop=(c == 3))
                    x.then_inc(*did(("mix", t)))
                elif k == "h2":
                    pe.wait_ge(*at("dve_did", ("h2", t)))
                    pe.wait_ge(*(at("act_did", ("h2", t - 1)) if t else at("act_did", ("spread", 11))))
                    if t:
                        pe.wait_ge(*at("dve_did", ("h2_T", t - 1)))
                    for c in range(KD):
                        x = T_.transpose(ps[1 + c // 4][:, (c % 4) * P:(c % 4 + 1) * P], h2[:, t % 2, c * P:(c + 1) * P], ident[:, :])
                    x.then_inc(*did(("turn_h2", t)))
                    pe.wait_ge(*at("act_did", ("h2", t)))
                    pe.wait_ge(*at("dve_did", ("h2_T", t)))
                    pe.wait_ge(*at("norm2_landed"))
                    if t == 0:
                        pe.wait_ge(*at("dve_did", ("ada", 11)))
                    for c in range(KD):
                        x = T_.matmul(ps[0][:, t * NEXP:(t + 1) * NEXP], h2T[:, c, :], wr_sb[:, c, :], start=(c == 0), stop=(c == KD - 1))
                    x.then_inc(*did(("router", t)))
            pe.wait_ge(*at("dve_did", "picks"))
            T_.matmul(ps[3][:, 0:NT * NEXP], gmask[:, 0, 0, :], prod, start=True, stop=True)
            T_.matmul(ps[3][:, NT * NEXP:2 * NT * NEXP], ones, prod, start=True, stop=True).then_inc(*did("counts"))
            pe.wait_ge(*at("slots_read"))
            T_.transpose(ps[4][:, 0:CAP], stok[0:CAP, :], ident[0:CAP, 0:CAP]).then_inc(*did("slot_tokens"))
            def turn_h(i):
                pe.wait_ge(*at(f"rows_landed{i % 2}", i))
                if i:
                    pe.wait_ge(*at("act_did", ("turn_h", i - 1)))
                    pe.wait_ge(*at("dve_did", ("turn_h", i - 1)))
                hv = hrow[:, i % 2, :].rearrange("p (q k) -> p k q", k=KD)
                for c in range(KD):
                    x = T_.transpose(ps[c // 4][:, (c % 4) * P:(c % 4 + 1) * P], hv[:, c, :], ident[:, :])
                x.then_inc(*did(("turn_h", i)))

            def gate_up(i):
                s = i % 2
                pe.wait_ge(*at("act_did", ("turn_h", i)))
                pe.wait_ge(*at("dve_did", ("turn_h", i)))
                pe.wait_ge(*at(f"gu_landed{s}", i))
                if i >= 2:
                    pe.wait_ge(*at("dve_did", ("gu", i - 2)))
                for c in range(KD):
                    x = T_.matmul(ps[2 + s][:, :], hT[:, s, c, :], wgu[:, s, c, :], start=(c == 0), stop=(c == KD - 1))
                x.then_inc(*did(("gu", i)))

            def down(i):
                s = i % 2
                pe.wait_ge(*at("dve_did", ("gu", i)))
                if i:
                    pe.wait_ge(*at("dve_did", ("turn_act", i - 1)))
                else:
                    pe.wait_ge(*at("dve_did", "tokens"))
                av = actg[:, s, :].rearrange("p (q k) -> p k q", k=2)
                for c in range(2):
                    x = T_.transpose(ps[4][:, c * P:(c + 1) * P], av[:, c, :], ident[:, :])
                x.then_inc(*did(("turn_act", i)))
                pe.wait_ge(*at("dve_did", ("turn_act", i)))
                pe.wait_ge(*at(f"down_landed{s}", i))
                if i:
                    pe.wait_ge(*at("act_did", ("down", i - 1)))
                    pe.wait_ge(*at("dve_did", ("down", i - 1)))
                for hf in range(2):
                    for c in range(2):
                        x = T_.matmul(ps[5 + hf][:, :], actT[:, s, c * P:(c + 1) * P], wdn[:, s, c, hf * 512:(hf + 1) * 512],
                                      start=(c == 0), stop=(c == 1))
                x.then_inc(*did(("down", i)))

            turn_h(0)
            gate_up(0)
            for i in range(CAP):
                if i + 1 < CAP:
                    turn_h(i + 1)
                down(i)
                if i + 1 < CAP:
                    gate_up(i + 1)

        block = ctx.enter_context(nc.Block())
        @block.sync
        def _(sp):
            def rows(name, ap):
                s, n = PR[name]
                sp.dma_start(prow[s:s + n, :], ap).then_inc(*up16("params_landed"))

            def x_load(t):
                src = A["x_prompt"][0] if t == 0 else A["x_sample"][0, (t - 1) * P:t * P, :]
                if t >= 2:
                    sp.wait_ge(*at("xn", t - 2))
                    sp.wait_ge(*at("x_square", t - 2))
                sp.dma_start(xin[:, t % 2, :], src).then_inc(*up16(f"x_landed{t % 2}", t))

            def ring_load(n):
                kind, j = RING[n]
                if n >= 2:
                    sp.wait_ge(*last_use(n - 2))
                if kind == "ada":
                    src = A["ada_w"][0].rearrange("(k p) n -> p k n", p=P)[:, :, j * 512:(j + 1) * 512]
                    sp.dma_start(wring[:, n % 2, :, :], src).then_inc(*up16(f"ring_landed{n % 2}", n))
                    if j >= 1:
                        sp.wait_ge(*at("mod_row", j - 1))
                    sp.dma_start(adab, A["ada_b"][:, j * 512:(j + 1) * 512].to_broadcast([2, 512])) \
                        .then_inc(*up16("ada_b_landed", j))
                else:
                    src = A["w_in"][0].rearrange("(k p) n -> p k n", p=P)[:, :, C0[j]:C0[j] + CW[j]]
                    sp.dma_start(wring[:, n % 2, :, 0:CW[j]], src).then_inc(*up16(f"ring_landed{n % 2}", n))

            rows("c_ctx", A["c_ctx"].rearrange("(r p) -> r p", p=P))
            rows("c", A["c"].rearrange("o (r p) -> (o r) p", p=P))
            rows("norm1", A["norm1_g"].rearrange("o (r p) -> (o r) p", p=P))
            rows("norm2", A["norm2_g"].rearrange("o (r p) -> (o r) p", p=P))
            rows("mu", A["mu_shift"].rearrange("o (r p) -> (o r) p", p=P))
            for n in ("w0", "a0", "k_k", "k_a"):
                rows(n, A[n].rearrange("o d (r p) -> (o d r) p", p=P))
            rows("r_k", A["r_k"].rearrange("o (r h) c -> (o r) (h c)", h=2))
            rows("conv_b", A["conv_b"].rearrange("o (r p) -> (o r) p", p=P))
            rows("gmlp_bs", A["gmlp_bs"].rearrange("o g p -> (o g) p"))
            sp.dma_start(crow, A["conv_w"].rearrange("o k (r p) -> (o k r) p", p=P)).then_inc(*up16("params_landed"))
            x_load(0)
            x_load(1)
            sp.dma_start(wsrow, A["gmlp_ws"][0].rearrange("g p q -> p g q")).then_inc(*up16("ws_landed"))
            ring_load(0)
            x_load(2)
            x_load(3)
            ring_load(1)
            for i, n in enumerate(("gmlp_norm_g", "gmlp_norm_b", "beta_b", "conv_norm_g", "conv_norm_b", "beta_c")):
                sp.dma_start(bc_b[:, i, :], A[n].to_broadcast([P, 256])).then_inc(*up16("bc_landed"))
            for d in range(2):
                for i, n in enumerate(("w2", "a2")):
                    sp.dma_start(lora_w[d * HD:(d + 1) * HD, i, :], A[n][0, d]).then_inc(*up16("lora_w_landed"))
            sp.dma_start(g2_sb[:, :], A["g2"][0]).then_inc(*up16("lora_w_landed"))
            for n in range(2, len(RING)):
                ring_load(n)
                if n == 3:
                    x_load(4)
            scan_loads(sp)

        @block.gpsimd
        def _(pool):
            g = nc.gpsimd
            g.memset(same[:, :, :], 1.0).then_inc(*up("ones"))
            g.memset(gmask[:, :, :, :], 1.0).then_inc(*up("ones"))
            g.memset(keep[:, :], 1.0).then_inc(*up("ones", "all"))
            pool.wait_ge(*at("ones", "all"))
            for l in range(7):
                b = 1 << l
                v = same[:, l, :].rearrange("p (n b) -> p n b", b=b)
                g.affine_select(out=v, in_=v, pattern=[[-b, P // b], [0, b]], compare_op=ALU.is_ge, fill=0.0,
                                base=0, channel_multiplier=1).then_inc(*up("same_lower", l))
            for l in range(7):
                b = 1 << l
                v = same[:, l, :].rearrange("p (n b) -> p n b", b=b)
                pool.wait_ge(*at("same_lower", l))
                g.affine_select(out=v, in_=v, pattern=[[b, P // b], [0, b]], compare_op=ALU.is_ge, fill=0.0,
                                base=b - 1, channel_multiplier=-1).then_inc(*up("same", l))
            g.memset(keep[:, 0:1], 0.0).then_inc(*up("const"))
            g.memset(keep[:, SEQ:SEQ + 2], 0.0).then_inc(*up("const"))
            for t in range(2, NT):
                g.memset(keep[:, col(t):col(t) + 1], 0.0).then_inc(*up("const"))
            for d in range(2):
                s = 1 - 2 * d
                for q in range(2):
                    v = gmask[:, d, q, :]
                    g.affine_select(out=v, in_=v, pattern=[[s, P]], compare_op=ALU.is_ge if q else ALU.is_gt,
                                    fill=0.0, base=0, channel_multiplier=-s).then_inc(*up("const"))
            g.memset(glu[:, :, :, :], 0.0).then_inc(*up("const", "all"))
            scan_pool(pool)

        @block.scalar
        def _(act):
            a = nc.scalar
            act.wait_ge(*at("pcol"))
            for gi, n in enumerate(("c_ctx", "c")):
                s, w = PR[n]
                a.activation(silu_c[:, :, gi], pcol[:, s:s + w], ACT.Silu).then_inc(*up("silu_c"))
            act.wait_ge(*at("eps"))
            for t in range(NT):
                act.wait_ge(*at(f"x_landed{t % 2}", t))
                if t == 0:
                    act.wait_ge(*at("ws_T"))
                else:
                    act.wait_ge(*at("x_square", t - 1))
                a.activation(gl[:, 0:2, :].rearrange("p t n -> p (t n)"), xin[:, t % 2, :], ACT.Square,
                             accum_out=sumsq[:, 0, t:t + 1]).then_inc(*up("x_square", t))
                act.wait_ge(*at("x_square", t))
                a.activation(rstd[:, 0, t:t + 1], sumsq[:, 0, t:t + 1], ACT.Abs_reciprocal_sqrt, bias=eps[:, 0:1],
                             scale=1.0 / D).then_inc(*up("rstd1", t))
                if t >= 2:
                    h1_act(act, t - 2)
            h1_act(act, NT - 2)
            h1_act(act, NT - 1)

            for i, (c, m) in enumerate(TILES):
                act.wait_ge(*at("proj", (c, m)))
                lat, ctx_ = ps[4 + 2 * (i % 2)], ps[5 + 2 * (i % 2)]
                if c == 5:
                    f, name, dst = (ACT.Copy, "conv_a", acc[:, m % 2, :]) if m < 2 else (ACT.Sigmoid, "conv_gate", psc[:, m % 2, 0:T])
                    a.activation(dst[:, 0:P], ctx_[:, 0:P], f).then_inc(*up(name))
                    a.activation(dst[:, P:T], lat[:, :], f).then_inc(*up(name, m))
                    if m == 3:
                        for t in range(NT):
                            act.wait_ge(*at("proj_B", t))
                            a.activation(gl[:, t, :], ps[2 + t % 2][:, :], ACT.Gelu_apprx_tanh).then_inc(*up("gelu", t))
                        act.wait_ge(*at("pad_zero"))
                        act.wait_ge(*at("conv_glu"))
                    continue
                n = i - 4
                s = n % 2
                j = c * 4 + m
                if n >= 2:
                    act.wait_ge(*at("mixed", n - 2))
                a.activation(praw[:, s, 1:1 + P], ctx_[:, 0:P], ACT.Copy).then_inc(*up("p_raw"))
                a.activation(praw[:, s, P + 2:P + 2 + LAT], lat[:, :], ACT.Copy).then_inc(*up("p_raw"))
                a.activation(psc[:, s, 0:P], ctx_[:, 0:P], ACT.Copy, scale=mu_keep[:, j:j + 1]).then_inc(*up("p_raw"))
                a.activation(psc[:, s, P + 1:TW], lat[:, :], ACT.Copy, scale=mu_keep[:, j:j + 1]).then_inc(*up("p_raw", n))
                if n == 2:
                    act.wait_ge(*at("gmlp_stat"))
                    a.activation(rstd[:, 1, :], mv[:, 0, :, 1], ACT.Abs_reciprocal_sqrt, bias=eps[:, 1:2]).then_inc(*up("gmlp_rstd"))
                if n == 3:
                    act.wait_ge(*at("mixed", 2))
                    a.activation(loraT[:, 0, :], loraT[:, 0, :], ACT.Tanh).then_inc(*up("lora"))
                    a.activation(loraT[:, 2, :], loraT[:, 2, :], ACT.Sigmoid).then_inc(*up("lora"))
                if n == 7:
                    for t in range(NT):
                        act.wait_ge(*at("gmlp_prod", t))
                        a.activation(gl[:, t, 256:512], gl[:, t, 0:256], ACT.Square, accum_out=sumsq[:, 1, t:t + 1]) \
                            .then_inc(*up("gmlp_square", t))
                    act.wait_ge(*at("gmlp_square", NT - 1))
                    a.activation(rstd[:, 2, :], sumsq[:, 1, :], ACT.Abs_reciprocal_sqrt, bias=eps[:, 0:1], scale=1.0 / DB) \
                        .then_inc(*up("gmlp_rrms"))
                if n == 11:
                    cat_copy(act, 0, "yb_T")
            act.wait_ge(*at("conv_stat"))
            a.activation(rstd[:, 3, :], mv[:, 1, :, 1], ACT.Abs_reciprocal_sqrt, bias=eps[:, 1:2]).then_inc(*up("conv_rstd"))
            for t in range(NT):
                act.wait_ge(*at("conv_norm", t))
                a.activation(gl[:, t, 256:512], gl[:, t, 0:256], ACT.Silu).then_inc(*up("conv_silu", t))
            for t in range(NT):
                act.wait_ge(*at("conv_silu", t))
                a.activation(gl[:, t, 0:256], gl[:, t, 256:512], ACT.Square, accum_out=sumsq[:, 2, t:t + 1]) \
                    .then_inc(*up("conv_square", t))
            act.wait_ge(*at("conv_square", NT - 1))
            a.activation(rstd[:, 4, :], sumsq[:, 2, :], ACT.Abs_reciprocal_sqrt, bias=eps[:, 0:1], scale=1.0 / DC) \
                .then_inc(*up("conv_rrms"))
            cat_copy(act, 2, "yc_T")
            scan_act(act)

        @block.vector
        def _(dve):
            v = nc.vector
            for h in range(2):
                for q in range(2):
                    v.memset(headsel[64 * h:64 * h + 64, q:q + 1], float(h == q)).then_inc(*up("head_select"))
            v.memset(eps[:, 0:1], EPS_RMS).then_inc(*up("eps"))
            v.memset(eps[:, 1:2], EPS_LN).then_inc(*up("eps"))
            v.memset(eps[:, 2:3], EPS_LNX).then_inc(*up("eps"))
            dve.wait_ge(*at("same", 6))
            v.tensor_copy(ident[:, :], same[:, 0, :]).then_inc(*up("ident", 0))
            v.tensor_copy(halfones[:, :], same[:, 6, :]).then_inc(*up("ident", 1))
            for l in range(7):
                v.tensor_tensor(level[:, l, :], same[:, l + 1, :], same[:, l, :], ALU.subtract).then_inc(*up("level"))
            dve.wait_ge(*at("param_T"))
            v.tensor_copy(pcol[:, :], ps[0][:, 0:NPR]).then_inc(*up("pcol"))
            v.tensor_copy(ccol, ps[0][:, 128:128 + 2 * CONV_K]).then_inc(*up("pcol"))
            dve.wait_ge(*at("ws_T"))
            v.tensor_copy(wsT.rearrange("p g q -> p (g q)"), ps[1][:, :]).then_inc(*up("wsT"))
            dve.wait_ge(*at("pcol"))
            s, w = PR["mu"]
            v.tensor_scalar(mu_keep, pcol[:, s:s + w], -1.0, 1.0, ALU.mult, ALU.add).then_inc(*up("mu_made"))
            v.tensor_scalar(mu_half, pcol[:, s:s + w], 0.5, None, ALU.mult).then_inc(*up("mu_made"))
            s, w = PR["k_a"]
            v.tensor_scalar(ka_keep[:, :], pcol[:, s:s + w], -1.0, 1.0, ALU.mult, ALU.add).then_inc(*up("mu_made"))

            def xnorm(t):
                dve.wait_ge(*at("rstd1", t))
                if t >= 2:
                    dve.wait_ge(*at("xn_T", (t - 2, 1)))
                v.tensor_scalar(xn[:, t % 2, :], xin[:, t % 2, :], rstd[:, 0, t:t + 1], None, ALU.mult).then_inc(*up("xn", t))

            xnorm(0)
            xnorm(1)
            for j in range(4):
                ada_row(dve, j)
            dve.wait_ge(*at("mod_row_used", 3))
            mt = ps[0][:, 256:256 + 64].rearrange("p (w k g) -> p w k g", w=4, k=KD)
            v.tensor_copy(modT[:, 0:2, :, :], mt[:, 0:2, :, :]).then_inc(*up("mod1"))
            dve.wait_ge(*at("mod1"))
            for gi in range(2):
                v.scalar_tensor_tensor(gain[:, 0, :, gi], modT[:, SC1, :, gi], 1.0, pcol[:, 0:8], ALU.add, ALU.mult) \
                    .then_inc(*up("gain1"))
            dve.wait_ge(*at("gain1"))
            for t in range(NT):
                gi = min(t, 1)
                for hf in range(1, 2):
                    dve.wait_ge(*at("xn_T", (t, hf)))
                    for k in range(4, 8):
                        v.tensor_scalar(h1T[:, k, t * P:(t + 1) * P], ps[4 + (2 * t + hf) % 4][:, (k % 4) * P:(k % 4 + 1) * P],
                                        gain[:, 0, k, gi:gi + 1], modT[:, SH1, k, gi:gi + 1], ALU.mult, ALU.add) \
                            .then_inc(*up("h1T_dve", (t, hf)))
                if t + 2 < NT:
                    xnorm(t + 2)
            v.memset(praw[:, :, 0:1], 0.0).then_inc(*up("pad_zero"))
            v.memset(praw[:, :, P + 1:P + 2], 0.0).then_inc(*up("pad_zero"))
            v.memset(praw[:, :, 642:643], 0.0).then_inc(*up("pad_zero"))
            dve.wait_ge(*at("const", "all"))
            dve.wait_ge(*at("conv_a", 1))
            dve.wait_ge(*at("conv_gate", 3))
            for c in range(2):
                va, ga = acc[:, c, :], psc[:, c, 0:T]
                v.tensor_tensor(glu[:, c, :, HALF:HALF + GRID], va.rearrange("p (r w) -> p r w", w=GRID),
                                ga.rearrange("p (r w) -> p r w", w=GRID), ALU.mult).then_inc(*up("conv_glu"))
                v.tensor_tensor(glu[:, c, 0, HALF + GRID:CONVW], va[:, GRID:GRID + HALF], ga[:, GRID:GRID + HALF], ALU.mult) \
                    .then_inc(*up("conv_glu"))
                v.tensor_tensor(glu[:, c, 1, 0:HALF], va[:, GRID - HALF:GRID], ga[:, GRID - HALF:GRID], ALU.mult) \
                    .then_inc(*up("conv_glu"))
            dve.wait_ge(*at("conv_glu"))
            v.memset(psc[:, :, P:P + 1], 0.0).then_inc(*up("pad_zero"))
            dve.wait_ge(*at("bc_landed"))

            cb = PR["conv_b"][0]

            def tap(i):
                k, c = i // 2, i % 2
                src = glu[:, c, :, k:k + GRID]
                dst = acc[:, c, :].rearrange("p (r w) -> p r w", w=GRID)
                if k == 0:
                    v.tensor_scalar(dst, src, ccol[:, c:c + 1], pcol[:, cb + c:cb + c + 1], ALU.mult, ALU.add) \
                        .then_inc(*up("conv_tap", i))
                else:
                    dve.wait_ge(*at("conv_tap", i - 2))
                    v.scalar_tensor_tensor(dst, src, ccol[:, 2 * k + c:2 * k + c + 1], dst, ALU.mult, ALU.add) \
                        .then_inc(*up("conv_tap", i))

            taps = iter(range(2 * CONV_K))
            for n, (c, m) in enumerate(ATILES):
                j, s = c * 4 + m, n % 2
                dve.wait_ge(*at("p_raw", n))
                if n:
                    dve.wait_ge(*at("mixed", n - 1))
                v.tensor_tensor(nbsum, praw[:, s, 0:TW], praw[:, s, 2:TW + 2], ALU.add).then_inc(*up("neighbours", n))
                dst = rkvT[:, c, m, :] if c < 3 else loraT[:, m, :]
                for _ in range(2):
                    for i in taps:
                        tap(i)
                        break
                dve.wait_ge(*at("neighbours", n))
                v.scalar_tensor_tensor(dst, nbsum, mu_half[:, j:j + 1], psc[:, s, :], ALU.mult, ALU.add).then_inc(*up("mixed", n))
                for _ in range(3):
                    for i in taps:
                        tap(i)
                        break
                if n == 0:
                    for t in range(NT):
                        dve.wait_ge(*at("gelu", t))
                        v.bn_stats(bst[:, 0, t, :], gl[:, t, 256:512]).then_inc(*up("gmlp_bn", t))
                    for t in range(NT):
                        dve.wait_ge(*at("gmlp_bn", t))
                        v.bn_aggr(mv[:, 0, t, :], bst[:, 0, t, :]).then_inc(*up("gmlp_stat"))
                if n == 2:
                    dve.wait_ge(*at("gmlp_rstd"))
                    norm_rows(dve, "gmlp", 0, 1, lambda t: gl[:, t, 256:512], lambda t: gl[:, t, 256:512], GN_G, GN_B)
                if n == 5:
                    for t in range(NT):
                        b, o = turned(t)
                        dve.wait_ge(*at("spatial", bank_done(t)))
                        bs = PR["gmlp_bs"][0]
                        for q in range(4):
                            u = gl[:, t, q * HD:(q + 1) * HD]
                            v.scalar_tensor_tensor(u, ps[b][:, o + q * HD:o + (q + 1) * HD], pcol[:, bs + q:bs + q + 1], u,
                                                   ALU.add, ALU.mult).then_inc(*up("gmlp_prod", t))
                if n == 8:
                    dve.wait_ge(*at("gmlp_rrms"))
                    for t in range(NT):
                        v.scalar_tensor_tensor(gl[:, t, 0:256], gl[:, t, 0:256], rstd[:, 2, t:t + 1], bc_b[:, BETA_B, :],
                                               ALU.mult, ALU.mult).then_inc(*up("yb", t))
            for t in range(NT):
                b, o = turned(t)
                dve.wait_ge(*at("conv_T", bank_done(t)))
                v.bn_stats(bst[:, 1, t, :], ps[b][:, o:o + 256]).then_inc(*up("conv_bn", t))
            for t in range(NT):
                dve.wait_ge(*at("conv_bn", t))
                v.bn_aggr(mv[:, 1, t, :], bst[:, 1, t, :]).then_inc(*up("conv_stat"))
            dve.wait_ge(*at("conv_rstd"))
            dve.wait_ge(*at("yb_T", NT - 1))
            norm_rows(dve, "conv", 1, 3, lambda t: ps[turned(t)[0]][:, turned(t)[1]:turned(t)[1] + 256],
                      lambda t: gl[:, t, 0:256], CN_G, CN_B)
            dve.wait_ge(*at("conv_rrms"))
            for t in range(NT):
                v.scalar_tensor_tensor(gl[:, t, 0:256], gl[:, t, 256:512], rstd[:, 4, t:t + 1], bc_b[:, BETA_C, :],
                                       ALU.mult, ALU.mult).then_inc(*up("yc", t))
            scan_dve(dve)

        @block.tensor
        def _(pe):
            T_ = nc.tensor
            pe.wait_ge(*at("params_landed"))
            pe.wait_ge(*at("ident", 0))
            T_.transpose(ps[0][:, 0:NPR], prow, ident[0:NPR, 0:NPR])
            T_.transpose(ps[0][:, 128:128 + 2 * CONV_K], crow, ident[0:2 * CONV_K, 0:2 * CONV_K]).then_inc(*up("param_T"))
            pe.wait_ge(*at("ws_landed"))
            for q in range(4):
                x = T_.transpose(ps[1][:, q * P:(q + 1) * P], wsrow[:, q, :], ident[:, :])
            x.then_inc(*up("ws_T"))

            def xn_T(t):
                pe.wait_ge(*at("xn", t))
                for hf in range(2):
                    n = 2 * t + hf
                    if n >= 4:
                        q = ((n - 4) // 2, (n - 4) % 2)
                        pe.wait_ge(*at("h1T_dve" if hf else "h1T_act", q))
                    for i in range(4):
                        x = T_.transpose(ps[4 + n % 4][:, i * P:(i + 1) * P], xn[:, t % 2, (4 * hf + i) * P:(4 * hf + i + 1) * P],
                                         ident[:, :])
                    x.then_inc(*up("xn_T", (t, hf)))

            xn_T(0)
            xn_T(1)
            pe.wait_ge(*at("silu_c"))
            for n in range(4):
                ada_mm(pe, n)
                ada_cols(pe, n)
            for t in range(2, NT):
                xn_T(t)
            pe.wait_ge(*at("h1T_act", (NT - 1, 0)))
            pe.wait_ge(*at("h1T_dve", (NT - 1, 1)))
            i = 0
            for n, (kind, c) in enumerate(RING):
                if kind != "proj":
                    continue
                s = n % 2
                pe.wait_ge(*at(f"ring_landed{s}", n))
                if c == 4:
                    for t in range(NT):
                        if t >= 2:
                            pe.wait_ge(*at("gelu", t - 2))
                        for k in range(KD):
                            x = T_.matmul(ps[2 + t % 2][:, :], h1T[:, k, t * P:(t + 1) * P], wring[:, s, k, :],
                                          start=(k == 0), stop=(k == KD - 1))
                        x.then_inc(*up("proj_B", t))
                    continue
                for m in range(CW[c] // P):
                    if i >= 2:
                        cp, mp = TILES[i - 2]
                        if cp == 5:
                            pe.wait_ge(*at("conv_a" if mp < 2 else "conv_gate", mp))
                        else:
                            pe.wait_ge(*at("p_raw", i - 2 - 4))
                    lat, ctx_ = ps[4 + 2 * (i % 2)], ps[5 + 2 * (i % 2)]
                    for k in range(KD):
                        w = wring[:, s, k, m * P:(m + 1) * P]
                        T_.matmul(ctx_[:, 0:P], w, h1T[:, k, 0:P], start=(k == 0), stop=(k == KD - 1))
                        x = T_.matmul(lat[:, :], w, h1T[:, k, P:T], start=(k == 0), stop=(k == KD - 1))
                    x.then_inc(*up("proj", (c, m)))
                    a_i = i - 4
                    if a_i == 4:
                        for t in range(NT):
                            pe.wait_ge(*at("gmlp_norm", t))
                            if t == 0:
                                pe.wait_ge(*at("wsT"))
                                pe.wait_ge(*at("gelu", NT - 1))
                            b, o = turned(t)
                            for q in range(4):
                                x = T_.matmul(ps[b][:, o + q * HD:o + (q + 1) * HD], wsT[:, q, :],
                                              gl[:, t, 256 + q * HD:256 + (q + 1) * HD], start=True, stop=True)
                            x.then_inc(*up("spatial", t))
                    if a_i == 10:
                        turn(pe, "yb_T", "yb", lambda t: [gl[:, t, c * P:(c + 1) * P] for c in range(2)])
                    i += 1
            pe.wait_ge(*at("conv_tap", 2 * CONV_K - 1))
            pe.wait_ge(*at("catBC", (0, 2)))
            for t in range(NT):
                b, o = turned(t)
                for c in range(2):
                    x = T_.transpose(ps[b][:, o + c * P:o + (c + 1) * P], acc[:, c, t * P:(t + 1) * P], ident[:, :])
                x.then_inc(*up("conv_T", t))
            turn(pe, "yc_T", "yc", lambda t: [gl[:, t, c * P:(c + 1) * P] for c in range(2)])
            scan_pe(pe)


INPUTS = ['x_prompt', 'x_sample', 'state_rwkv', 'c', 'c_ctx', 'norm1_g', 'norm2_g', 'ada_w', 'ada_b', 'w_in', 'mu_shift',
          'w0', 'w2', 'a0', 'a2', 'k_k', 'k_a', 'g2', 'r_k', 'lnx_g', 'lnx_b', 'gmlp_norm_g', 'gmlp_norm_b', 'gmlp_ws',
          'gmlp_bs', 'beta_b', 'conv_w', 'conv_b', 'conv_norm_g', 'conv_norm_b', 'beta_c', 'w_out', 'w_router', 'b_router',
          'moe_w_gu', 'moe_w_down', 'final_g']
OUTPUTS = [(1, 128, 1024), (1, 512, 1024), (1, 1, 2, 8, 64, 64)]


def kernel(**inputs):
    import numpy as np
    import concourse.bacc as bacc
    from concourse.bass_utils import run_bass_kernel_spmd

    known = None
    for _ in range(2):
        nc = bacc.Bacc("TRN2", target_bir_lowering=False, num_devices=1)
        arrays, A = {}, {}
        for name in INPUTS:
            a = np.ascontiguousarray(inputs[name])
            arrays[f"in_{name}_dram"] = a
            A[name] = nc.dram_tensor(f"in_{name}_dram", a.shape, mybir.dt.from_np(a.dtype), kind="ExternalInput").ap()
        outs = [nc.dram_tensor(f"out_{i}_dram", shape, F32, kind="ExternalOutput").ap() for i, shape in enumerate(OUTPUTS)]
        counts = Counts(known)
        build(nc, A, outs, counts)
        known = counts.seen
    r = run_bass_kernel_spmd(nc, [arrays], core_ids=[0])
    return tuple(r.results[0][f"out_{i}_dram"] for i in range(len(OUTPUTS)))
```

```python
from contextlib import ExitStack

import concourse.bass as bass
from concourse import mybir

ALU = mybir.AluOpType
ACT = mybir.ActivationFunctionType
AX = mybir.AxisListType
F32 = mybir.dt.float32
I32 = mybir.dt.int32
U32 = mybir.dt.uint32

P = 128


class Counts:

    def __init__(self, known):
        self.known, self.seen, self.total, self.sems = known, {}, {}, {}

    def open(self, nc, ctx):
        self.nc, self.ctx = nc, ctx

    def sem(self, name):
        if name not in self.sems:
            self.sems[name] = self.ctx.enter_context(self.nc.semaphore(name))
        return self.sems[name]

    def up(self, name, key=None, by=1):
        self.total[name] = self.total.get(name, 0) + by
        self.seen[(name, key)] = self.seen[(name, None)] = self.total[name]
        return self.sem(name), by

    def at(self, name, key=None):
        return self.sem(name), self.known[(name, key)] if self.known is not None else 1


def build(nc, A, outs, counts):
    D = 1024
    KD = D // P
    NT = 5
    SEQ, LAT = 128, 512
    T = SEQ + LAT
    TW = T + 1
    DA, DB, DC = 512, 256, 256
    HD = 64
    NH = DA // HD
    CONV_K = 31
    HALF = CONV_K // 2
    GRID = 64
    COLS_A = 1920
    NEXP = 16
    EPS_RMS, EPS_LN, EPS_LNX = 1e-6, 1e-5, 64e-5
    up, at = counts.up, counts.at

    def up16(name, key=None):
        return up(name, key, 16)

    def col(t):
        return 0 if t == 0 else 1 + t * P

    ctx = ExitStack()
    with ctx:
        counts.open(nc, ctx)

        def sb(name, shape, dt=F32):
            return ctx.enter_context(nc.sbuf_tensor(name, shape, dt))

        ps = [ctx.enter_context(nc.psum_tensor(f"bank{i}", [P, 512], F32)) for i in range(8)]

        ident = sb("ident", [P, P])
        halfones = sb("half_ones", [P, P])
        level = sb("level_mask", [P, 7, P])
        gmask = sb("causal_mask", [P, 2, 2, P])
        keep = sb("scan_keep", [P, TW])
        headsel = sb("head_select", [P, 2])

        PR = dict(norm1=(0, 8), norm2=(8, 8), mu=(16, 15), w0=(31, 8), a0=(39, 8), k_k=(47, 8), k_a=(55, 8),
                  r_k=(63, 4), conv_b=(67, 2), c_ctx=(69, 8), c=(77, 8), gmlp_bs=(85, 4))
        NPR = 89
        pcol = sb("param_cols", [P, NPR])
        ka_keep = sb("ka_keep", [P, 8])
        eps = sb("eps", [P, 4])
        GN_G, GN_B, BETA_B, CN_G, CN_B, BETA_C = range(6)
        silu_c = sb("silu_c", [P, KD, 2])
        modT = sb("mod_cols", [P, 2, KD, 2])
        SH1, SC1 = range(2)
        gain = sb("gain_cols", [P, 1, KD, 2])
        rkvT = sb("rkvT", [P, 3, 4, TW])
        loraT = sb("loraT", [P, 3, TW])
        lora_w = sb("lora_w", [P, 2, DA])
        g2_sb = sb("g2", [P, DA])
        sumsq = sb("sum_squares", [P, 3, NT])
        rstd = sb("rstd", [P, 5, NT])
        mv = sb("mean_var", [P, 2, NT, 2])
        bst = sb("bn_stats", [P, 2, NT, 6])
        catBC = sb("catBC", [P, 4, T])

        AR = 36752
        arena = sb("arena", [P, AR])
        pos = [0]

        def carve(n, at_=None):
            if at_ is not None:
                pos[0] = at_
            v = arena[:, pos[0]:pos[0] + n]
            pos[0] += n
            assert pos[0] <= AR, pos[0]
            return v

        def region(ap):
            at_ = [0]

            def take(n):
                v = ap[:, at_[0]:at_[0] + n]
                at_[0] += n
                assert at_[0] <= ap.shape[1], at_[0]
                return v
            return take

        wring = carve(2 * KD * 512).rearrange("p (s k n) -> p s k n", s=2, k=KD)
        h1T = carve(KD * T).rearrange("p (k t) -> p k t", k=KD)
        CONVW = GRID + 2 * HALF
        NROW = T // GRID
        NORM = pos[0]
        xin = carve(2 * D).rearrange("p (s d) -> p s d", s=2)
        xn = carve(2 * D).rearrange("p (s d) -> p s d", s=2)
        nend = pos[0]
        praw = carve(2 * 643, at_=NORM).rearrange("p (s t) -> p s t", s=2)
        psc = carve(2 * TW).rearrange("p (s t) -> p s t", s=2)
        nbsum = carve(TW)
        gl = carve(NT * 512, at_=nend).rearrange("p (t n) -> p t n", t=NT)
        glu = carve(2 * NROW * CONVW).rearrange("p (c r w) -> p c r w", c=2, r=NROW)
        acc = carve(2 * T).rearrange("p (c t) -> p c t", c=2)
        same = carve(8 * P).rearrange("p (l q) -> p l q", l=8)
        bc_b = carve(6 * 256).rearrange("p (i n) -> p i n", i=6)
        wsT = carve(4 * P).rearrange("p (g q) -> p g q", g=4)
        modrow = carve(512)[0:2, :]
        adab = carve(512)[0:2, :]
        prow = carve(P)[0:NPR, :]
        crow = carve(P)[0:2 * CONV_K, :]
        ccol, mu_keep, mu_half = carve(2 * CONV_K), carve(15), carve(15)
        wsrow = gl[:, 4, :].rearrange("p (g q) -> p g q", g=4)


        CHUNKS = [5, 4, 3, 1, 0, 2]
        CW = {c: COLS_A - 3 * 512 if c == 3 else 512 for c in range(6)}
        C0 = {c: c * 512 if c < 4 else COLS_A + (c - 4) * 512 for c in range(6)}
        RING = [("ada", j) for j in range(4)] + [("proj", c) for c in CHUNKS] + [("ada", j) for j in range(4, 12)]
        mod_dram = nc.dram_tensor("modulations", (2, 8 * 512), F32).ap()
        LATE_ADA = [RING.index(("ada", j)) for j in range(4, 12)]
        TILES = [(c, m) for c in CHUNKS if c != 4 for m in range(CW[c] // P)]
        ATILES = [x for x in TILES if x[0] != 5]

        def last_use(n):
            kind, j = RING[n]
            if kind == "ada":
                return at("ada_mm", j)
            return at("proj_B", NT - 1) if j == 4 else at("proj", (j, CW[j] // P - 1))

        TURN = [(1, 0, 2), (3, 2, 2), (2, 4, 1)]

        def turned(t):
            return ((1, 0), (1, 256), (3, 0), (3, 256), (2, 0))[t]

        def bank_done(t):
            return (1, 1, 3, 3, 4)[t]

        def h1_act(act, t):
            gi = min(t, 1)
            act.wait_ge(*at("gain1"))
            act.wait_ge(*at("mod1"))
            act.wait_ge(*at("xn_T", (t, 0)))
            for k in range(4):
                nc.scalar.activation(h1T[:, k, t * P:(t + 1) * P], ps[4 + 2 * t % 4][:, k * P:(k + 1) * P],
                                     ACT.Identity, bias=modT[:, SH1, k, gi:gi + 1], scale=gain[:, 0, k, gi:gi + 1]) \
                    .then_inc(*up("h1T_act", (t, 0)))

        def cat_copy(act, c0, name):
            for b, t0, n in TURN:
                act.wait_ge(*at(name, t0 + n - 1))
                for c in range(2):
                    src = ps[b][:, 0:n * 256].rearrange("p (t c q) -> p c t q", t=n, c=2)[:, c]
                    dst = catBC[:, c0 + c, t0 * P:(t0 + n) * P].rearrange("p (t q) -> p t q", q=P)
                    nc.scalar.copy(dst, src).then_inc(*up("catBC", (c0, b)))

        def row_made(j):
            return at("mod_row" if j < 4 else "late_mod_row", j)

        def late_row(act, i):
            j = RING[LATE_ADA[i]][1]
            act.wait_ge(*at("ada_mm", j))
            act.wait_ge(*(at("mod_stored", j - 1) if j > 4 else at("mod_row_used", 3)))
            nc.scalar.copy(modrow, ps[6][0:2, :]).then_inc(*up("mod_row_copy", j))

        def ada_row(dve, j):
            dve.wait_ge(*at("ada_mm", j))
            dve.wait_ge(*at("ada_b_landed", j))
            if j >= 1:
                dve.wait_ge(*at("mod_row_used", j - 1))
            nc.vector.tensor_tensor(modrow, ps[2][0:2, :], adab, ALU.add).then_inc(*up("mod_row", j))

        def norm_rows(dve, name, i, r, src, dst, g, b):
            v = nc.vector
            for t in range(NT):
                v.tensor_scalar(dst(t), src(t), mv[:, i, t, 0:1], rstd[:, r, t:t + 1], ALU.subtract, ALU.mult) \
                    .then_inc(*up(name + "_centred", t))
            for t in range(NT):
                dve.wait_ge(*at(name + "_centred", t))
                v.tensor_tensor(dst(t), dst(t), bc_b[:, g, :], ALU.mult).then_inc(*up(name + "_scaled", t))
            for t in range(NT):
                dve.wait_ge(*at(name + "_scaled", t))
                v.tensor_tensor(dst(t), dst(t), bc_b[:, b, :], ALU.add).then_inc(*up(name + "_norm", t))

        def ada_mm(pe, n):
            kind, j = RING[n]
            pe.wait_ge(*at(f"ring_landed{n % 2}", n))
            if j >= 1:
                pe.wait_ge(*row_made(j - 1))
            if j == 4:
                pe.wait_ge(*at("p_raw", len(ATILES) - 2))
            for k in range(KD):
                x = nc.tensor.matmul(ps[2 if j < 4 else 6][0:2, :], silu_c[:, k, :], wring[:, n % 2, k, :], start=(k == 0), stop=(k == KD - 1))
            x.then_inc(*up("ada_mm", j))

        def ada_cols(pe, j):
            pe.wait_ge(*at("mod_row", j))
            which = (SH1, SC1)[j // 2]
            for i in range(4):
                o = 256 + (which * KD + (j % 2) * 4 + i) * 2
                x = nc.tensor.transpose(ps[0][:, o:o + 2], modrow[:, i * P:(i + 1) * P], ident[0:2, 0:2])
            x.then_inc(*up("mod_row_used", j))

        def turn(pe, name, src_name, src):
            for t in range(NT):
                b, o = turned(t)
                pe.wait_ge(*at(src_name, t))
                for c in range(2):
                    x = nc.tensor.transpose(ps[b][:, o + c * P:o + (c + 1) * P], src(t)[c], ident[:, :])
                x.then_inc(*up(name, t))

        QT, RT, BT, KT = range(4)
        qrkb = carve(2 * 2 * 4 * TW, at_=0).rearrange("p (r d i t) -> p r d i t", r=2, d=2, i=4)
        SCRATCH0 = pos[0]
        lw, iclr, cum, excl, rn, kk, kt, ktsum = [carve(TW) for _ in range(8)]
        mats = carve(4 * 4 * 512).rearrange("p (s u i q) -> p s u i q", s=4, u=4, i=4)
        MAT_N, MAT_NR, MAT_L, MAT_LR = range(4)
        invT = carve(4 * 512).rearrange("p (s u q) -> p s u q", s=4, u=4)
        inv = carve(2 * 512).rearrange("p (s u q) -> p s u q", s=2, u=4)
        wmat = carve(2 * 512).rearrange("p (s u q) -> p s u q", s=2, u=4)
        nlev = carve(2 * 512).rearrange("p (s u q) -> p s u q", s=2, u=4)
        kbtm = carve(4 * 512).rearrange("p (s d i c) -> p s d i c", s=4, d=2, i=2)
        vtm = carve(2 * NT * P).rearrange("p (r t c) -> p r t c", r=2, t=NT)
        xsb = carve(2 * 256).rearrange("p (s c) -> p s c", s=2)
        usb = carve(2 * 256).rearrange("p (s c) -> p s c", s=2)
        YTM0 = pos[0]
        ytm = carve(NT * DA).rearrange("p (t c) -> p t c", t=NT)
        state = carve(2 * 256).rearrange("p (r d c) -> p r d c", r=2, d=2)
        stin = carve(256).rearrange("p (d c) -> p d c", d=2)
        stout = carve(256).rearrange("p (d c) -> p d c", d=2)
        edge = carve(2 * 20).rearrange("p (r d i t) -> p r d i t", r=2, d=2, i=2)
        eedge = carve(2 * 20).rearrange("p (r d i t) -> p r d i t", r=2, d=2, i=2)
        comb = carve(2 * 6).rearrange("p (r d j) -> p r d j", r=2, d=2)
        bonus = sb("bonus", [P, NT, NH])
        DECAY = float(2.718281828459045 ** -0.5)

        BATCH = [(m, s) for m in range(4) for s in range(NT)]
        PAIRS = [(2 * q, 2 * q + 1) for q in range(len(BATCH) // 2)]

        def tile_of(d, s):
            return s if (s == 0 or d == 0) else NT - s

        def merge(main, extra):
            out, k = [], 0
            for i, x in enumerate(main):
                out.append(x)
                while k < len(extra) and (k + 1) * len(main) <= (i + 1) * len(extra):
                    out.append(extra[k])
                    k += 1
            return out + extra[k:]

        def prep_steps(m):
            out = []
            for d in range(2):
                out += [("low_rank", m, d, 0), ("low_rank", m, d, 1), ("key_square", m, d), ("key_norm", m, d), ("decay", m, d), ("centre", m, d), ("operands", m, d),
                        ("scaled", m, d)]
            if m == 0:
                out = out[:2] + [("ada", LATE_ADA[4])] + out[2:4] + [("ada", n) for n in LATE_ADA[5:]] + out[4:]
            return [("values", m)] + out + [("bonus", m)]

        SCHEDULE = list(prep_steps(0))
        for b in PAIRS[0]:
            SCHEDULE += [("gram", b), ("turn_keys", b)]
        for q, (b0, b1) in enumerate(PAIRS):
            rec = []
            if q:
                for b in PAIRS[q - 1]:
                    rec += [("solve_x", b), ("solve_u", b), ("update", b)]
            nxt = []
            if q + 1 < len(PAIRS):
                for b in PAIRS[q + 1]:
                    nxt += [("gram", b), ("turn_keys", b)]
            main = []
            for l in range(1, 7):
                main += [("w", l, b0), ("w", l, b1), ("ma", l, b0), ("ma", l, b1)]
            early, late = main[:12], main[12:]
            if q == 0:
                early = [("level0_sum", b0), ("level0_sum", b1), ("level0", b0), ("level0", b1)] + early
            ahead = PAIRS[q + 1] if nxt else ()
            last = [late[-4]] + [("level0_sum", b) for b in ahead[:1]] + [late[-3]] + [("level0_sum", b) for b in ahead[1:]] + \
                late[-2:] + [("level0", b) for b in ahead]
            a, z = merge(early, rec), merge(late[:-4], nxt) + last
            for m in range(1, 4):
                first, todo = (5 * m) // 2, prep_steps(m)
                if q == first - 2:
                    if q:
                        z = merge(z, todo[:len(todo) * 3 // 5])
                    else:
                        a, z = merge(a, todo[:len(todo) // 4]), merge(z, todo[len(todo) // 4:len(todo) * 3 // 5])
                if q == first - 1:
                    a = merge(a, todo[len(todo) * 3 // 5:])
            steps = a + z
            SCHEDULE += steps
        for b in PAIRS[-1]:
            SCHEDULE += [("solve_x", b), ("solve_u", b), ("update", b)]
        HEAD_STEPS = ["head_stats", "head_centre", "head_scale", "head_gain", "head_bias", "head_bonus"]
        for m in range(4):
            i = SCHEDULE.index(("update", 5 * m + 4)) + 1
            for k in HEAD_STEPS:
                SCHEDULE.insert(min(i, len(SCHEDULE)), (k, m))
                i += 3 if m < 3 else 1

        TEMPS = []
        for st in SCHEDULE:
            k = st[0]
            if k == "low_rank":
                TEMPS += [("low_rank", st[1], st[2], st[3], part) for part in range(2)]
            elif k == "key_norm":
                TEMPS += [("key_norm", st[1], st[2], part) for part in range(2)]
            elif k == "values":
                TEMPS += [("values", st[1], part) for part in range(2)]
            elif k == "bonus":
                TEMPS += [("state_in", st[1]), ("bonus", st[1])]
            elif k == "gram":
                TEMPS += [("gram", st[1], u) for u in range(4)]
            elif k == "turn_keys":
                TEMPS += [("turn_keys", st[1])]
            elif k == "update" and BATCH[st[1]][1] == 0:
                TEMPS += [("state_out", st[1])]
        TEMP_AT = {k: i for i, k in enumerate(TEMPS)}

        def temp(key):
            return ps[TEMP_AT[key] % 2]

        def temp_free(pe, key):
            i = TEMP_AT[key]
            if i >= 2:
                pe.wait_ge(*at("read_" + TEMPS[i - 2][0], TEMPS[i - 2]))

        PARTS = [(0, P + 1), (P + 1, LAT)]

        def cols_of(part):
            c0, n = PARTS[part]
            return slice(c0, c0 + n)

        def tcols(t):
            return slice(col(t), col(t) + P)

        def lora_ap(w, d, m):
            return lora_w[d * HD:(d + 1) * HD, w, m * P:(m + 1) * P]

        take_rk = region(rkvT[:, 0:2, :, :].rearrange("p a m t -> p (a m t)"))
        bc_lnx = take_rk(2 * DA).rearrange("p (i n) -> p i n", i=2)
        hmv = take_rk(NT * NH * 2).rearrange("p (t h i) -> p t h i", t=NT, h=NH)
        hrstd = take_rk(NT * NH).rearrange("p (t h) -> p t h", t=NT)
        bst2 = take_rk(NT * 2 * 6).rearrange("p (t h i) -> p t h i", t=NT, h=2)
        vbonus = rkvT[:, 1, 0, 0:NT * P]

        def head_dve(dve, k, m):
            v = nc.vector
            y = ytm[:, :, m * P:(m + 1) * P]
            yh = y.rearrange("p t (h c) -> p t h c", h=2)
            hs = slice(2 * m, 2 * m + 2)
            if k == "head_stats":
                dve.wait_ge(*at("y_part", 5 * m + 4))
                if m:
                    dve.wait_ge(*at("dve_did", ("head_stats", m - 1)))
                else:
                    dve.wait_ge(*at("bonus_terms", 1))
                for t in range(NT):
                    for h in range(2):
                        v.bn_stats(bst2[:, t, h, :], yh[:, t, h, :]).then_inc(*up("dve_did", ("head_bn", m)))
                dve.wait_ge(*at("dve_did", ("head_bn", m)))
                for t in range(NT):
                    for h in range(2):
                        v.bn_aggr(hmv[:, t, 2 * m + h, :], bst2[:, t, h, :]).then_inc(*up("dve_did", ("head_stats", m)))
                return
            dve.wait_ge(*at("dve_did", (HEAD_STEPS[HEAD_STEPS.index(k) - 1], m)))
            if k == "head_centre":
                v.tensor_tensor(yh, yh, hmv[:, :, hs, 0].unsqueeze(3).to_broadcast([P, NT, 2, HD]), ALU.subtract) \
                    .then_inc(*up("dve_did", (k, m)))
            elif k == "head_scale":
                dve.wait_ge(*at("act_did", ("head_rstd", m)))
                v.tensor_tensor(yh, yh, hrstd[:, :, hs].unsqueeze(3).to_broadcast([P, NT, 2, HD]), ALU.mult) \
                    .then_inc(*up("dve_did", (k, m)))
            elif k in ("head_gain", "head_bias"):
                dve.wait_ge(*at("lnx_landed"))
                i = int(k == "head_bias")
                v.tensor_tensor(y, y, bc_lnx[:, i, m * P:(m + 1) * P].unsqueeze(1).to_broadcast([P, NT, P]),
                                ALU.add if i else ALU.mult).then_inc(*up("dve_did", (k, m)))
            else:
                dve.wait_ge(*at("pool_did", ("v_bonus", m)))
                v.tensor_tensor(y, y, vbonus.rearrange("p (t c) -> p t c", t=NT), ALU.add).then_inc(*up("dve_did", (k, m)))

        def v_bonus(pool, m):
            pool.wait_ge(*at("read_bonus", ("bonus", m)))
            pool.wait_ge(*at("read_values", ("values", m, 1)))
            pool.wait_ge(*at("bonus_terms", 1))
            pool.wait_ge(*at("key_square", (1, 1)))
            if m:
                pool.wait_ge(*at("dve_did", ("head_bonus", m - 1)))
            nc.gpsimd.tensor_tensor(vbonus.rearrange("p (t h c) -> p t h c", t=NT, h=2),
                                    vtm[:, m % 2, :, :].rearrange("p t (h c) -> p t h c", h=2),
                                    bonus[:, :, 2 * m:2 * m + 2].unsqueeze(3).to_broadcast([P, NT, 2, HD]), ALU.mult) \
                .then_inc(*up("pool_did", ("v_bonus", m)))

        def scan_loads(sp):
            fill_slots(sp)
            for st in SCHEDULE:
                if st[0] == "values":
                    m = st[1]
                    if m:
                        sp.wait_ge(*at("state_in_T", m - 1))
                    else:
                        sp.wait_ge(*at("state_in_zero"))
                    for d in range(2):
                        for h in range(2):
                            sp.dma_start(stin[h * HD:(h + 1) * HD, d, h * HD:(h + 1) * HD],
                                         A["state_rwkv"][0, 0, d, 2 * m + h]).then_inc(*up16("state_in_landed", m))
                if st == ("update", 4):
                    sp.wait_ge(*at("bonus_terms", 1))
                    sp.wait_ge(*at("key_square", (1, 1)))
                    for i, n in enumerate(("lnx_g", "lnx_b")):
                        sp.dma_start(bc_lnx[:, i, :], A[n].to_broadcast([P, DA])).then_inc(*up16("lnx_landed"))
                if st == ("update", 14):
                    sp.wait_ge(*at("y_mm", 14))
                    sp.wait_ge(*at("bonus_terms", 3))
                    for n in ("factor", "key_mix", "kk_iclr", "kt", "centred", "comb", "operands_done", "bonus_mm"):
                        sp.wait_ge(*at(n))
                    early_loads(sp)
                if st[0] == "update" and BATCH[st[1]][1] == 0:
                    m = BATCH[st[1]][0]
                    sp.wait_ge(*at("read_state_out", ("state_out", st[1])))
                    for d in range(2):
                        for h in range(2):
                            sp.dma_start(outs[2][0, 0, d, 2 * m + h], stout[h * HD:(h + 1) * HD, d, h * HD:(h + 1) * HD]) \
                                .then_inc(*up16("state_stored", m))
            post_loads(sp)

        def scan_pool(pool):
            g = nc.gpsimd
            pool.wait_ge(*at("yc_T", NT - 1))
            pool.wait_ge(*at("catBC"))
            g.memset(stin[:, :, :], 0.0).then_inc(*up("state_in_zero"))
            g.memset(state[:, :, :, :], 0.0).then_inc(*up("state_zero"))
            for st in SCHEDULE:
                if st[0] == "head_stats":
                    v_bonus(pool, st[1])
                if st[0] in ("level0_sum", "w"):
                    b = st[-1]
                    l = 0 if st[0] == "level0_sum" else st[1] + 1
                    if l > 6:
                        continue
                    s = b % 2
                    if l == 0:
                        pool.wait_ge(*at("read_gram", ("gram", b, 3)))
                        if b >= 2:
                            pool.wait_ge(*at("w_mm", (6, b - 2)))
                    elif l == 1:
                        pass
                    else:
                        pool.wait_ge(*at("w_mm", (l - 1, b)))
                    g.tensor_tensor(nlev[:, s, :, :], mats[:, b % 4, :, MAT_N, :],
                                    level[:, l:l + 1, :].to_broadcast([P, 4, P]), ALU.mult).then_inc(*up("n_level", (l, b)))
                    if st[0] == "level0_sum":
                        pool.wait_ge(*at("level0_sum", b))
                        g.tensor_tensor(nlev[:, s, :, :], mats[:, b % 4, :, MAT_N, :],
                                        level[:, 1:2, :].to_broadcast([P, 4, P]), ALU.mult).then_inc(*up("n_level", (1, b)))
            post_pool(pool)

        def scan_act(act):
            a = nc.scalar
            for st in SCHEDULE:
                k = st[0]
                if k == "values":
                    m = st[1]
                    r = m % 2
                    act.wait_ge(*at("values_T", (m, 0)))
                    if m >= 2:
                        act.wait_ge(*at("pool_did", ("v_bonus", m - 2)))
                        act.wait_ge(*at("y_mm", 5 * (m - 2) + 4))
                    a.copy(vtm[:, r, 0:4, :].rearrange("p t c -> p (t c)"), temp(("values", m, 0))[:, :]) \
                        .then_inc(*up("read_values", ("values", m, 0)))
                    act.wait_ge(*at("values_T", (m, 1)))
                    a.copy(vtm[:, r, 4, :], temp(("values", m, 1))[:, 0:P]).then_inc(*up("read_values", ("values", m, 1)))
                elif k == "low_rank":
                    _, m, d, w = st
                    if (m, d) == (0, 0):
                        act.wait_ge(*at("lora"))
                    else:
                        act.wait_ge(*at("operands_done", (m, d - 1) if d else (m - 1, 1)))
                    bias = PR["w0" if w == 0 else "a0"][0] + 4 * d + m
                    dst = (lw, iclr)[w]
                    for part in range(2):
                        act.wait_ge(*at("low_rank_mm", (m, d, w, part)))
                        a.activation(dst[:, cols_of(part)], temp(("low_rank", m, d, w, part))[:, 0:PARTS[part][1]],
                                     ACT.Sigmoid, bias=pcol[:, bias:bias + 1]) \
                            .then_inc(*up("read_low_rank", ("low_rank", m, d, w, part)))
                elif k == "key_square":
                    _, m, d = st
                    kc = PR["k_k"][0] + 4 * d + m
                    a.activation(rn, rkvT[:, 1, m, :], ACT.Square, scale=pcol[:, kc:kc + 1]).then_inc(*up("key_square", (m, d)))
                elif k == "centre":
                    _, m, d = st
                    r = m % 2
                    act.wait_ge(*at("read_key_norm", ("key_norm", m, d, 1)))
                    a.activation(rn, rn, ACT.Abs_reciprocal_sqrt).then_inc(*up("key_rnorm", (m, d)))
                    act.wait_ge(*at("centred", (m, d)))
                    if m >= 2:
                        act.wait_ge(*at("y_mm", 5 * (m - 2) + 4))
                    a.activation(eedge[:, r, d, :, :], edge[:, r, d, :, :], ACT.Exp).then_inc(*up("edge_exp", (m, d)))
                    if (m, d) == (0, 0):
                        act.wait_ge(*at("ada_mm", 11))
                    qe, re, ke = ((excl, 1.0), (cum, 1.0), (cum, -1.0)) if d == 0 else ((cum, -1.0), (excl, -1.0), (excl, 1.0))
                    for i, (src, sc) in ((QT, qe), (KT, ke), (RT, re)):
                        a.activation(qrkb[:, r, d, i, :], src, ACT.Exp, scale=sc).then_inc(*up("factor", (m, d, i)))
                elif k == "head_centre":
                    m = st[1]
                    act.wait_ge(*at("dve_did", ("head_stats", m)))
                    hs = slice(2 * m, 2 * m + 2)
                    a.activation(hrstd[:, :, hs], hmv[:, :, hs, 1], ACT.Abs_reciprocal_sqrt, bias=eps[:, 2:3]) \
                        .then_inc(*up("act_did", ("head_rstd", m)))
                elif k == "ada":
                    late_row(act, LATE_ADA.index(st[1]))
                elif k == "bonus":
                    m = st[1]
                    act.wait_ge(*at("bonus_mm", m))
                    a.copy(bonus[:, :, 2 * m:2 * m + 2], temp(("bonus", m))[:, 0:2 * NT].rearrange("p (t h) -> p t h", t=NT)) \
                        .then_inc(*up("read_bonus", ("bonus", m)))
                elif k == "turn_keys":
                    b = st[1]
                    act.wait_ge(*at("keys_T", b))
                    if b >= 4:
                        act.wait_ge(*at("s_mm", b - 4))
                    a.copy(kbtm[:, b % 4, :, :, :].rearrange("p d i c -> p (d i c)"), temp(("turn_keys", b))[:, :]) \
                        .then_inc(*up("read_turn_keys", ("turn_keys", b)))
                elif k == "level0":
                    b = st[1]
                    act.wait_ge(*at("inv_T", b))
                    if b == 0:
                        act.wait_ge(*at("mod_stored", 11))
                    a.copy(inv[:, b % 2, :, :].rearrange("p u q -> p (u q)"), ps[2 + 2 * (b % 2)][:, :]).then_inc(*up("inv", (0, b)))
                elif k == "ma":
                    _, l, b = st
                    if l < 6:
                        act.wait_ge(*at("m_mm", (l, b)))
                        act.wait_ge(*at("a_mm", (l, b)))
                        a.copy(inv[:, b % 2, :, :].rearrange("p u q -> p (u q)"), ps[2 + 2 * (b % 2)][:, :]) \
                            .then_inc(*up("inv", (l, b)))
                    act.wait_ge(*at("a_mm", (l, b)))
                    a.copy(invT[:, b % 4, :, :].rearrange("p u q -> p (u q)"), ps[3 + 2 * (b % 2)][:, :]) \
                        .then_inc(*up("inv_t", (l, b)))
                elif k == "solve_x":
                    b = st[1]
                    act.wait_ge(*at("x_mm", b))
                    a.copy(xsb[:, b % 2, :], ps[6][:, 0:256]).then_inc(*up("x_copy", b))
                elif k == "solve_u":
                    b = st[1]
                    act.wait_ge(*at("u_mm", b))
                    a.copy(usb[:, b % 2, :], ps[7][:, 0:256]).then_inc(*up("u_copy", b))
            post_act(act)

        def scan_dve(dve):
            v = nc.vector
            dve.wait_ge(*at("yc_T", NT - 1))
            dve.wait_ge(*at("catBC"))
            for st in SCHEDULE:
                k = st[0]
                if k in HEAD_STEPS:
                    head_dve(dve, *st)
                if k == "decay":
                    _, m, d = st
                    r = m % 2
                    dve.wait_ge(*at("read_low_rank", ("low_rank", m, d, 0, 1)))
                    if m or d:
                        dve.wait_ge(*at("factor", (m, d - 1, RT) if d else (m - 1, 1, RT)))
                    v.tensor_scalar(lw, lw, -DECAY, None, ALU.mult).then_inc(*up("log_decay", (m, d)))
                    dve.wait_ge(*at("log_decay", (m, d)))
                    dve.wait_ge(*at("const", "all"))
                    v.tensor_tensor_scan(cum, keep[:, :], lw, 0.0, ALU.mult, ALU.add).then_inc(*up("decay_sum", (m, d)))
                    dve.wait_ge(*at("decay_sum", (m, d)))
                    v.tensor_copy(edge[:, r, d, 0, 0:1], cum[:, 63:64]).then_inc(*up("edge", (m, d)))
                    v.tensor_copy(edge[:, r, d, 0, 1:NT], cum[:, P + 1:TW].rearrange("p (t q) -> p t q", q=P)[:, :, 63]) \
                        .then_inc(*up("edge", (m, d)))
                elif k == "key_norm":
                    _, m, d = st
                    for part in range(2):
                        dve.wait_ge(*at("key_norm_mm", (m, d, part)))
                        v.tensor_scalar(rn[:, cols_of(part)], temp(("key_norm", m, d, part))[:, 0:PARTS[part][1]], 1e-24, None,
                                        ALU.max).then_inc(*up("read_key_norm", ("key_norm", m, d, part)))
                elif k == "centre":
                    _, m, d = st
                    r = m % 2
                    dve.wait_ge(*at("edge", (m, d)))
                    v.tensor_scalar(cum[:, 0:P + 1], cum[:, 0:P + 1], edge[:, r, d, 0, 0:1], None, ALU.subtract) \
                        .then_inc(*up("centre", (m, d)))
                    lat = cum[:, P + 1:TW].rearrange("p (t q) -> p t q", q=P)
                    v.tensor_tensor(lat, lat, edge[:, r, d, 0, 1:NT].unsqueeze(2).to_broadcast([P, NT - 1, P]), ALU.subtract) \
                        .then_inc(*up("centre", (m, d)))
                    dve.wait_ge(*at("centre", (m, d)))
                    v.tensor_copy(edge[:, r, d, 1, 0:1], cum[:, P - 1:P]).then_inc(*up("centred"))
                    v.tensor_copy(edge[:, r, d, 1, 1:NT], lat[:, :, P - 1]).then_inc(*up("centred"))
                    v.tensor_tensor(excl, cum, lw, ALU.subtract).then_inc(*up("centred", (m, d)))
                elif k == "operands":
                    _, m, d = st
                    kc, ka = PR["k_k"][0] + 4 * d + m, PR["k_a"][0] + 4 * d + m
                    K = rkvT[:, 1, m, :]
                    dst = ktsum if d == 0 else kt
                    dve.wait_ge(*at("key_rnorm", (m, d)))
                    if m or d:
                        dve.wait_ge(*at("operands_done", (m, d - 1) if d else (m - 1, 1)))
                    if m and d == 0:
                        dve.wait_ge(*at("bonus_terms", m - 1))
                    v.scalar_tensor_tensor(kk, K, pcol[:, kc:kc + 1], rn, ALU.mult, ALU.mult).then_inc(*up("kk", (m, d)))
                    dve.wait_ge(*at("read_low_rank", ("low_rank", m, d, 1, 1)))
                    v.tensor_scalar(dst, iclr, pcol[:, ka:ka + 1], ka_keep[:, 4 * d + m:4 * d + m + 1], ALU.mult, ALU.add) \
                        .then_inc(*up("key_mix", (m, d)))
                    dve.wait_ge(*at("kk", (m, d)))
                    dve.wait_ge(*at("key_mix", (m, d)))
                    v.tensor_tensor(dst, dst, K, ALU.mult).then_inc(*up("kt", (m, d)))
                    v.tensor_tensor(iclr, iclr, kk, ALU.mult).then_inc(*up("kk_iclr", (m, d)))
                elif k == "scaled":
                    _, m, d = st
                    r = m % 2
                    src = ktsum if d == 0 else kt
                    q = qrkb[:, r, d]
                    dve.wait_ge(*at("factor", (m, d, RT)))
                    v.scalar_tensor_tensor(q[:, QT, :], kk, -1.0, q[:, QT, :], ALU.mult, ALU.mult).then_inc(*up("scaled", (m, d)))
                    v.tensor_tensor(q[:, RT, :], rkvT[:, 0, m, :], q[:, RT, :], ALU.mult).then_inc(*up("scaled", (m, d)))
                    dve.wait_ge(*at("kk_iclr", (m, d)))
                    v.tensor_tensor(q[:, BT, :], iclr, q[:, KT, :], ALU.mult).then_inc(*up("scaled_b", (m, d)))
                    dve.wait_ge(*at("scaled_b", (m, d)))
                    v.tensor_tensor(q[:, KT, :], src, q[:, KT, :], ALU.mult).then_inc(*up("operands_done", (m, d)))
                elif k == "bonus":
                    m = st[1]
                    r = m % 2
                    rk = PR["r_k"][0] + m
                    dve.wait_ge(*at("operands_done", (m, 1)))
                    v.tensor_tensor(ktsum, ktsum, kt, ALU.add).then_inc(*up("kt_sum", m))
                    dve.wait_ge(*at("kt_sum", m))
                    v.scalar_tensor_tensor(ktsum, ktsum, pcol[:, rk:rk + 1], rkvT[:, 0, m, :], ALU.mult, ALU.mult) \
                        .then_inc(*up("bonus_terms", m))
                    dve.wait_ge(*at("edge_exp", (m, 1)))
                    for d in range(2):
                        v.tensor_tensor(comb[:, r, d, :], eedge[:, r, d, 1, 1:4], eedge[:, r, d, 0, 2:5], ALU.mult) \
                            .then_inc(*up("comb", m))
                    dve.wait_ge(*at("state_in_T", m))
                    if m >= 2:
                        dve.wait_ge(*at("y_mm", 5 * (m - 2) + 4))
                    dve.wait_ge(*at("state_zero"))
                    for d in range(2):
                        pre = eedge[:, r, 0, 0, 1:2] if d == 0 else eedge[:, r, 1, 1, 4:5]
                        v.tensor_scalar(state[:, r, d, :], temp(("state_in", m))[:, d * P:(d + 1) * P], pre, None, ALU.mult) \
                            .then_inc(*up("read_state_in", ("state_in", m)))
                elif k == "gram":
                    b = st[1]
                    for u in range(4):
                        dve.wait_ge(*at("gram_mm", (b, u)))
                        if b >= 4:
                            dve.wait_ge(*at("y_mm", b - 4))
                        if b == 0 and u == 0:
                            dve.wait_ge(*at("const", "all"))
                        v.tensor_tensor(mats[:, b % 4, u, :, :].rearrange("p (k q) t -> p k q t", k=2),
                                        temp(("gram", b, u))[:, :].rearrange("p (k q t) -> p k q t", k=2, q=2),
                                        gmask[:, u // 2, :, :].unsqueeze(1).to_broadcast([P, 2, 2, P]), ALU.mult) \
                            .then_inc(*up("read_gram", ("gram", b, u)))
                elif k == "level0_sum":
                    b = st[1]
                    dve.wait_ge(*at("n_level", (0, b)))
                    if b >= 4:
                        dve.wait_ge(*at("u_mm", b - 4))
                    v.tensor_tensor(invT[:, b % 4, :, :], nlev[:, b % 2, :, :], ident[:, :].unsqueeze(1).to_broadcast([P, 4, P]),
                                    ALU.add).then_inc(*up("level0_sum", b))
                elif k == "w":
                    _, l, b = st
                    dve.wait_ge(*at("w_mm", (l, b)))
                    if (l, b) == (1, 0):
                        dve.wait_ge(*at("mod_stored", 11))
                    v.tensor_tensor(wmat[:, b % 2, :, :], ps[2 + 2 * (b % 2)][:, :].rearrange("p (u q) -> p u q", u=4),
                                    ident[:, :].unsqueeze(1).to_broadcast([P, 4, P]), ALU.add).then_inc(*up("w_sum", (l, b)))
                elif k == "update":
                    b = st[1]
                    m, s = BATCH[b]
                    r = m % 2
                    dve.wait_ge(*at("s_mm", b))
                    if s == 0:
                        if m:
                            dve.wait_ge(*at("state_stored", m - 1))
                        for d in range(2):
                            post = eedge[:, r, 0, 1, 0:1] if d == 0 else eedge[:, r, 1, 0, 0:1]
                            v.tensor_scalar(stout[:, d, :], ps[6][:, d * P:(d + 1) * P], post, None, ALU.mult) \
                                .then_inc(*up("state_scaled", b))
                        dve.wait_ge(*at("state_out_T", b))
                        v.tensor_copy(stout[:, :, :].rearrange("p d c -> p (d c)"), temp(("state_out", b))[:, 0:256]) \
                            .then_inc(*up("read_state_out", ("state_out", b)))
                    elif s < NT - 1:
                        dve.wait_ge(*at("y_mm", b))
                        for d in range(2):
                            j = s - 1 if d == 0 else NT - 2 - s
                            for h in range(2):
                                hs = slice(h * HD, (h + 1) * HD)
                                v.tensor_scalar(state[hs, r, d, hs], ps[6][hs, d * P + h * HD:d * P + (h + 1) * HD],
                                                comb[hs, r, d, j:j + 1], None, ALU.mult).then_inc(*up("state_next", b))
                    dve.wait_ge(*at("y_mm", b))
                    for d in range(2):
                        dst = ytm[:, tile_of(d, s), m * P:(m + 1) * P]
                        src = ps[7][:, 256 + d * P:256 + (d + 1) * P]
                        if s in (1, 2) or (s == 0 and d == 0):
                            v.tensor_copy(dst, src).then_inc(*up("y_part", b))
                        else:
                            if s:
                                dve.wait_ge(*at("y_part", b - 1 if s == 3 else 5 * m + 1))
                            else:
                                dve.wait_ge(counts.sem("y_part"), counts.total["y_part"])
                            v.tensor_tensor(dst, dst, src, ALU.add).then_inc(*up("y_part", b))
            post_dve(dve)

        def scan_pe(pe):
            T_ = nc.tensor
            for st in SCHEDULE:
                k = st[0]
                if k == "values":
                    m = st[1]
                    if m == 0:
                        pe.wait_ge(*at("mixed"))
                        pe.wait_ge(*at("catBC"))
                    for part in range(2):
                        temp_free(pe, ("values", m, part))
                        for t in (range(4) if part == 0 else [4]):
                            x = T_.transpose(temp(("values", m, part))[:, (t % 4) * P:(t % 4 + 1) * P], rkvT[:, 2, m, tcols(t)],
                                             ident[:, :])
                        x.then_inc(*up("values_T", (m, part)))
                elif k == "low_rank":
                    _, m, d, w = st
                    if (m, d, w) == (0, 0, 0):
                        pe.wait_ge(*at("lora"))
                        pe.wait_ge(*at("lora_w_landed"))
                    for part in range(2):
                        temp_free(pe, ("low_rank", m, d, w, part))
                        T_.matmul(temp(("low_rank", m, d, w, part))[:, 0:PARTS[part][1]], lora_ap(w, d, m),
                                  loraT[d * HD:(d + 1) * HD, w, cols_of(part)], start=True, stop=True) \
                            .then_inc(*up("low_rank_mm", (m, d, w, part)))
                elif k == "ada":
                    ada_mm(pe, st[1])
                elif k == "key_norm":
                    _, m, d = st
                    pe.wait_ge(*at("key_square", (m, d)))
                    for part in range(2):
                        temp_free(pe, ("key_norm", m, d, part))
                        T_.matmul(temp(("key_norm", m, d, part))[:, 0:PARTS[part][1]], halfones[:, :], rn[:, cols_of(part)],
                                  start=True, stop=True).then_inc(*up("key_norm_mm", (m, d, part)))
                elif k == "bonus":
                    m = st[1]
                    temp_free(pe, ("state_in", m))
                    pe.wait_ge(*at("state_in_landed", m))
                    for d in range(2):
                        x = T_.transpose(temp(("state_in", m))[:, d * P:(d + 1) * P], stin[:, d, :], ident[:, :])
                    x.then_inc(*up("state_in_T", m))
                    temp_free(pe, ("bonus", m))
                    pe.wait_ge(*at("bonus_terms", m))
                    for t in range(NT):
                        x = T_.matmul(temp(("bonus", m))[:, 2 * t:2 * t + 2], ktsum[:, tcols(t)], headsel[:, :], start=True, stop=True)
                    x.then_inc(*up("bonus_mm", m))
                elif k == "gram":
                    b = st[1]
                    m, s = BATCH[b]
                    pe.wait_ge(*at("operands_done", (m, 1)))
                    for u in range(4):
                        d, h = u // 2, u % 2
                        hs = slice(h * HD, (h + 1) * HD)
                        tc = tcols(tile_of(d, s))
                        out = temp(("gram", b, u))
                        temp_free(pe, ("gram", b, u))
                        for i, key in enumerate((BT, KT)):
                            x = T_.matmul(out[:, i * 256:(i + 1) * 256], qrkb[hs, m % 2, d, key, tc],
                                          qrkb[hs, m % 2, d, QT:RT + 1, tc], start=True, stop=True)
                        x.then_inc(*up("gram_mm", (b, u)))
                elif k == "turn_keys":
                    b = st[1]
                    m, s = BATCH[b]
                    temp_free(pe, ("turn_keys", b))
                    for d in range(2):
                        for i, key in enumerate((BT, KT)):
                            x = T_.transpose(temp(("turn_keys", b))[:, (2 * d + i) * P:(2 * d + i + 1) * P],
                                             qrkb[:, m % 2, d, key, tcols(tile_of(d, s))], ident[:, :])
                    x.then_inc(*up("keys_T", b))
                elif k == "level0":
                    b = st[1]
                    pe.wait_ge(*at("level0_sum", b))
                    if b >= 2:
                        pe.wait_ge(*at("w_sum", (6, b - 2)))
                    for u in range(4):
                        x = T_.transpose(ps[2 + 2 * (b % 2)][:, u * P:(u + 1) * P], invT[:, b % 4, u, :], ident[:, :])
                    x.then_inc(*up("inv_T", b))
                elif k == "w":
                    _, l, b = st
                    pe.wait_ge(*at("inv", (l - 1, b)))
                    pe.wait_ge(*at("n_level", (l, b)))
                    for u in range(4):
                        x = T_.matmul(ps[2 + 2 * (b % 2)][:, u * P:(u + 1) * P], nlev[:, b % 2, u, :], inv[:, b % 2, u, :],
                                      start=True, stop=True)
                    x.then_inc(*up("w_mm", (l, b)))
                elif k == "ma":
                    _, l, b = st
                    pe.wait_ge(*at("w_sum", (l, b)))
                    if l > 1:
                        pe.wait_ge(*at("inv_t", (l - 1, b)))
                    elif b >= 2:
                        pe.wait_ge(*at("inv_t", (6, b - 2)))
                    if l < 6:
                        for u in range(4):
                            x = T_.matmul(ps[2 + 2 * (b % 2)][:, u * P:(u + 1) * P], invT[:, b % 4, u, :], wmat[:, b % 2, u, :],
                                          start=True, stop=True)
                        x.then_inc(*up("m_mm", (l, b)))
                    for u in range(4):
                        x = T_.matmul(ps[3 + 2 * (b % 2)][:, u * P:(u + 1) * P], wmat[:, b % 2, u, :], invT[:, b % 4, u, :],
                                      start=True, stop=True)
                    x.then_inc(*up("a_mm", (l, b)))
                elif k == "solve_x":
                    b = st[1]
                    m, s = BATCH[b]
                    r = m % 2
                    if b == 0:
                        pe.wait_ge(*row_made(11))
                    else:
                        pe.wait_ge(*(at("state_scaled", b - 1) if BATCH[b - 1][1] == 0 else
                                     at("state_next", b - 1) if BATCH[b - 1][1] < NT - 1 else at("y_part", b - 1)))
                    if s == 1:
                        pe.wait_ge(*at("read_state_in", ("state_in", m)))
                    for d in range(2):
                        if s:
                            T_.matmul(ps[6][:, d * P:(d + 1) * P], qrkb[:, r, d, QT, tcols(tile_of(d, s))], state[:, r, d, :],
                                      start=(d == 0), stop=False, skip_group_check=True)
                        for h in range(2):
                            o = d * P + h * HD
                            x = T_.matmul(ps[6][:, o:o + HD], mats[:, b % 4, 2 * d + h, MAT_L, :],
                                          vtm[:, r, tile_of(d, s), h * HD:(h + 1) * HD], start=(s == 0 and o == 0),
                                          stop=(o == 192),
                                          skip_group_check=True)
                    x.then_inc(*up("x_mm", b))
                elif k == "solve_u":
                    b = st[1]
                    pe.wait_ge(*at("x_copy", b))
                    pe.wait_ge(*at("inv_t", (6, b)))
                    if b:
                        pe.wait_ge(*at("y_part", b - 1))
                    for u in range(4):
                        o = u * HD
                        x = T_.matmul(ps[7][:, o:o + HD], invT[:, b % 4, u, :], xsb[:, b % 2, o:o + HD], start=True, stop=True)
                    x.then_inc(*up("u_mm", b))
                elif k == "update":
                    b = st[1]
                    m, s = BATCH[b]
                    r = m % 2
                    pe.wait_ge(*at("u_copy", b))
                    pe.wait_ge(*at("read_turn_keys", ("turn_keys", b)))
                    for d in range(2):
                        out = ps[6][:, d * P:(d + 1) * P]
                        t = tile_of(d, s)
                        if s:
                            T_.matmul(out, ident[:, :], state[:, r, d, :], start=True, stop=False)
                        T_.matmul(out, kbtm[:, b % 4, d, 1, :], vtm[:, r, t, :], start=(s == 0), stop=False)
                        x = T_.matmul(out, kbtm[:, b % 4, d, 0, :], usb[:, b % 2, d * P:(d + 1) * P], start=False, stop=True)
                    x.then_inc(*up("s_mm", b))
                    for d in range(2):
                        t = tile_of(d, s)
                        if s:
                            T_.matmul(ps[7][:, 256 + d * P:256 + (d + 1) * P], qrkb[:, r, d, RT, tcols(t)], state[:, r, d, :],
                                      start=(d == 0), stop=False, skip_group_check=True)
                        for h in range(2):
                            o = d * P + h * HD
                            T_.matmul(ps[7][:, 256 + o:256 + o + HD], mats[:, b % 4, 2 * d + h, MAT_LR, :],
                                      vtm[:, r, t, h * HD:(h + 1) * HD], start=(s == 0 and o == 0), stop=False,
                                      skip_group_check=True)
                            x = T_.matmul(ps[7][:, 256 + o:256 + o + HD], mats[:, b % 4, 2 * d + h, MAT_NR, :],
                                          usb[:, b % 2, o:o + HD], start=False, stop=(o == 192), skip_group_check=True)
                    x.then_inc(*up("y_mm", b))
                    if s == 0:
                        temp_free(pe, ("state_out", b))
                        pe.wait_ge(*at("state_scaled", b))
                        for d in range(2):
                            x = T_.transpose(temp(("state_out", b))[:, d * P:(d + 1) * P], stout[:, d, :], ident[:, :])
                        x.then_inc(*up("state_out_T", b))
            post_pe(pe)

        FE = 2 * 256
        DE = FE // 2
        ENDLESS = 1e30
        CAP = (2 * T - NEXP) // P + NEXP
        GATE1, SHIFT2, SCALE2, GATE2 = range(4)
        WROWS = [4, 5, 6, 7, 0, 1, 2, 3]
        wout = carve(KD * D, at_=0).rearrange("p (k n) -> p k n", k=KD)
        bc_row = carve(D)
        x1 = carve(NT * D, at_=SCRATCH0).rearrange("p (t n) -> p t n", t=NT)
        mods = carve(4 * 2 * D).rearrange("p (i g n) -> p i g n", i=4, g=2)
        h2 = carve(2 * D).rearrange("p (s n) -> p s n", s=2)
        wdn = carve(2 * 2 * D).rearrange("p (s k n) -> p s k n", s=2, k=2)
        hT = carve(2 * D).rearrange("p (s k q) -> p s k q", s=2, k=KD)
        act_in = carve(DE)
        actg = carve(2 * DE).rearrange("p (s n) -> p s n", s=2)
        actT = carve(2 * DE).rearrange("p (s n) -> p s n", s=2)
        assert pos[0] <= YTM0, pos[0]
        wgu = carve(2 * KD * FE, at_=0).rearrange("p (s k n) -> p s k n", s=2, k=KD)
        hrow = h2
        yrow = carve(2 * D, at_=YTM0).rearrange("p (s n) -> p s n", s=2)
        pos[0] = YTM0 + NT * DA

        take = take_rk
        catA = take(2 * 4 * P).rearrange("p (s k q) -> p s k q", s=2, k=4)
        h2T = take(D).rearrange("p (k q) -> p k q", k=KD)
        mixed = take(D)
        take = region(loraT[:, 0:2, :].rearrange("p a t -> p (a t)"))
        ones = take(P)
        w1, w2_ = [take(NT) for _ in range(2)]
        pick_gate = [w1, w2_]
        tokid = take(NT)
        first_slot = take(CAP)
        prio16, prio4, step128, tile_no, part_no = take(NEXP), take(4), take(NT), take(CAP), take(1)
        b_router_bc = take(NEXP)
        wr_sb = take(KD * NEXP).rearrange("p (k e) -> p k e", k=KD)
        slot_no = take(P)
        slot_u = take(2 * NT).bitcast(U32).rearrange("p (k t) -> p k t", k=2)
        used_i = take(1).bitcast(I32)
        weight_u, token_u = [take(CAP).bitcast(U32) for _ in range(2)]
        take = region(arena[:, YTM0:YTM0 + NT * DA])
        logit, sel, masked, pick1, pick2, prod, prefix, tot = [take(NT * NEXP) for _ in range(8)]
        pairs = take(NT * 4 * 6).rearrange("p (t g i) -> p t g i", t=NT, g=4)
        gsc, gpr = take(NT * 4), take(NT * 4)
        rmax, rsum, p1, p2 = [take(NT) for _ in range(4)]
        nexp, ctile, cend, base = [take(NEXP) for _ in range(4)]
        steps5 = take(NEXP * NT)
        tcmp = take(CAP * NEXP)
        texp = take(CAP)
        slots = take(2 * NT)
        tile_end = take(2 * NT)
        in_tile = take(2 * NT * CAP)
        in_row = mods[:, GATE1, :, :].rearrange("p g n -> p (g n)")[:, 0:2 * NT * P]

        h_dram = nc.dram_tensor("h2_rows", (T, D), F32).ap()
        y_dram = nc.dram_tensor("slot_rows", (CAP * P, D), F32).ap()
        wgu_rows = A["moe_w_gu"].rearrange("l e (p k) n -> (l e p) (k n)", k=KD)
        wdn_rows = A["moe_w_down"].rearrange("l e (p k) n -> (l e p) (k n)", k=2)

        ORDER = [("head", 0), ("mix_bc", 0), ("turn_a", 0), ("head", 1), ("mix", 0), ("turn_a", 1), ("head", 2), ("h2", 0),
                 ("mix", 1), ("turn_a", 2), ("head", 3), ("turn_h2", 0), ("h2", 1), ("mix", 2), ("router", 0), ("turn_a", 3),
                 ("head", 4), ("turn_h2", 1), ("h2", 2), ("mix", 3), ("router", 1), ("turn_a", 4), ("turn_h2", 2), ("h2", 3),
                 ("mix", 4), ("router", 2), ("turn_h2", 3), ("h2", 4), ("router", 3), ("turn_h2", 4), ("router", 4)]

        def fill_slots(sp):
            for i in range(ALWAYS, CAP, 4):
                n = min(4, CAP - i) * P
                sp.dma_start(y_dram[i * P:i * P + n, :], A["x_sample"][0, 0:n, :]).then_inc(*up16("slots_cleared"))

        def early_loads(sp):
            w = A["w_out"][0].rearrange("(k p) n -> p k n", p=P)
            sp.dma_start(wout[:, 0:4, :], w[:, 4:8, :]).then_inc(*up16("w_out_landed"))
            sp.dma_start(wout[:, 4, :], w[:, 0, :]).then_inc(*up16("w_out_landed"))
            sp.dma_start(x1[:, 0, :], A["x_prompt"][0]).then_inc(*up16("w_out_landed"))
            sp.dma_start(x1[:, 1:NT, :], A["x_sample"][0].rearrange("(t p) n -> p t n", p=P)) \
                .then_inc(*up16("w_out_landed", "early"))

        GATHERS = [f"{n}_landed{s}" for n in ("gu", "down", "rows") for s in range(2)]
        ALWAYS, SINGLES = 14, 19

        def if_used(eng, used, i, run):
            before = dict(counts.total)
            with eng.If(used > i):
                run()
            made = {n: v - before[n] for n, v in counts.total.items() if v != before.get(n, 0)}
            made = {n: by for n, by in made.items() if n not in GATHERS}
            if made:
                with eng.Else():
                    for n in made:
                        eng.wait_ge(counts.sem(n), before[n])
                    for n, by in made.items():
                        eng.sem_inc(counts.sem(n), by)

        def each_tile(eng, used, i, step):
            if ALWAYS <= i < SINGLES:
                if_used(eng, used, i, lambda: step(i))
            else:
                step(i)

        def tiles_used(eng):
            eng.wait_ge(*at("dve_did", "used"))
            return eng.value_load(used_i[0:1, :], min_val=0, max_val=CAP)

        def all_tiles(eng, run):
            used = tiles_used(eng)
            run(0, SINGLES, lambda i, step: each_tile(eng, used, i, step))
            if_used(eng, used, SINGLES, lambda: run(SINGLES, CAP, lambda i, step: step(i)))

        def scan_done(eng):
            for n in ("y_part", "u_copy", "y_mm", "n_level", "read_turn_keys", "read_gram", "state_stored", "read_bonus",
                      "bonus_terms", "factor", "read_values", "inv_t", "comb", "read_state_in", "read_state_out",
                      "state_next", "key_mix", "read_low_rank"):
                eng.wait_ge(*at(n))

        def post_loads(sp):
            scan_done(sp)

            sp.wait_ge(*at("w_out_landed", "early"))
            sp.dma_start(wout[:, 5:8, :], A["w_out"][0].rearrange("(k p) n -> p k n", p=P)[:, 1:4, :]) \
                .then_inc(*up16("w_out_landed"))

            def spread(i):
                for gi in range(2):
                    sp.dma_start(mods[:, i, gi, :], mod_dram[gi:gi + 1, i * D:(i + 1) * D].to_broadcast([P, D])) \
                        .then_inc(*up16("gate1_landed" if i == GATE1 else "mods_landed"))
            spread(GATE1)
            sp.dma_start(bc_row, A["norm2_g"].to_broadcast([P, D])).then_inc(*up16("vectors_landed"))
            sp.dma_start(wr_sb, A["w_router"].rearrange("(k p) e -> p k e", p=P)).then_inc(*up16("vectors_landed"))
            sp.dma_start(b_router_bc, A["b_router"].rearrange("(o e) -> o e", o=1).to_broadcast([P, NEXP])) \
                .then_inc(*up16("vectors_landed", "second norm"))
            for i in (SCALE2, SHIFT2, GATE2):
                spread(i)
            for t in range(NT):
                sp.wait_ge(*at("dve_did", ("h2", t)))
                if t:
                    sp.wait_ge(*at("h2_stored", t - 1))
                sp.dma_start(h_dram[t * P:(t + 1) * P, :], h2[:, t % 2, :]).then_inc(*up16("h2_stored", t))
            sp.wait_ge(*at("dve_did", "scale2"))
            sp.dma_start(bc_row, A["final_g"].rearrange("(o e) -> o e", o=1).to_broadcast([P, D])).then_inc(*up16("vectors_landed"))
            def store_rows(i):
                sp.wait_ge(*at("act_did", ("down", i)))
                sp.wait_ge(*at("dve_did", ("down", i)))
                sp.dma_start(y_dram[i * P:(i + 1) * P, :], yrow[:, i % 2, :]).then_inc(*up16(f"y_stored{i % 2}", i))

            def stores(first, end, call):
                if first == 0:
                    sp.wait_ge(*at("slots_cleared"))
                for i in range(first, end):
                    call(i, store_rows)
            all_tiles(sp, stores)
            for t in range(NT):
                sp.wait_ge(*at("pool_did" if t % 2 else "dve_did", ("out", t)))
                dst = outs[0][0] if t == 0 else outs[1][0, (t - 1) * P:t * P, :]
                sp.dma_start(dst, comb_rows[t][0]).then_inc(*up16("stored"))

        rows12 = [wgu[:, s, 2 * i:2 * i + 2, :].rearrange("p k n -> p (k n)") for s in range(2) for i in range(4)] + \
            [wdn[:, s, i, :] for s in range(2) for i in range(2)]
        comb_rows = [(rows12[2 * t], rows12[2 * t + 1]) for t in range(NT)]
        PICKS = [f"picks_landed{(t + 1) // 2}" for t in range(NT)]

        def post_pool(pool):
            g = nc.gpsimd
            scan_done(pool)
            g.memset(ones, 1.0).then_inc(*up("pool_did", "ones"))
            g.iota(slot_no, pattern=[[1, P]], base=0, channel_multiplier=0, allow_small_or_imprecise_dtypes=True) \
                .then_inc(*up("pool_did"))
            g.iota(tokid, pattern=[[P, NT]], base=0, channel_multiplier=1, allow_small_or_imprecise_dtypes=True) \
                .then_inc(*up("pool_did"))
            g.iota(prio16, pattern=[[-1, NEXP]], base=NEXP, channel_multiplier=0, allow_small_or_imprecise_dtypes=True) \
                .then_inc(*up("pool_did"))
            g.iota(prio4, pattern=[[-1, 4]], base=4, channel_multiplier=0, allow_small_or_imprecise_dtypes=True) \
                .then_inc(*up("pool_did"))
            g.iota(step128, pattern=[[P, NT]], base=0, channel_multiplier=0, allow_small_or_imprecise_dtypes=True) \
                .then_inc(*up("pool_did"))
            g.iota(tile_no, pattern=[[1, CAP]], base=0, channel_multiplier=0, allow_small_or_imprecise_dtypes=True) \
                .then_inc(*up("pool_did"))
            g.iota(first_slot, pattern=[[P, CAP]], base=0, channel_multiplier=0, allow_small_or_imprecise_dtypes=True) \
                .then_inc(*up("pool_did"))
            g.iota(part_no, pattern=[[0, 1]], base=0, channel_multiplier=1, allow_small_or_imprecise_dtypes=True) \
                .then_inc(*up("pool_did", "consts"))
            def fetch_weights(i):
                s = i % 2
                if i >= 2:
                    pool.wait_ge(*at("pe_did", ("gu", i - 2)))
                g.indirect_dma_start(wgu[:, s, :, :].rearrange("p k n -> p (k n)"), None, wgu_rows,
                                     bass.IndirectOffsetOnAxis(ap=weight_u[:, i:i + 1], axis=0)).then_inc(*up16(f"gu_landed{s}", i))

            def fetch_down(i):
                s = i % 2
                if i >= 2:
                    pool.wait_ge(*at("pe_did", ("down", i - 2)))
                g.indirect_dma_start(wdn[:, s, :, :].rearrange("p k n -> p (k n)"), None, wdn_rows,
                                     bass.IndirectOffsetOnAxis(ap=weight_u[:, i:i + 1], axis=0)).then_inc(*up16(f"down_landed{s}", i))

            def fetch_rows(i):
                s = i % 2
                if i >= 2:
                    pool.wait_ge(*at("pe_did", ("turn_h", i - 2)))
                g.indirect_dma_start(hrow[:, s, :], None, h_dram,
                                     bass.IndirectOffsetOnAxis(ap=token_u[:, i:i + 1], axis=0)).then_inc(*up16(f"rows_landed{s}", i))
            pool.wait_ge(*at("dve_did", "experts"))
            for n in (("pe_did", ("mix", NT - 1)), ("pe_did", ("turn_h2", NT - 1)), ("h2_stored", NT - 1)):
                pool.wait_ge(*at(*n))

            def fetches(first, end, call):
                if first == 0:
                    fetch_weights(0)
                    pool.wait_ge(*at("dve_did", "tokens"))
                    fetch_rows(0)
                    fetch_rows(1)
                    fetch_weights(1)
                else:
                    for i in (first, first + 1):
                        call(i, fetch_rows)
                        call(i, fetch_weights)
                call(first, fetch_down)
                for i in range(first, end):
                    if i + 2 < end:
                        call(i + 2, fetch_rows)
                        call(i + 2, fetch_weights)
                    if i + 1 < end:
                        call(i + 1, fetch_down)
            all_tiles(pool, fetches)
            for s in range(2):
                pool.wait_ge(*at(f"y_stored{s}"))
            pool.wait_ge(*at("pe_did", ("gu", CAP - 1)))
            pool.wait_ge(*at("pe_did", ("down", CAP - 1)))
            for t in range(NT):
                for k in range(2):
                    g.indirect_dma_start(comb_rows[t][k], None, y_dram,
                                         bass.IndirectOffsetOnAxis(ap=slot_u[:, k, t:t + 1], axis=0)) \
                        .then_inc(*up16(PICKS[t]))
            pool.wait_ge(*at("vectors_landed"))
            for t in range(1, NT, 2):
                pool.wait_ge(*at("act_did", ("out", t)))
                g.tensor_tensor(comb_rows[t][0], comb_rows[t][0], bc_row, ALU.mult).then_inc(*up("pool_did", ("out", t)))
            pool.wait_ge(*at("stored"))

        def post_act(act):
            a = nc.scalar
            scan_done(act)
            for k, t in ORDER:
                if k == "turn_a":
                    act.wait_ge(*at("pe_did", ("turn_a", t)))
                    if t >= 2:
                        act.wait_ge(*at("pe_did", ("mix", t - 2)))
                    a.copy(catA[:, t % 2, :, :].rearrange("p k q -> p (k q)"), ps[5][:, :]).then_inc(*up("act_did", ("turn_a", t)))
                elif k == "mix":
                    act.wait_ge(*at("dve_did", ("mix", t)))
                    if t >= 2:
                        act.wait_ge(*at("pe_did", ("turn_h2", t - 2)))
                        act.wait_ge(*at("h2_stored", t - 2))
                    a.activation(h2[:, t % 2, :], x1[:, t, :], ACT.Square, accum_out=sumsq[:, 0, t:t + 1]).then_inc(*up("act_did", ("square", t)))
                    act.wait_ge(*at("act_did", ("square", t)))
                    a.activation(rstd[:, 0, t:t + 1], sumsq[:, 0, t:t + 1], ACT.Abs_reciprocal_sqrt, bias=eps[:, 0:1],
                                 scale=1.0 / D).then_inc(*up("act_did", ("mix", t)))
                elif k == "turn_h2":
                    act.wait_ge(*at("pe_did", ("turn_h2", t)))
                    if t:
                        act.wait_ge(*at("pe_did", ("router", t - 1)))
                    a.copy(h2T[:, 0:4, :].rearrange("p k q -> p (k q)"), ps[1][:, :]).then_inc(*up("act_did", ("h2", t)))
            act.wait_ge(*at("dve_did", "shifted"))
            a.activation(logit, logit, ACT.Exp).then_inc(*up("act_did", "exp"))
            def rows_half(i):
                act.wait_ge(*at("pe_did", ("turn_h", i)))
                if i >= 2:
                    act.wait_ge(*at("pe_did", ("gu", i - 2)))
                a.copy(hT[:, i % 2, 0:4, :].rearrange("p k q -> p (k q)"), ps[0][:, :]).then_inc(*up("act_did", ("turn_h", i)))

            def silu(i):
                act.wait_ge(*at("pe_did", ("gu", i)))
                if i:
                    act.wait_ge(*at("dve_did", ("gu", i - 1)))
                a.activation(act_in, ps[2 + i % 2][:, 0:DE], ACT.Silu).then_inc(*up("act_did", ("gu", i)))

            def down_half(i):
                act.wait_ge(*at("pe_did", ("down", i)))
                if i >= 2:
                    act.wait_ge(*at(f"y_stored{i % 2}", i - 2))
                a.copy(yrow[:, i % 2, 0:512], ps[5][:, :]).then_inc(*up("act_did", ("down", i)))

            def act_tiles(first, end, call):
                call(first, rows_half)
                call(first, silu)
                call(first + 1, rows_half)
                for i in range(first, end):
                    if i + 1 < end:
                        call(i + 1, silu)
                    if i + 2 < end:
                        call(i + 2, rows_half)
                    call(i, down_half)
            all_tiles(act, act_tiles)
            for t in range(NT + 1):
                if t < NT:
                    ra = comb_rows[t][0]
                    act.wait_ge(*at(PICKS[t]))
                    a.activation(ra, ra, ACT.Copy, scale=w1[:, t:t + 1]).then_inc(*up("act_did", ("gate_a", t)))
                if t:
                    t -= 1
                    act.wait_ge(*at("dve_did", ("x2", t)))
                    if t:
                        act.wait_ge(*at("act_did", ("out_square", t - 1)))
                    a.activation(mixed, x1[:, t, :], ACT.Square, accum_out=sumsq[:, 1, t:t + 1]) \
                        .then_inc(*up("act_did", ("out_square", t)))
                    act.wait_ge(*at("act_did", ("out_square", t)))
                    a.activation(rstd[:, 1, t:t + 1], sumsq[:, 1, t:t + 1], ACT.Abs_reciprocal_sqrt, bias=eps[:, 0:1],
                                 scale=1.0 / D).then_inc(*up("act_did", ("out_rms", t)))
                    act.wait_ge(*at("act_did", ("out_rms", t)))
                    a.activation(comb_rows[t][0], x1[:, t, :], ACT.Copy, scale=rstd[:, 1, t:t + 1]) \
                        .then_inc(*up("act_did", ("out", t)))

        def post_dve(dve):
            v = nc.vector
            scan_done(dve)

            def did(key):
                return up("dve_did", key)

            def after(key):
                dve.wait_ge(*at("dve_did", key))

            def bc(ap, n):
                return ap.unsqueeze(2).to_broadcast(list(ap.shape) + [n])

            for k, t in ORDER:
                if k == "head":
                    after(("head_bonus", 3))
                    dve.wait_ge(*at("pe_did", ("head", t)))
                    v.tensor_tensor(ytm[:, t, :], ytm[:, t, :], ps[2 + t % 2][:, :], ALU.mult).then_inc(*did(("head", t)))
                elif k == "mix":
                    gi = min(t, 1)
                    dve.wait_ge(*at("w_out_landed"))
                    dve.wait_ge(*at("gate1_landed"))
                    for hf in range(2):
                        dve.wait_ge(*at("pe_did", ("mix", t)))
                        cs = slice(hf * 512, hf * 512 + 512)
                        if t:
                            after(("mix", t - 1))
                        v.tensor_tensor(mixed[:, cs], ps[6 + hf][:, :], mods[:, GATE1, gi, cs], ALU.mult).then_inc(*did(("mixed", t)))
                    after(("mixed", t))
                    v.tensor_tensor(x1[:, t, :], x1[:, t, :], mixed, ALU.add).then_inc(*did(("mix", t)))
                elif k == "h2":
                    gi = min(t, 1)
                    dve.wait_ge(*at("act_did", ("mix", t)))
                    if t >= 2:
                        dve.wait_ge(*at("h2_stored", t - 2))
                        dve.wait_ge(*at("pe_did", ("turn_h2", t - 2)))
                    if t == 0:
                        dve.wait_ge(*at("vectors_landed", "second norm"))
                        dve.wait_ge(*at("mods_landed"))
                        for both in range(2):
                            v.scalar_tensor_tensor(mods[:, SCALE2, both, :], mods[:, SCALE2, both, :], 1.0, bc_row, ALU.add, ALU.mult) \
                                .then_inc(*did("scale2"))
                        after("scale2")
                    v.scalar_tensor_tensor(h2[:, t % 2, :], x1[:, t, :], rstd[:, 0, t:t + 1], mods[:, SCALE2, gi, :],
                                           ALU.mult, ALU.mult).then_inc(*did(("h2_scaled", t)))
                    after(("h2_scaled", t))
                    v.tensor_tensor(h2[:, t % 2, :], h2[:, t % 2, :], mods[:, SHIFT2, gi, :], ALU.add).then_inc(*did(("h2", t)))
                elif k == "turn_h2":
                    dve.wait_ge(*at("pe_did", ("turn_h2", t)))
                    if t:
                        dve.wait_ge(*at("pe_did", ("router", t - 1)))
                    v.tensor_copy(h2T[:, 4:8, :].rearrange("p k q -> p (k q)"), ps[4][:, :]).then_inc(*did(("h2_T", t)))
            dve.wait_ge(*at("pool_did", "consts"))
            dve.wait_ge(*at("pe_did", ("router", NT - 1)))
            after(("h2_T", NT - 1))

            def by(ap, n=NEXP):
                return ap.rearrange("p (t e) -> p t e", t=NT)

            lg = ps[0][:, 0:NT * NEXP]
            v.tensor_reduce(rmax, by(lg), AX.X, ALU.max).then_inc(*did("row_max"))
            after("row_max")
            v.tensor_tensor(by(logit), by(lg), bc(rmax, NEXP), ALU.subtract).then_inc(*did("shifted"))
            dve.wait_ge(*at("act_did", "exp"))
            v.tensor_reduce(rsum, by(logit), AX.X, ALU.add).then_inc(*did("exp_sum"))
            after("exp_sum")
            v.reciprocal(rsum, rsum).then_inc(*did("exp_rsum"))
            after("exp_rsum")
            v.tensor_tensor(by(logit), by(logit), bc(rsum, NEXP), ALU.mult).then_inc(*did("probs"))
            after("probs")
            v.tensor_tensor(by(sel), by(logit), b_router_bc.unsqueeze(1).to_broadcast([P, NT, NEXP]), ALU.add).then_inc(*did("sel"))
            after("sel")
            sg = sel.rearrange("p (t g i) -> p t g i", t=NT, g=4)
            for o, n, lag in ((0, 3, 1), (3, 2, 2), (5, 1, 3)):
                v.tensor_tensor(pairs[:, :, :, o:o + n], sg[:, :, :, 0:n], sg[:, :, :, lag:lag + n], ALU.add).then_inc(*did("pairs"))
            after("pairs")
            gs = gsc.rearrange("p (t g) -> p t g", t=NT)
            gp = gpr.rearrange("p (t g) -> p t g", t=NT)
            v.tensor_reduce(gs, pairs, AX.X, ALU.max).then_inc(*did("group_score"))
            after("group_score")

            def first_max(x, w, prio, pick, key):
                v.tensor_reduce(rmax, x, AX.X, ALU.max).then_inc(*did(key + "_max"))
                after(key + "_max")
                v.tensor_tensor(pick, x, bc(rmax, w), ALU.is_equal).then_inc(*did(key + "_ties"))
                after(key + "_ties")
                v.tensor_tensor(pick, pick, prio.unsqueeze(1).to_broadcast([P, NT, w]), ALU.mult).then_inc(*did(key + "_prio"))
                after(key + "_prio")
                v.tensor_reduce(rmax, pick, AX.X, ALU.max).then_inc(*did(key + "_best"))
                after(key + "_best")
                v.tensor_tensor(pick, pick, bc(rmax, w), ALU.is_equal).then_inc(*did(key))
                after(key)

            first_max(gs, 4, prio4, gp, "group")
            v.tensor_scalar(gpr, gpr, 1.0, ENDLESS, ALU.subtract, ALU.mult).then_inc(*did("outside"))
            after("outside")
            v.tensor_tensor(masked.rearrange("p (t g i) -> p t g i", t=NT, g=4), sg, gp.unsqueeze(3).to_broadcast([P, NT, 4, 4]),
                            ALU.add).then_inc(*did("masked"))
            after("masked")
            first_max(by(masked), NEXP, prio16, by(pick1), "pick1")
            v.scalar_tensor_tensor(masked, pick1, -3 * ENDLESS, masked, ALU.mult, ALU.add).then_inc(*did("masked2"))
            after("masked2")
            first_max(by(masked), NEXP, prio16, by(pick2), "pick2")
            for k, (pk, p) in enumerate(((pick1, p1), (pick2, p2))):
                v.tensor_tensor(prod, pk, logit, ALU.mult).then_inc(*did(("prod", k)))
                after(("prod", k))
                v.tensor_reduce(p, by(prod), AX.X, ALU.add).then_inc(*did(("pick_prob", k)))
                after(("pick_prob", k))
            v.tensor_tensor(rsum, p1, p2, ALU.add).then_inc(*did("pick_sum"))
            v.tensor_tensor(prod, pick1, pick2, ALU.add).then_inc(*did("picks"))
            after("pick_sum")
            v.reciprocal(rsum, rsum).then_inc(*did("pick_rsum"))
            after("pick_rsum")
            for w, p in ((w1, p1), (w2_, p2)):
                v.tensor_tensor(w, p, rsum, ALU.mult).then_inc(*did("gates"))
            dve.wait_ge(*at("pe_did", "counts"))
            cn = ps[3][:, 0:NT * NEXP]
            v.tensor_copy(tot, ps[3][:, NT * NEXP:2 * NT * NEXP]).then_inc(*did("tile_counts"))
            v.tensor_copy(prefix[:, 0:NEXP], cn[:, 0:NEXP]).then_inc(*did("prefix0"))
            after("tile_counts")
            v.tensor_copy(nexp, tot[:, 0:NEXP]).then_inc(*did(("prefix", 0)))
            for t in range(1, NT):
                after(("prefix", t - 1))
                es = slice(t * NEXP, (t + 1) * NEXP)
                v.tensor_tensor(prefix[:, es], cn[:, es], nexp, ALU.add).then_inc(*did(("before", t)))
                after(("before", t))
                v.tensor_tensor(nexp, nexp, tot[:, es], ALU.add).then_inc(*did(("prefix", t)))
            after(("prefix", NT - 1))
            s5 = steps5.rearrange("p (e j) -> p e j", e=NEXP)
            v.tensor_tensor(s5, bc(nexp, NT), step128.unsqueeze(1).to_broadcast([P, NEXP, NT]), ALU.is_gt).then_inc(*did("steps"))
            after("steps")
            v.tensor_reduce(ctile, s5, AX.X, ALU.add).then_inc(*did("expert_tiles"))
            after("expert_tiles")
            v.tensor_tensor_scan(cend, ones[:, 0:NEXP], ctile, 0.0, ALU.mult, ALU.add).then_inc(*did("expert_end"))
            after("expert_end")
            v.tensor_tensor(base, cend, ctile, ALU.subtract).then_inc(*did("expert_start"))
            after("expert_start")
            v.tensor_scalar(base, base, float(P), None, ALU.mult).then_inc(*did("expert_base"))
            after("expert_base")
            v.tensor_tensor(by(prefix), by(prefix), base.unsqueeze(1).to_broadcast([P, NT, NEXP]), ALU.add).then_inc(*did("slot_all"))
            after("slot_all")
            for k, (pk, sl) in enumerate(((pick1, slots[:, 0:NT]), (pick2, slots[:, NT:2 * NT]))):
                after("picks")
                if k:
                    after(("slot", 0))
                else:
                    dve.wait_ge(*at("pe_did", "counts"))
                v.tensor_tensor(prod, pk, prefix, ALU.mult).then_inc(*did(("slot_prod", k)))
                after(("slot_prod", k))
                v.tensor_reduce(sl, by(prod), AX.X, ALU.add).then_inc(*did(("slot", k)))
                after(("slot", k))
                v.tensor_copy(slot_u[:, k, :], sl).then_inc(*did("slots"))
            tc = tcmp.rearrange("p (i e) -> p i e", i=CAP)
            v.tensor_tensor(tc, bc(tile_no, NEXP), cend.unsqueeze(1).to_broadcast([P, CAP, NEXP]), ALU.is_ge).then_inc(*did("ended"))
            after("ended")
            v.tensor_reduce(texp, tc, AX.X, ALU.add).then_inc(*did("tile_expert"))
            after("tile_expert")
            v.tensor_scalar(texp, texp, float(NEXP - 1), float(P), ALU.min, ALU.mult).then_inc(*did("expert_row"))
            after("expert_row")
            v.tensor_scalar(texp, texp, part_no, None, ALU.add).then_inc(*did("expert_rows"))
            after("expert_rows")
            v.tensor_copy(weight_u, texp).then_inc(*did("experts"))
            v.tensor_copy(used_i, cend[:, NEXP - 1:NEXP]).then_inc(*did("used"))
            after("slots")
            s2 = in_tile.rearrange("p (s i) -> p s i", i=CAP)
            v.tensor_tensor(s2, bc(slots, CAP), first_slot.unsqueeze(1).to_broadcast([P, 2 * NT, CAP]), ALU.is_ge) \
                .then_inc(*did("reached"))
            after("reached")
            v.tensor_reduce(tile_end, s2, AX.X, ALU.add).then_inc(*did("tile_end"))
            after("tile_end")
            v.tensor_scalar(tile_end, tile_end, 1.0, None, ALU.subtract).then_inc(*did("tile_of_slot"))
            after("tile_of_slot")
            v.scalar_tensor_tensor(slots, tile_end, -float(P), slots, ALU.mult, ALU.add).then_inc(*did("place"))
            v.tensor_tensor(s2, tile_no.unsqueeze(1).to_broadcast([P, 2 * NT, CAP]), bc(tile_end, CAP), ALU.is_equal) \
                .then_inc(*did("in_tile"))
            after("in_tile")
            v.tensor_tensor(in_tile.rearrange("p (k t i) -> p k t i", k=2, t=NT), in_tile.rearrange("p (k t i) -> p k t i", k=2, t=NT),
                            tokid.unsqueeze(1).unsqueeze(3).to_broadcast([P, 2, NT, CAP]), ALU.mult).then_inc(*did("token_in_tile"))
            v.tensor_tensor(in_row.rearrange("p (s q) -> p s q", q=P), slot_no.unsqueeze(1).to_broadcast([P, 2 * NT, P]),
                            bc(slots, P), ALU.is_equal).then_inc(*did("in_row"))
            dve.wait_ge(*at("pe_did", "slot_tokens"))
            v.tensor_copy(token_u, ps[5][:, 0:CAP]).then_inc(*did("tokens"))
            def rows_half(i):
                dve.wait_ge(*at("pe_did", ("turn_h", i)))
                if i >= 2:
                    dve.wait_ge(*at("pe_did", ("gu", i - 2)))
                v.tensor_copy(hT[:, i % 2, 4:8, :].rearrange("p k q -> p (k q)"), ps[1][:, :]).then_inc(*did(("turn_h", i)))

            def product(i):
                dve.wait_ge(*at("act_did", ("gu", i)))
                if i >= 2:
                    dve.wait_ge(*at("pe_did", ("turn_act", i - 2)))
                v.tensor_tensor(actg[:, i % 2, :], act_in, ps[2 + i % 2][:, DE:FE], ALU.mult).then_inc(*did(("gu", i)))

            def act_copy(i):
                dve.wait_ge(*at("pe_did", ("turn_act", i)))
                if i >= 2:
                    dve.wait_ge(*at("pe_did", ("down", i - 2)))
                v.tensor_copy(actT[:, i % 2, :], ps[4][:, 0:DE]).then_inc(*did(("turn_act", i)))

            def down_half(i):
                dve.wait_ge(*at("pe_did", ("down", i)))
                if i >= 2:
                    dve.wait_ge(*at(f"y_stored{i % 2}", i - 2))
                v.tensor_copy(yrow[:, i % 2, 512:1024], ps[6][:, :]).then_inc(*did(("down", i)))

            def dve_tiles(first, end, call):
                call(first, rows_half)
                call(first, product)
                call(first + 1, rows_half)
                call(first, act_copy)
                for i in range(first, end):
                    if i + 1 < end:
                        call(i + 1, product)
                    if i + 2 < end:
                        call(i + 2, rows_half)
                    if i + 1 < end:
                        call(i + 1, act_copy)
                    call(i, down_half)
            all_tiles(dve, dve_tiles)
            for t in range(NT + 1):
                if t < NT:
                    ra, rb = comb_rows[t]
                    gi = min(t, 1)
                    dve.wait_ge(*at(PICKS[t]))
                    dve.wait_ge(*at("act_did", ("gate_a", t)))
                    v.scalar_tensor_tensor(ra, rb, w2_[:, t:t + 1], ra, ALU.mult, ALU.add).then_inc(*did(("gate_b", t)))
                    after(("gate_b", t))
                    v.tensor_tensor(ra, ra, mods[:, GATE2, gi, :], ALU.mult).then_inc(*did(("moe", t)))
                    after(("moe", t))
                    v.tensor_tensor(x1[:, t, :], x1[:, t, :], ra, ALU.add).then_inc(*did(("x2", t)))
                if t and t % 2 == 1:
                    t -= 1
                    dve.wait_ge(*at("act_did", ("out", t)))
                    dve.wait_ge(*at("vectors_landed"))
                    v.tensor_tensor(comb_rows[t][0], comb_rows[t][0], bc_row, ALU.mult).then_inc(*did(("out", t)))

        def post_pe(pe):
            T_ = nc.tensor
            scan_done(pe)

            def did(key):
                return up("pe_did", key)

            def mix_part(t, part):
                if part == 0:
                    pe.wait_ge(*at("w_out_landed", "early"))
                    if t:
                        pe.wait_ge(*at("dve_did", ("mixed", t - 1)))
                else:
                    pe.wait_ge(*at("act_did", ("turn_a", t)))
                    pe.wait_ge(*at("w_out_landed"))
                for hf in range(2):
                    for i in range(4 * part, 4 * part + 4):
                        c = WROWS[i]
                        lhs = catA[:, t % 2, c, :] if c < 4 else catBC[:, c - 4, t * P:(t + 1) * P]
                        x = T_.matmul(ps[6 + hf][:, :], lhs, wout[:, i, hf * 512:(hf + 1) * 512], start=(i == 0), stop=(i == KD - 1))
                if part:
                    x.then_inc(*did(("mix", t)))

            for k, t in ORDER:
                if k == "head":
                    if t >= 2:
                        pe.wait_ge(*at("dve_did", ("head", t - 2)))
                    T_.matmul(ps[2 + t % 2][:, :], loraT[:, 2, tcols(t)], g2_sb[:, :], start=True, stop=True).then_inc(*did(("head", t)))
                elif k == "turn_a":
                    pe.wait_ge(*at("dve_did", ("head", t)))
                    if t:
                        pe.wait_ge(*at("act_did", ("turn_a", t - 1)))
                    for m in range(4):
                        x = T_.transpose(ps[5][:, m * P:(m + 1) * P], ytm[:, t, m * P:(m + 1) * P], ident[:, :])
                    x.then_inc(*did(("turn_a", t)))
                elif k == "mix":
                    if t:
                        mix_part(t, 0)
                    mix_part(t, 1)
                elif k == "mix_bc":
                    mix_part(t, 0)
                elif k == "turn_h2":
                    pe.wait_ge(*at("dve_did", ("h2", t)))
                    if t:
                        pe.wait_ge(*at("act_did", ("h2", t - 1)))
                        pe.wait_ge(*at("dve_did", ("h2_T", t - 1)))
                    for c in range(KD):
                        x = T_.transpose(ps[(1, 4)[c // 4]][:, (c % 4) * P:(c % 4 + 1) * P], h2[:, t % 2, c * P:(c + 1) * P], ident[:, :])
                    x.then_inc(*did(("turn_h2", t)))
                elif k == "router":
                    pe.wait_ge(*at("act_did", ("h2", t)))
                    pe.wait_ge(*at("dve_did", ("h2_T", t)))
                    pe.wait_ge(*at("vectors_landed", "second norm"))
                    for c in range(KD):
                        x = T_.matmul(ps[0][:, t * NEXP:(t + 1) * NEXP], h2T[:, c, :], wr_sb[:, c, :], start=(c == 0), stop=(c == KD - 1))
                    x.then_inc(*did(("router", t)))
            pe.wait_ge(*at("dve_did", "picks"))
            T_.matmul(ps[3][:, 0:NT * NEXP], gmask[:, 0, 0, :], prod, start=True, stop=True)
            T_.matmul(ps[3][:, NT * NEXP:2 * NT * NEXP], ones, prod, start=True, stop=True).then_inc(*did("counts"))
            pe.wait_ge(*at("dve_did", "in_row"))
            for s in range(2 * NT):
                x = T_.matmul(ps[5][:, 0:CAP], in_row[:, s * P:(s + 1) * P], in_tile[:, s * CAP:(s + 1) * CAP],
                              start=(s == 0), stop=(s == 2 * NT - 1))
            x.then_inc(*did("slot_tokens"))
            def turn_h(i):
                pe.wait_ge(*at(f"rows_landed{i % 2}", i))
                if i:
                    pe.wait_ge(*at("act_did", ("turn_h", i - 1)))
                    pe.wait_ge(*at("dve_did", ("turn_h", i - 1)))
                hv = hrow[:, i % 2, :].rearrange("p (q k) -> p k q", k=KD)
                for c in range(KD):
                    x = T_.transpose(ps[c // 4][:, (c % 4) * P:(c % 4 + 1) * P], hv[:, c, :], ident[:, :])
                x.then_inc(*did(("turn_h", i)))

            def gate_up(i):
                s = i % 2
                pe.wait_ge(*at("act_did", ("turn_h", i)))
                pe.wait_ge(*at("dve_did", ("turn_h", i)))
                pe.wait_ge(*at(f"gu_landed{s}", i))
                if i >= 2:
                    pe.wait_ge(*at("dve_did", ("gu", i - 2)))
                for c in range(KD):
                    x = T_.matmul(ps[2 + s][:, :], hT[:, s, c, :], wgu[:, s, c, :], start=(c == 0), stop=(c == KD - 1))
                x.then_inc(*did(("gu", i)))

            def turn_act(i):
                s = i % 2
                pe.wait_ge(*at("dve_did", ("gu", i)))
                if i:
                    pe.wait_ge(*at("dve_did", ("turn_act", i - 1)))
                else:
                    pe.wait_ge(*at("dve_did", "tokens"))
                av = actg[:, s, :].rearrange("p (q k) -> p k q", k=2)
                for c in range(2):
                    x = T_.transpose(ps[4][:, c * P:(c + 1) * P], av[:, c, :], ident[:, :])
                x.then_inc(*did(("turn_act", i)))

            def down(i):
                s = i % 2
                pe.wait_ge(*at("dve_did", ("turn_act", i)))
                pe.wait_ge(*at(f"down_landed{s}", i))
                if i:
                    pe.wait_ge(*at("act_did", ("down", i - 1)))
                    pe.wait_ge(*at("dve_did", ("down", i - 1)))
                for hf in range(2):
                    for c in range(2):
                        x = T_.matmul(ps[5 + hf][:, :], actT[:, s, c * P:(c + 1) * P], wdn[:, s, c, hf * 512:(hf + 1) * 512],
                                      start=(c == 0), stop=(c == 1))
                x.then_inc(*did(("down", i)))

            def pe_tiles(first, end, call):
                call(first, turn_h)
                call(first, gate_up)
                call(first + 1, turn_h)
                call(first, turn_act)
                for i in range(first, end):
                    if i + 1 < end:
                        call(i + 1, gate_up)
                    if i + 2 < end:
                        call(i + 2, turn_h)
                    if i + 1 < end:
                        call(i + 1, turn_act)
                    call(i, down)
            all_tiles(pe, pe_tiles)

        block = ctx.enter_context(nc.Block())
        @block.sync
        def _(sp):
            def rows(name, ap):
                s, n = PR[name]
                sp.dma_start(prow[s:s + n, :], ap).then_inc(*up16("params_landed"))

            def x_load(t):
                src = A["x_prompt"][0] if t == 0 else A["x_sample"][0, (t - 1) * P:t * P, :]
                if t >= 2:
                    sp.wait_ge(*at("xn", t - 2))
                    sp.wait_ge(*at("x_square", t - 2))
                sp.dma_start(xin[:, t % 2, :], src).then_inc(*up16(f"x_landed{t % 2}", t))

            def mod_store(j):
                sp.dma_start(mod_dram[:, (j - 4) * 512:(j - 3) * 512], modrow).then_inc(*up16("mod_stored", j))

            def ring_load(n):
                kind, j = RING[n]
                if n >= 2:
                    sp.wait_ge(*last_use(n - 2))
                if kind == "ada":
                    src = A["ada_w"][0].rearrange("(k p) n -> p k n", p=P)[:, :, j * 512:(j + 1) * 512]
                    sp.dma_start(wring[:, n % 2, :, :], src).then_inc(*up16(f"ring_landed{n % 2}", n))
                    if j >= 1:
                        sp.wait_ge(*row_made(j - 1))
                    if j >= 5:
                        mod_store(j - 1)
                    sp.dma_start(adab, A["ada_b"][:, j * 512:(j + 1) * 512].to_broadcast([2, 512])) \
                        .then_inc(*up16("ada_b_landed", j))
                else:
                    src = A["w_in"][0].rearrange("(k p) n -> p k n", p=P)[:, :, C0[j]:C0[j] + CW[j]]
                    sp.dma_start(wring[:, n % 2, :, 0:CW[j]], src).then_inc(*up16(f"ring_landed{n % 2}", n))

            rows("c_ctx", A["c_ctx"].rearrange("(r p) -> r p", p=P))
            rows("c", A["c"].rearrange("o (r p) -> (o r) p", p=P))
            rows("norm1", A["norm1_g"].rearrange("o (r p) -> (o r) p", p=P))
            rows("norm2", A["norm2_g"].rearrange("o (r p) -> (o r) p", p=P))
            rows("mu", A["mu_shift"].rearrange("o (r p) -> (o r) p", p=P))
            for n in ("w0", "a0", "k_k", "k_a"):
                rows(n, A[n].rearrange("o d (r p) -> (o d r) p", p=P))
            rows("r_k", A["r_k"].rearrange("o (r h) c -> (o r) (h c)", h=2))
            rows("conv_b", A["conv_b"].rearrange("o (r p) -> (o r) p", p=P))
            rows("gmlp_bs", A["gmlp_bs"].rearrange("o g p -> (o g) p"))
            sp.dma_start(crow, A["conv_w"].rearrange("o k (r p) -> (o k r) p", p=P)).then_inc(*up16("params_landed"))
            x_load(0)
            x_load(1)
            sp.dma_start(wsrow, A["gmlp_ws"][0].rearrange("g p q -> p g q")).then_inc(*up16("ws_landed"))
            ring_load(0)
            x_load(2)
            x_load(3)
            ring_load(1)
            for i, n in enumerate(("gmlp_norm_g", "gmlp_norm_b", "beta_b", "conv_norm_g", "conv_norm_b", "beta_c")):
                sp.dma_start(bc_b[:, i, :], A[n].to_broadcast([P, 256])).then_inc(*up16("bc_landed"))
            for d in range(2):
                for i, n in enumerate(("w2", "a2")):
                    sp.dma_start(lora_w[d * HD:(d + 1) * HD, i, :], A[n][0, d]).then_inc(*up16("lora_w_landed"))
            sp.dma_start(g2_sb[:, :], A["g2"][0]).then_inc(*up16("lora_w_landed"))
            for n in range(2, len(RING)):
                ring_load(n)
                if n == 3:
                    x_load(4)
            sp.wait_ge(*row_made(11))
            mod_store(11)
            scan_loads(sp)

        @block.gpsimd
        def _(pool):
            g = nc.gpsimd
            g.memset(same[:, :, :], 1.0).then_inc(*up("ones"))
            g.memset(gmask[:, :, :, :], 1.0).then_inc(*up("ones"))
            g.memset(keep[:, :], 1.0).then_inc(*up("ones", "all"))
            pool.wait_ge(*at("ones", "all"))
            for l in range(7):
                b = 1 << l
                v = same[:, l, :].rearrange("p (n b) -> p n b", b=b)
                g.affine_select(out=v, in_=v, pattern=[[-b, P // b], [0, b]], compare_op=ALU.is_ge, fill=0.0,
                                base=0, channel_multiplier=1).then_inc(*up("same_lower", l))
            for l in range(7):
                b = 1 << l
                v = same[:, l, :].rearrange("p (n b) -> p n b", b=b)
                pool.wait_ge(*at("same_lower", l))
                g.affine_select(out=v, in_=v, pattern=[[b, P // b], [0, b]], compare_op=ALU.is_ge, fill=0.0,
                                base=b - 1, channel_multiplier=-1).then_inc(*up("same", l))
            g.memset(keep[:, 0:1], 0.0).then_inc(*up("const"))
            g.memset(keep[:, SEQ:SEQ + 2], 0.0).then_inc(*up("const"))
            for t in range(2, NT):
                g.memset(keep[:, col(t):col(t) + 1], 0.0).then_inc(*up("const"))
            for d in range(2):
                s = 1 - 2 * d
                for q in range(2):
                    v = gmask[:, d, q, :]
                    g.affine_select(out=v, in_=v, pattern=[[s, P]], compare_op=ALU.is_ge if q else ALU.is_gt,
                                    fill=0.0, base=0, channel_multiplier=-s).then_inc(*up("const"))
            g.memset(glu[:, :, :, :], 0.0).then_inc(*up("const", "all"))
            for j in range(4, 12):
                pool.wait_ge(*at("mod_row_copy", j))
                pool.wait_ge(*at("ada_b_landed", j))
                g.tensor_tensor(modrow, modrow, adab, ALU.add).then_inc(*up("late_mod_row", j))
            scan_pool(pool)

        @block.scalar
        def _(act):
            a = nc.scalar
            act.wait_ge(*at("pcol"))
            for gi, n in enumerate(("c_ctx", "c")):
                s, w = PR[n]
                a.activation(silu_c[:, :, gi], pcol[:, s:s + w], ACT.Silu).then_inc(*up("silu_c"))
            act.wait_ge(*at("eps"))
            for t in range(NT):
                act.wait_ge(*at(f"x_landed{t % 2}", t))
                if t == 0:
                    act.wait_ge(*at("ws_T"))
                else:
                    act.wait_ge(*at("x_square", t - 1))
                a.activation(gl[:, 0:2, :].rearrange("p t n -> p (t n)"), xin[:, t % 2, :], ACT.Square,
                             accum_out=sumsq[:, 0, t:t + 1]).then_inc(*up("x_square", t))
                act.wait_ge(*at("x_square", t))
                a.activation(rstd[:, 0, t:t + 1], sumsq[:, 0, t:t + 1], ACT.Abs_reciprocal_sqrt, bias=eps[:, 0:1],
                             scale=1.0 / D).then_inc(*up("rstd1", t))
                if t >= 2:
                    h1_act(act, t - 2)
            h1_act(act, NT - 2)
            h1_act(act, NT - 1)

            for i, (c, m) in enumerate(TILES):
                act.wait_ge(*at("proj", (c, m)))
                lat, ctx_ = ps[4 + 2 * (i % 2)], ps[5 + 2 * (i % 2)]
                if c == 5:
                    f, name, dst = (ACT.Copy, "conv_a", acc[:, m % 2, :]) if m < 2 else (ACT.Sigmoid, "conv_gate", psc[:, m % 2, 0:T])
                    a.activation(dst[:, 0:P], ctx_[:, 0:P], f).then_inc(*up(name))
                    a.activation(dst[:, P:T], lat[:, :], f).then_inc(*up(name, m))
                    if m == 3:
                        for t in range(NT):
                            act.wait_ge(*at("proj_B", t))
                            a.activation(gl[:, t, :], ps[2 + t % 2][:, :], ACT.Gelu_apprx_tanh).then_inc(*up("gelu", t))
                        act.wait_ge(*at("pad_zero"))
                        act.wait_ge(*at("conv_glu"))
                    continue
                n = i - 4
                s = n % 2
                j = c * 4 + m
                if n >= 2:
                    act.wait_ge(*at("mixed", n - 2))
                a.activation(praw[:, s, 1:1 + P], ctx_[:, 0:P], ACT.Copy).then_inc(*up("p_raw"))
                a.activation(praw[:, s, P + 2:P + 2 + LAT], lat[:, :], ACT.Copy).then_inc(*up("p_raw"))
                a.activation(psc[:, s, 0:P], ctx_[:, 0:P], ACT.Copy, scale=mu_keep[:, j:j + 1]).then_inc(*up("p_raw"))
                a.activation(psc[:, s, P + 1:TW], lat[:, :], ACT.Copy, scale=mu_keep[:, j:j + 1]).then_inc(*up("p_raw", n))
                if n == 2:
                    act.wait_ge(*at("gmlp_stat"))
                    a.activation(rstd[:, 1, :], mv[:, 0, :, 1], ACT.Abs_reciprocal_sqrt, bias=eps[:, 1:2]).then_inc(*up("gmlp_rstd"))
                if n == 3:
                    act.wait_ge(*at("mixed", 2))
                    a.activation(loraT[:, 0, :], loraT[:, 0, :], ACT.Tanh).then_inc(*up("lora"))
                    a.activation(loraT[:, 2, :], loraT[:, 2, :], ACT.Sigmoid).then_inc(*up("lora"))
                if n == 7:
                    for t in range(NT):
                        act.wait_ge(*at("gmlp_prod", t))
                        a.activation(gl[:, t, 256:512], gl[:, t, 0:256], ACT.Square, accum_out=sumsq[:, 1, t:t + 1]) \
                            .then_inc(*up("gmlp_square", t))
                    act.wait_ge(*at("gmlp_square", NT - 1))
                    a.activation(rstd[:, 2, :], sumsq[:, 1, :], ACT.Abs_reciprocal_sqrt, bias=eps[:, 0:1], scale=1.0 / DB) \
                        .then_inc(*up("gmlp_rrms"))
                if n == 11:
                    cat_copy(act, 0, "yb_T")
            act.wait_ge(*at("conv_stat"))
            a.activation(rstd[:, 3, :], mv[:, 1, :, 1], ACT.Abs_reciprocal_sqrt, bias=eps[:, 1:2]).then_inc(*up("conv_rstd"))
            late_row(act, 0)
            for t in range(NT):
                act.wait_ge(*at("conv_norm", t))
                a.activation(gl[:, t, 256:512], gl[:, t, 0:256], ACT.Silu).then_inc(*up("conv_silu", t))
            late_row(act, 1)
            for t in range(NT):
                act.wait_ge(*at("conv_silu", t))
                a.activation(gl[:, t, 0:256], gl[:, t, 256:512], ACT.Square, accum_out=sumsq[:, 2, t:t + 1]) \
                    .then_inc(*up("conv_square", t))
            act.wait_ge(*at("conv_square", NT - 1))
            a.activation(rstd[:, 4, :], sumsq[:, 2, :], ACT.Abs_reciprocal_sqrt, bias=eps[:, 0:1], scale=1.0 / DC) \
                .then_inc(*up("conv_rrms"))
            late_row(act, 2)
            cat_copy(act, 2, "yc_T")
            late_row(act, 3)
            scan_act(act)

        @block.vector
        def _(dve):
            v = nc.vector
            for h in range(2):
                for q in range(2):
                    v.memset(headsel[64 * h:64 * h + 64, q:q + 1], float(h == q)).then_inc(*up("eps"))
            v.memset(eps[:, 0:1], EPS_RMS).then_inc(*up("eps"))
            v.memset(eps[:, 1:2], EPS_LN).then_inc(*up("eps"))
            v.memset(eps[:, 2:3], EPS_LNX).then_inc(*up("eps"))
            dve.wait_ge(*at("same", 6))
            v.tensor_copy(ident[:, :], same[:, 0, :]).then_inc(*up("ident", 0))
            v.tensor_copy(halfones[:, :], same[:, 6, :]).then_inc(*up("ident", 1))
            for l in range(7):
                v.tensor_tensor(level[:, l, :], same[:, l + 1, :], same[:, l, :], ALU.subtract).then_inc(*up("level"))
            dve.wait_ge(*at("param_T"))
            v.tensor_copy(pcol[:, :], ps[0][:, 0:NPR]).then_inc(*up("pcol"))
            v.tensor_copy(ccol, ps[0][:, 128:128 + 2 * CONV_K]).then_inc(*up("pcol"))
            dve.wait_ge(*at("ws_T"))
            v.tensor_copy(wsT.rearrange("p g q -> p (g q)"), ps[1][:, :]).then_inc(*up("wsT"))
            dve.wait_ge(*at("pcol"))
            s, w = PR["mu"]
            v.tensor_scalar(mu_keep, pcol[:, s:s + w], -1.0, 1.0, ALU.mult, ALU.add).then_inc(*up("mu_made"))
            v.tensor_scalar(mu_half, pcol[:, s:s + w], 0.5, None, ALU.mult).then_inc(*up("mu_made"))
            s, w = PR["k_a"]
            v.tensor_scalar(ka_keep[:, :], pcol[:, s:s + w], -1.0, 1.0, ALU.mult, ALU.add).then_inc(*up("mu_made"))

            def xnorm(t):
                dve.wait_ge(*at("rstd1", t))
                if t >= 2:
                    dve.wait_ge(*at("xn_T", (t - 2, 1)))
                v.tensor_scalar(xn[:, t % 2, :], xin[:, t % 2, :], rstd[:, 0, t:t + 1], None, ALU.mult).then_inc(*up("xn", t))

            xnorm(0)
            xnorm(1)
            for j in range(4):
                ada_row(dve, j)
            dve.wait_ge(*at("mod_row_used", 3))
            mt = ps[0][:, 256:256 + 64].rearrange("p (w k g) -> p w k g", w=4, k=KD)
            v.tensor_copy(modT[:, 0:2, :, :], mt[:, 0:2, :, :]).then_inc(*up("mod1"))
            dve.wait_ge(*at("mod1"))
            for gi in range(2):
                v.scalar_tensor_tensor(gain[:, 0, :, gi], modT[:, SC1, :, gi], 1.0, pcol[:, 0:8], ALU.add, ALU.mult) \
                    .then_inc(*up("gain1"))
            dve.wait_ge(*at("gain1"))
            for t in range(NT):
                gi = min(t, 1)
                dve.wait_ge(*at("xn_T", (t, 1)))
                for k in range(4, 8):
                    v.tensor_scalar(h1T[:, k, t * P:(t + 1) * P], ps[4 + (2 * t + 1) % 4][:, (k - 4) * P:(k - 3) * P],
                                    gain[:, 0, k, gi:gi + 1], modT[:, SH1, k, gi:gi + 1], ALU.mult, ALU.add) \
                        .then_inc(*up("h1T_dve", (t, 1)))
                if t + 2 < NT:
                    xnorm(t + 2)
            v.memset(praw[:, :, 0:1], 0.0).then_inc(*up("pad_zero"))
            v.memset(praw[:, :, P + 1:P + 2], 0.0).then_inc(*up("pad_zero"))
            v.memset(praw[:, :, 642:643], 0.0).then_inc(*up("pad_zero"))
            dve.wait_ge(*at("const", "all"))
            dve.wait_ge(*at("conv_a", 1))
            dve.wait_ge(*at("conv_gate", 3))
            for c in range(2):
                va, ga = acc[:, c, :], psc[:, c, 0:T]
                v.tensor_tensor(glu[:, c, :, HALF:HALF + GRID], va.rearrange("p (r w) -> p r w", w=GRID),
                                ga.rearrange("p (r w) -> p r w", w=GRID), ALU.mult).then_inc(*up("conv_glu"))
                v.tensor_tensor(glu[:, c, 0, HALF + GRID:CONVW], va[:, GRID:GRID + HALF], ga[:, GRID:GRID + HALF], ALU.mult) \
                    .then_inc(*up("conv_glu"))
                v.tensor_tensor(glu[:, c, 1, 0:HALF], va[:, GRID - HALF:GRID], ga[:, GRID - HALF:GRID], ALU.mult) \
                    .then_inc(*up("conv_glu"))
            dve.wait_ge(*at("conv_glu"))
            v.memset(psc[:, :, P:P + 1], 0.0).then_inc(*up("pad_zero"))
            dve.wait_ge(*at("bc_landed"))

            cb = PR["conv_b"][0]

            def tap(i):
                k, c = i // 2, i % 2
                src = glu[:, c, :, k:k + GRID]
                dst = acc[:, c, :].rearrange("p (r w) -> p r w", w=GRID)
                if k == 0:
                    v.tensor_scalar(dst, src, ccol[:, c:c + 1], pcol[:, cb + c:cb + c + 1], ALU.mult, ALU.add) \
                        .then_inc(*up("conv_tap", i))
                else:
                    dve.wait_ge(*at("conv_tap", i - 2))
                    v.scalar_tensor_tensor(dst, src, ccol[:, 2 * k + c:2 * k + c + 1], dst, ALU.mult, ALU.add) \
                        .then_inc(*up("conv_tap", i))

            taps = iter(range(2 * CONV_K))
            for n, (c, m) in enumerate(ATILES):
                j, s = c * 4 + m, n % 2
                dve.wait_ge(*at("p_raw", n))
                if n:
                    dve.wait_ge(*at("mixed", n - 1))
                v.tensor_tensor(nbsum, praw[:, s, 0:TW], praw[:, s, 2:TW + 2], ALU.add).then_inc(*up("neighbours", n))
                dst = rkvT[:, c, m, :] if c < 3 else loraT[:, m, :]
                for _ in range(2):
                    for i in taps:
                        tap(i)
                        break
                dve.wait_ge(*at("neighbours", n))
                v.scalar_tensor_tensor(dst, nbsum, mu_half[:, j:j + 1], psc[:, s, :], ALU.mult, ALU.add).then_inc(*up("mixed", n))
                for _ in range(3):
                    for i in taps:
                        tap(i)
                        break
                if n == 0:
                    for t in range(NT):
                        dve.wait_ge(*at("gelu", t))
                        v.bn_stats(bst[:, 0, t, :], gl[:, t, 256:512]).then_inc(*up("gmlp_bn", t))
                    for t in range(NT):
                        dve.wait_ge(*at("gmlp_bn", t))
                        v.bn_aggr(mv[:, 0, t, :], bst[:, 0, t, :]).then_inc(*up("gmlp_stat"))
                if n == 2:
                    dve.wait_ge(*at("gmlp_rstd"))
                    norm_rows(dve, "gmlp", 0, 1, lambda t: gl[:, t, 256:512], lambda t: gl[:, t, 256:512], GN_G, GN_B)
                if n == 5:
                    for t in range(NT):
                        b, o = turned(t)
                        dve.wait_ge(*at("spatial", bank_done(t)))
                        bs = PR["gmlp_bs"][0]
                        for q in range(4):
                            u = gl[:, t, q * HD:(q + 1) * HD]
                            v.scalar_tensor_tensor(u, ps[b][:, o + q * HD:o + (q + 1) * HD], pcol[:, bs + q:bs + q + 1], u,
                                                   ALU.add, ALU.mult).then_inc(*up("gmlp_prod", t))
                if n == 8:
                    dve.wait_ge(*at("gmlp_rrms"))
                    for t in range(NT):
                        v.scalar_tensor_tensor(gl[:, t, 0:256], gl[:, t, 0:256], rstd[:, 2, t:t + 1], bc_b[:, BETA_B, :],
                                               ALU.mult, ALU.mult).then_inc(*up("yb", t))
            for t in range(NT):
                b, o = turned(t)
                dve.wait_ge(*at("conv_T", bank_done(t)))
                v.bn_stats(bst[:, 1, t, :], ps[b][:, o:o + 256]).then_inc(*up("conv_bn", t))
            for t in range(NT):
                dve.wait_ge(*at("conv_bn", t))
                v.bn_aggr(mv[:, 1, t, :], bst[:, 1, t, :]).then_inc(*up("conv_stat"))
            dve.wait_ge(*at("conv_rstd"))
            dve.wait_ge(*at("yb_T", NT - 1))
            norm_rows(dve, "conv", 1, 3, lambda t: ps[turned(t)[0]][:, turned(t)[1]:turned(t)[1] + 256],
                      lambda t: gl[:, t, 0:256], CN_G, CN_B)
            dve.wait_ge(*at("conv_rrms"))
            for t in range(NT):
                v.scalar_tensor_tensor(gl[:, t, 0:256], gl[:, t, 256:512], rstd[:, 4, t:t + 1], bc_b[:, BETA_C, :],
                                       ALU.mult, ALU.mult).then_inc(*up("yc", t))
            scan_dve(dve)

        @block.tensor
        def _(pe):
            T_ = nc.tensor
            pe.wait_ge(*at("params_landed"))
            pe.wait_ge(*at("ident", 0))
            T_.transpose(ps[0][:, 0:NPR], prow, ident[0:NPR, 0:NPR])
            T_.transpose(ps[0][:, 128:128 + 2 * CONV_K], crow, ident[0:2 * CONV_K, 0:2 * CONV_K]).then_inc(*up("param_T"))
            pe.wait_ge(*at("ws_landed"))
            for q in range(4):
                x = T_.transpose(ps[1][:, q * P:(q + 1) * P], wsrow[:, q, :], ident[:, :])
            x.then_inc(*up("ws_T"))

            def xn_T(t):
                pe.wait_ge(*at("xn", t))
                for hf in range(2):
                    n = 2 * t + hf
                    if n >= 4:
                        q = ((n - 4) // 2, (n - 4) % 2)
                        pe.wait_ge(*at("h1T_dve" if hf else "h1T_act", q))
                    for i in range(4):
                        x = T_.transpose(ps[4 + n % 4][:, i * P:(i + 1) * P], xn[:, t % 2, (4 * hf + i) * P:(4 * hf + i + 1) * P],
                                         ident[:, :])
                    x.then_inc(*up("xn_T", (t, hf)))

            xn_T(0)
            xn_T(1)
            pe.wait_ge(*at("silu_c"))
            for n in range(4):
                ada_mm(pe, n)
                ada_cols(pe, n)
            for t in range(2, NT):
                xn_T(t)
            pe.wait_ge(*at("h1T_act", (NT - 1, 0)))
            pe.wait_ge(*at("h1T_dve", (NT - 1, 1)))
            i = 0
            for n, (kind, c) in enumerate(RING[0:4 + len(CHUNKS)]):
                if kind != "proj":
                    continue
                s = n % 2
                pe.wait_ge(*at(f"ring_landed{s}", n))
                if c == 4:
                    for t in range(NT):
                        if t >= 2:
                            pe.wait_ge(*at("gelu", t - 2))
                        for k in range(KD):
                            x = T_.matmul(ps[2 + t % 2][:, :], h1T[:, k, t * P:(t + 1) * P], wring[:, s, k, :],
                                          start=(k == 0), stop=(k == KD - 1))
                        x.then_inc(*up("proj_B", t))
                    continue
                for m in range(CW[c] // P):
                    if i >= 2:
                        cp, mp = TILES[i - 2]
                        if cp == 5:
                            pe.wait_ge(*at("conv_a" if mp < 2 else "conv_gate", mp))
                        else:
                            pe.wait_ge(*at("p_raw", i - 2 - 4))
                    lat, ctx_ = ps[4 + 2 * (i % 2)], ps[5 + 2 * (i % 2)]
                    for k in range(KD):
                        w = wring[:, s, k, m * P:(m + 1) * P]
                        T_.matmul(ctx_[:, 0:P], w, h1T[:, k, 0:P], start=(k == 0), stop=(k == KD - 1))
                        x = T_.matmul(lat[:, :], w, h1T[:, k, P:T], start=(k == 0), stop=(k == KD - 1))
                    x.then_inc(*up("proj", (c, m)))
                    a_i = i - 4
                    if a_i == 4:
                        for t in range(NT):
                            pe.wait_ge(*at("gmlp_norm", t))
                            if t == 0:
                                pe.wait_ge(*at("wsT"))
                                pe.wait_ge(*at("gelu", NT - 1))
                            b, o = turned(t)
                            for q in range(4):
                                x = T_.matmul(ps[b][:, o + q * HD:o + (q + 1) * HD], wsT[:, q, :],
                                              gl[:, t, 256 + q * HD:256 + (q + 1) * HD], start=True, stop=True)
                            x.then_inc(*up("spatial", t))
                    if a_i == 10:
                        turn(pe, "yb_T", "yb", lambda t: [gl[:, t, c * P:(c + 1) * P] for c in range(2)])
                    i += 1
            pe.wait_ge(*at("conv_tap", 2 * CONV_K - 1))
            pe.wait_ge(*at("catBC", (0, 2)))
            for t in range(NT):
                b, o = turned(t)
                for c in range(2):
                    x = T_.transpose(ps[b][:, o + c * P:o + (c + 1) * P], acc[:, c, t * P:(t + 1) * P], ident[:, :])
                x.then_inc(*up("conv_T", t))
            for n in LATE_ADA[:3]:
                ada_mm(pe, n)
            turn(pe, "yc_T", "yc", lambda t: [gl[:, t, c * P:(c + 1) * P] for c in range(2)])
            ada_mm(pe, LATE_ADA[3])
            scan_pe(pe)


INPUTS = ['x_prompt', 'x_sample', 'state_rwkv', 'c', 'c_ctx', 'norm1_g', 'norm2_g', 'ada_w', 'ada_b', 'w_in', 'mu_shift',
          'w0', 'w2', 'a0', 'a2', 'k_k', 'k_a', 'g2', 'r_k', 'lnx_g', 'lnx_b', 'gmlp_norm_g', 'gmlp_norm_b', 'gmlp_ws',
          'gmlp_bs', 'beta_b', 'conv_w', 'conv_b', 'conv_norm_g', 'conv_norm_b', 'beta_c', 'w_out', 'w_router', 'b_router',
          'moe_w_gu', 'moe_w_down', 'final_g']
OUTPUTS = [(1, 128, 1024), (1, 512, 1024), (1, 1, 2, 8, 64, 64)]


def kernel(**inputs):
    import numpy as np
    import concourse.bacc as bacc
    from concourse.bass_utils import run_bass_kernel_spmd

    known = None
    for _ in range(2):
        nc = bacc.Bacc("TRN2", target_bir_lowering=False, num_devices=1)
        arrays, A = {}, {}
        for name in INPUTS:
            a = np.ascontiguousarray(inputs[name])
            arrays[f"in_{name}_dram"] = a
            A[name] = nc.dram_tensor(f"in_{name}_dram", a.shape, mybir.dt.from_np(a.dtype), kind="ExternalInput").ap()
        outs = [nc.dram_tensor(f"out_{i}_dram", shape, F32, kind="ExternalOutput").ap() for i, shape in enumerate(OUTPUTS)]
        counts = Counts(known)
        build(nc, A, outs, counts)
        known = counts.seen
    r = run_bass_kernel_spmd(nc, [arrays], core_ids=[0])
    return tuple(r.results[0][f"out_{i}_dram"] for i in range(len(OUTPUTS)))
```
